# Optimizing a Trainium2 kernel written in Bass

```python
import jax, jax.numpy as jnp
from jax import lax
import numpy as np
import math
import jax
import jax.numpy as jnp

D_MODEL = 1024
BATCH = 1
SEQ = 256
DEPTH = 2

HEAD_DIM = 64
N_HEADS_A = 8
N_HEADS_B = 8
N_KV_B = 2
GQA_GROUP = N_HEADS_B // N_KV_B
DILATED_BRANCHES = ((128, 1), (512, 4), (2048, 16))
SWA_WINDOW = 128
BLK = 128
ROPE_THETA = 10000.0
D_FF = 3584
N_EXPERTS = 8
TOP_K = 2
RMS_EPS = 1e-5
WIDTH_A = N_HEADS_A * HEAD_DIM
WIDTH_B = N_HEADS_B * HEAD_DIM
KV_WIDTH_B = N_KV_B * HEAD_DIM
MIX_WIDTH = WIDTH_A + WIDTH_B
IN_SIZES = (WIDTH_A, WIDTH_A, WIDTH_A, WIDTH_B, KV_WIDTH_B, KV_WIDTH_B)
IN_WIDTH = sum(IN_SIZES)
IN_SPLITS = tuple(int(c) for c in np.cumsum(IN_SIZES)[:-1])
N_DENSE = (DEPTH + 1) // 2
N_MOE = DEPTH // 2


def rmsnorm(x, g):
    xf = x.astype(jnp.float32)
    y = xf * lax.rsqrt(jnp.mean(xf * xf, axis=-1, keepdims=True) + RMS_EPS)
    return (y * g.astype(jnp.float32)).astype(x.dtype)

def rope_tables(positions):
    inv = ROPE_THETA ** (-jnp.arange(0, HEAD_DIM, 2, dtype=jnp.float32) / HEAD_DIM)
    ang = positions.astype(jnp.float32)[:, None] * inv[None, :]
    ang = jnp.concatenate([ang, ang], axis=-1)
    return jnp.cos(ang), jnp.sin(ang)

def apply_rope(t, cos, sin):
    t1, t2 = jnp.split(t, 2, axis=-1)
    rot = jnp.concatenate([-t2, t1], axis=-1)
    return t * cos.astype(t.dtype) + rot * sin.astype(t.dtype)

def banded_attention(q, k, v, max_dist, sink=None):
    *lead, G, L, Dh = q.shape
    nb = L // BLK
    qb = q.reshape(*lead, G, nb, BLK, Dh)

    def band(t):
        tb = t.reshape(*lead, nb, BLK, Dh)
        prev = jnp.concatenate([jnp.zeros_like(tb[..., :1, :, :]), tb[..., :-1, :, :]], axis=-3)
        return jnp.concatenate([prev, tb], axis=-2)

    s = jnp.einsum('...gnqd,...nkd->...gnqk', qb, band(k),
                   preferred_element_type=jnp.float32) * (Dh ** -0.5)
    dist = (BLK + jnp.arange(BLK))[:, None] - jnp.arange(2 * BLK)[None, :]
    in_band = (dist >= 0) & (dist <= max_dist)
    has_prev = (jnp.arange(nb) > 0)[:, None, None] | (jnp.arange(2 * BLK) >= BLK)[None, None, :]
    mask = in_band[None] & has_prev
    s = jnp.where(mask, s, -jnp.inf)
    m = jnp.max(s, axis=-1)
    if sink is not None:
        sk = sink.astype(jnp.float32)[..., None, None]
        m = jnp.maximum(m, sk)
    p = jnp.exp(s - m[..., None])
    l = jnp.sum(p, axis=-1)
    if sink is not None:
        l = l + jnp.exp(sk - m)
    o = jnp.einsum('...gnqk,...nkd->...gnqd', p.astype(v.dtype), band(v),
                   preferred_element_type=jnp.float32) / l[..., None]
    lse = m + jnp.log(l)
    return o.reshape(*lead, G, L, Dh).astype(q.dtype), lse.reshape(*lead, G, L)

def dilated_branch(q, k, v, window, dilation):
    B, H, S, Dh = q.shape
    seg = dilation * BLK
    Sp = -(-S // seg) * seg

    def by_stride(t):
        t = jnp.pad(t, ((0, 0), (0, 0), (0, Sp - S), (0, 0)))
        return t.reshape(B, H, Sp // dilation, dilation, Dh).transpose(0, 1, 3, 2, 4)

    o, lse = banded_attention(by_stride(q)[..., None, :, :], by_stride(k), by_stride(v),
                              max_dist=window // dilation)
    o = o[:, :, :, 0].transpose(0, 1, 3, 2, 4).reshape(B, H, Sp, Dh)[:, :, :S]
    lse = lse[:, :, :, 0].transpose(0, 1, 3, 2).reshape(B, H, Sp)[:, :, :S]
    return o, lse

def dilated_mixer(q, k, v):
    outs, lses = zip(*[dilated_branch(q, k, v, w, d) for (w, d) in DILATED_BRANCHES])
    wts = jax.nn.softmax(jnp.stack(lses, axis=0), axis=0)
    o = jnp.einsum('rbhs,rbhsd->bhsd', wts, jnp.stack(outs, axis=0).astype(jnp.float32))
    return o.astype(q.dtype)

def swiglu(h, wg, wu, wd):
    return (jax.nn.silu(h @ wg) * (h @ wu)) @ wd

def moe_swiglu(h, router, wg, wu, wd):
    logits = (h @ router).astype(jnp.float32)
    top_vals, top_idx = lax.top_k(logits, TOP_K)
    gates = jax.nn.softmax(top_vals, axis=-1)
    gate_e = jnp.sum(jax.nn.one_hot(top_idx, N_EXPERTS, dtype=jnp.float32) * gates[..., None], axis=-2)
    gate_e = gate_e.astype(h.dtype)
    out = jnp.zeros_like(h)
    for e in range(N_EXPERTS):
        out = out + gate_e[..., e:e + 1] * swiglu(h, wg[e], wu[e], wd[e])
    return out

def heads(t, n):
    B, S, _ = t.shape
    return t.reshape(B, S, n, HEAD_DIM).transpose(0, 2, 1, 3)

def merge_heads(t):
    B, H, S, Dh = t.shape
    return t.transpose(0, 2, 1, 3).reshape(B, S, H * Dh)

def first_inputs(seed: int = 0) -> dict:
    key = jax.random.key(seed)
    ks = jax.random.split(key, 20)
    f32 = jnp.float32
    nrm = lambda k, shape, fan_in: jax.random.normal(k, shape, f32) * (fan_in ** -0.5)
    gain = lambda k, shape: 1.0 + 0.02 * jax.random.normal(k, shape, f32)
    return {
        "x": jax.random.normal(ks[0], (BATCH, SEQ, D_MODEL), f32),
        "positions": jnp.arange(SEQ, dtype=jnp.int32),
        "attn_norm": gain(ks[1], (DEPTH, D_MODEL)),
        "w_in": nrm(ks[2], (DEPTH, D_MODEL, IN_WIDTH), D_MODEL),
        "mix_norm_a": gain(ks[3], (DEPTH, WIDTH_A)),
        "mix_norm_b": gain(ks[4], (DEPTH, WIDTH_B)),
        "sinks": 0.5 * jax.random.normal(ks[5], (DEPTH, N_HEADS_B), f32),
        "w_out": nrm(ks[6], (DEPTH, MIX_WIDTH, D_MODEL), MIX_WIDTH) * 0.5,
        "ffn_norm": gain(ks[7], (DEPTH, D_MODEL)),
        "dense_w_gate": nrm(ks[8], (N_DENSE, D_MODEL, D_FF), D_MODEL),
        "dense_w_up": nrm(ks[9], (N_DENSE, D_MODEL, D_FF), D_MODEL),
        "dense_w_down": nrm(ks[10], (N_DENSE, D_FF, D_MODEL), D_FF) * 0.5,
        "router": nrm(ks[11], (N_MOE, D_MODEL, N_EXPERTS), D_MODEL),
        "moe_w_gate": nrm(ks[12], (N_MOE, N_EXPERTS, D_MODEL, D_FF), D_MODEL),
        "moe_w_up": nrm(ks[13], (N_MOE, N_EXPERTS, D_MODEL, D_FF), D_MODEL),
        "moe_w_down": nrm(ks[14], (N_MOE, N_EXPERTS, D_FF, D_MODEL), D_FF) * 0.5,
        "final_norm": gain(ks[15], (D_MODEL,)),
    }

def first_block(x, positions, attn_norm, w_in, mix_norm_a, mix_norm_b, sinks, w_out,
              ffn_norm, dense_w_gate, dense_w_up, dense_w_down, router,
              moe_w_gate, moe_w_up, moe_w_down, final_norm):
    B, S, _ = x.shape
    cos, sin = rope_tables(positions)
    for i in range(DEPTH):
        h = rmsnorm(x, attn_norm[i])
        proj = h @ w_in[i]
        qa, ka, va, qb, kb, vb = jnp.split(proj, IN_SPLITS, axis=-1)
        qa = apply_rope(heads(qa, N_HEADS_A), cos, sin)
        ka = apply_rope(heads(ka, N_HEADS_A), cos, sin)
        oa = dilated_mixer(qa, ka, heads(va, N_HEADS_A))
        qb = apply_rope(heads(qb, N_HEADS_B), cos, sin).reshape(B, N_KV_B, GQA_GROUP, S, HEAD_DIM)
        kb = apply_rope(heads(kb, N_KV_B), cos, sin)
        ob, _ = banded_attention(qb, kb, heads(vb, N_KV_B), SWA_WINDOW - 1,
                                 sink=sinks[i].reshape(N_KV_B, GQA_GROUP))
        ob = ob.reshape(B, N_HEADS_B, S, HEAD_DIM)
        mix = jnp.concatenate([rmsnorm(merge_heads(oa), mix_norm_a[i]),
                               rmsnorm(merge_heads(ob), mix_norm_b[i])], axis=-1)
        x = x + mix @ w_out[i]
        h = rmsnorm(x, ffn_norm[i])
        j = i // 2
        if i % 2 == 0:
            x = x + swiglu(h, dense_w_gate[j], dense_w_up[j], dense_w_down[j])
        else:
            x = x + moe_swiglu(h, router[j], moe_w_gate[j], moe_w_up[j], moe_w_down[j])
    return rmsnorm(x, final_norm)


DEPTH_2 = 1

CTX_LEN = 256
GRID_W = 64
N_HEADS = 8
D_ATTN = N_HEADS * 2 * HEAD_DIM
D_HYENA = D_MODEL
SHORT_CONV = 3
FILTER_EMB = 33
FILTER_ORDER = 64
DECAY_TARGET = 1e-2
FAST_DECAY_PCT = 0.3
SLOW_DECAY_PCT = 1.5
D_FF_2 = 2816
Q_BLOCK = 128
N_MOD = 9
N_PROJ = 3 * D_HYENA + 3 * D_ATTN + 2 * D_MODEL
SPLITS = (3 * D_HYENA, 3 * D_HYENA + D_ATTN, 3 * D_HYENA + 2 * D_ATTN, 3 * D_HYENA + 3 * D_ATTN)
EPS = 1e-6


def rmsnorm_2(x, g):
    xf = x.astype(jnp.float32)
    y = xf * lax.rsqrt(jnp.mean(xf * xf, axis=-1, keepdims=True) + EPS)
    return (y * g.astype(jnp.float32)).astype(x.dtype)

def modulate(x, shift, scale):
    return x * (1.0 + scale) + shift

def swiglu_2(x, w_in, w_out):
    gate, up = jnp.split(x @ w_in, 2, axis=-1)
    return (jax.nn.silu(gate) * up) @ w_out

def ffn_half(s, shift, scale, gate, g_pre, g_post, w_in, w_out):
    h = swiglu_2(modulate(rmsnorm_2(s, g_pre), shift, scale), w_in, w_out)
    return s + 0.5 * gate * rmsnorm_2(h, g_post)

def short_conv(x, w, b):
    L = x.shape[1]
    pad = SHORT_CONV // 2
    xp = jnp.pad(x, ((0, 0), (pad, pad), (0, 0)))
    return sum(xp[:, j:j + L] * w[j] for j in range(SHORT_CONV)) + b

def hyena_kernel(L, w1, b1, w2, b2, w3, b3, w4, freq):
    f32 = jnp.float32
    bands = (FILTER_EMB - 1) // 2
    t = jnp.linspace(0.0, 1.0, L, dtype=f32)[:, None]
    w = 2.0 * math.pi * jnp.arange(L, dtype=f32)[:, None] / L
    f = jnp.linspace(1e-4, bands - 1, bands, dtype=f32)[None, :]
    z = jnp.concatenate([t, jnp.cos(f * w), -jnp.sin(f * w)], axis=-1)
    h = jnp.sin(freq * (z @ w1 + b1))
    h = jnp.sin(freq * (h @ w2 + b2))
    h = jnp.sin(freq * (h @ w3 + b3))
    h = (h @ w4).astype(f32)
    deltas = jnp.linspace(math.log(DECAY_TARGET) / SLOW_DECAY_PCT,
                          math.log(DECAY_TARGET) / FAST_DECAY_PCT, D_HYENA, dtype=f32)
    decay = jnp.exp(-t * jnp.abs(deltas))
    h_fwd, h_bwd = jnp.split(h, 2, axis=-1)
    h_fwd = h_fwd * decay
    h_bwd = h_bwd * decay
    k = jnp.concatenate([h_fwd, jnp.zeros_like(h_fwd[:1]), h_bwd[:0:-1]], axis=0)
    return k / (jnp.sum(jnp.abs(k), axis=0, keepdims=True) + EPS)

def bidir_long_conv(u, k):
    L = u.shape[1]
    uf = jnp.fft.rfft(u.astype(jnp.float32), n=2 * L, axis=1)
    kf = jnp.fft.rfft(k, n=2 * L, axis=0)
    y = jnp.fft.irfft(uf * kf[None], n=2 * L, axis=1)[:, :L]
    return y.astype(u.dtype)

def hyena_branch(z_hy, conv_w, conv_b, filt, hy_bias):
    z = short_conv(z_hy, conv_w, conv_b)
    x0, x1, v = jnp.split(z, 3, axis=-1)
    k = hyena_kernel(z.shape[1], *filt)
    u = v * x1
    y = bidir_long_conv(u, k) + u * hy_bias
    return y * x0

def axial_rope_tables(L):
    rows = L // GRID_W
    r, col = jnp.meshgrid(jnp.arange(rows), jnp.arange(GRID_W), indexing='ij')
    r = r.reshape(-1).astype(jnp.float32)
    col = col.reshape(-1).astype(jnp.float32)
    half = HEAD_DIM // 2
    inv = ROPE_THETA ** (-jnp.arange(0, half, 2, dtype=jnp.float32) / half)
    ang = jnp.stack([r[:, None] * inv, col[:, None] * inv], axis=1)
    return jnp.cos(ang), jnp.sin(ang)

def apply_axial_rope(x, cos, sin):
    B, L = x.shape[:2]
    xr = x.reshape(B, L, N_HEADS, 2, 2, 2, HEAD_DIM // 4)
    x0, x1 = xr[..., 0, :], xr[..., 1, :]
    c = cos[None, :, None, None]
    s = sin[None, :, None, None]
    out = jnp.stack([x0 * c - x1 * s, x0 * s + x1 * c], axis=-2)
    return out.reshape(x.shape).astype(x.dtype)

def diff_attention(q, k, v, lam):
    B, L = q.shape[:2]
    nb = L // Q_BLOCK
    qb = jnp.moveaxis(q.reshape(B, nb, Q_BLOCK, N_HEADS, 2, HEAD_DIM), 1, 0)

    def block(qblk):
        s = jnp.einsum('bqhmd,bkhmd->bhmqk', qblk, k).astype(jnp.float32) * (HEAD_DIM ** -0.5)
        p = jax.nn.softmax(s, axis=-1)
        p = p[:, :, 0] - lam * p[:, :, 1]
        return jnp.einsum('bhqk,bkhe->bqhe', p.astype(v.dtype), v)

    o = lax.map(block, qb)
    return jnp.moveaxis(o, 0, 1).reshape(B, L, N_HEADS, 2 * HEAD_DIM)

def context_kv(h, w_in):
    B, L = h.shape[:2]
    k, v = jnp.split(h @ w_in[:, SPLITS[1]:SPLITS[3]], 2, axis=-1)
    return k.reshape(B, L, N_HEADS, 2, HEAD_DIM), v.reshape(B, L, N_HEADS, 2 * HEAD_DIM)

def token_mixer(h, w_in, conv_w, conv_b, filt, hy_bias, lam, lam_init, subln_g,
                w_hy_out, w_da_out, w_o, rope, ctx_kv):
    B, L = h.shape[:2]
    z_hy, q, k, v, gates = jnp.split(h @ w_in, SPLITS, axis=-1)
    y_hy = hyena_branch(z_hy, conv_w, conv_b, filt, hy_bias) @ w_hy_out
    q = q.reshape(B, L, N_HEADS, 2, HEAD_DIM)
    k = k.reshape(B, L, N_HEADS, 2, HEAD_DIM)
    v = v.reshape(B, L, N_HEADS, 2 * HEAD_DIM)
    if rope is not None:
        q = apply_axial_rope(q, *rope)
        k = apply_axial_rope(k, *rope)
    if ctx_kv is not None:
        k = jnp.concatenate([k, ctx_kv[0]], axis=1)
        v = jnp.concatenate([v, ctx_kv[1]], axis=1)
    o = diff_attention(q, k, v, lam)
    o = rmsnorm_2(o, subln_g) * (1.0 - lam_init)
    y_da = o.reshape(B, L, D_ATTN) @ w_da_out
    g_hy, g_da = jnp.split(jax.nn.sigmoid(gates), 2, axis=-1)
    return (g_hy * y_hy + g_da * y_da) @ w_o

def second_inputs(seed: int = 0) -> dict:
    key = jax.random.key(seed)
    ks = jax.random.split(key, 32)
    f32 = jnp.float32

    def nrm(k, shape, scale):
        return jax.random.normal(k, shape, f32) * scale

    return {
        'x': nrm(ks[0], (BATCH, SEQ, D_MODEL), 1.0),
        'c': nrm(ks[1], (BATCH, D_MODEL), 1.0),
        'ctx': nrm(ks[2], (BATCH, CTX_LEN, D_MODEL), 1.0),
        'c_ctx': nrm(ks[3], (D_MODEL,), 1.0),
        'w_ada': nrm(ks[4], (DEPTH_2, D_MODEL, N_MOD * D_MODEL), 0.5 * D_MODEL ** -0.5),
        'b_ada': nrm(ks[5], (DEPTH_2, N_MOD * D_MODEL), 0.01),
        'norm_g': 1.0 + nrm(ks[6], (DEPTH_2, 6, D_MODEL), 0.02),
        'w_ff_in': nrm(ks[7], (DEPTH_2, 2, D_MODEL, 2 * D_FF_2), D_MODEL ** -0.5),
        'w_ff_out': nrm(ks[8], (DEPTH_2, 2, D_FF_2, D_MODEL), D_FF_2 ** -0.5),
        'w_in': nrm(ks[9], (DEPTH_2, D_MODEL, N_PROJ), D_MODEL ** -0.5),
        'hy_conv_w': nrm(ks[10], (DEPTH_2, SHORT_CONV, 3 * D_HYENA), SHORT_CONV ** -0.5),
        'hy_conv_b': nrm(ks[11], (DEPTH_2, 3 * D_HYENA), 0.01),
        'filt_w1': nrm(ks[12], (DEPTH_2, FILTER_EMB, FILTER_ORDER), FILTER_EMB ** -0.5),
        'filt_b1': nrm(ks[13], (DEPTH_2, FILTER_ORDER), 0.1),
        'filt_w2': nrm(ks[14], (DEPTH_2, FILTER_ORDER, FILTER_ORDER), FILTER_ORDER ** -0.5),
        'filt_b2': nrm(ks[15], (DEPTH_2, FILTER_ORDER), 0.1),
        'filt_w3': nrm(ks[16], (DEPTH_2, FILTER_ORDER, FILTER_ORDER), FILTER_ORDER ** -0.5),
        'filt_b3': nrm(ks[17], (DEPTH_2, FILTER_ORDER), 0.1),
        'filt_w4': nrm(ks[18], (DEPTH_2, FILTER_ORDER, 2 * D_HYENA), FILTER_ORDER ** -0.5),
        'filt_freq': 1.0 + nrm(ks[19], (DEPTH_2, FILTER_ORDER), 0.01),
        'hy_bias': nrm(ks[20], (DEPTH_2, D_HYENA), 0.1),
        'lambda_q1': nrm(ks[21], (DEPTH_2, HEAD_DIM), 0.1),
        'lambda_k1': nrm(ks[22], (DEPTH_2, HEAD_DIM), 0.1),
        'lambda_q2': nrm(ks[23], (DEPTH_2, HEAD_DIM), 0.1),
        'lambda_k2': nrm(ks[24], (DEPTH_2, HEAD_DIM), 0.1),
        'subln_g': 1.0 + nrm(ks[25], (DEPTH_2, 2 * HEAD_DIM), 0.02),
        'w_hy_out': nrm(ks[26], (DEPTH_2, D_HYENA, D_MODEL), D_HYENA ** -0.5),
        'w_da_out': nrm(ks[27], (DEPTH_2, D_ATTN, D_MODEL), D_ATTN ** -0.5),
        'w_o': nrm(ks[28], (DEPTH_2, D_MODEL, D_MODEL), D_MODEL ** -0.5),
    }

def second_block(x, c, ctx, c_ctx, w_ada, b_ada, norm_g, w_ff_in, w_ff_out, w_in,
              hy_conv_w, hy_conv_b, filt_w1, filt_b1, filt_w2, filt_b2, filt_w3, filt_b3,
              filt_w4, filt_freq, hy_bias, lambda_q1, lambda_k1, lambda_q2, lambda_k2,
              subln_g, w_hy_out, w_da_out, w_o):
    rope = axial_rope_tables(x.shape[1])
    xs, cs = x, ctx
    for l in range(DEPTH_2):
        lam_init = 0.8 - 0.6 * math.exp(-0.3 * l)
        lam = (jnp.exp(jnp.sum(lambda_q1[l] * lambda_k1[l]).astype(jnp.float32))
               - jnp.exp(jnp.sum(lambda_q2[l] * lambda_k2[l]).astype(jnp.float32)) + lam_init)
        mod_x = jnp.split((jax.nn.silu(c) @ w_ada[l] + b_ada[l])[:, None, :], N_MOD, axis=-1)
        mod_c = jnp.split((jax.nn.silu(c_ctx) @ w_ada[l] + b_ada[l])[None, None, :], N_MOD, axis=-1)
        g = norm_g[l]
        filt = (filt_w1[l], filt_b1[l], filt_w2[l], filt_b2[l], filt_w3[l], filt_b3[l],
                filt_w4[l], filt_freq[l])
        mixer_params = (w_in[l], hy_conv_w[l], hy_conv_b[l], filt, hy_bias[l], lam, lam_init,
                        subln_g[l], w_hy_out[l], w_da_out[l], w_o[l])
        xs = ffn_half(xs, mod_x[0], mod_x[1], mod_x[2], g[0], g[1], w_ff_in[l, 0], w_ff_out[l, 0])
        cs = ffn_half(cs, mod_c[0], mod_c[1], mod_c[2], g[0], g[1], w_ff_in[l, 0], w_ff_out[l, 0])
        hx = modulate(rmsnorm_2(xs, g[2]), mod_x[3], mod_x[4])
        hc = modulate(rmsnorm_2(cs, g[2]), mod_c[3], mod_c[4])
        y = token_mixer(hx, *mixer_params, rope, context_kv(hc, w_in[l]))
        xs = xs + mod_x[5] * rmsnorm_2(y, g[3])
        if l < DEPTH_2 - 1:
            yc = token_mixer(hc, *mixer_params, None, None)
            cs = cs + mod_c[5] * rmsnorm_2(yc, g[3])
            cs = ffn_half(cs, mod_c[6], mod_c[7], mod_c[8], g[4], g[5], w_ff_in[l, 1], w_ff_out[l, 1])
        xs = ffn_half(xs, mod_x[6], mod_x[7], mod_x[8], g[4], g[5], w_ff_in[l, 1], w_ff_out[l, 1])
    return xs


def setup_inputs(seed=0):
    out = dict(first_inputs(seed))
    for name, value in second_inputs(seed + 1).items():
        if name != "x":
            out[name + "_2"] = value
    return out


def reference(
    x, positions, attn_norm, w_in, mix_norm_a, mix_norm_b, sinks, w_out, ffn_norm, dense_w_gate,
    dense_w_up, dense_w_down, router, moe_w_gate, moe_w_up, moe_w_down, final_norm, c_2, ctx_2,
    c_ctx_2, w_ada_2, b_ada_2, norm_g_2, w_ff_in_2, w_ff_out_2, w_in_2, hy_conv_w_2,
    hy_conv_b_2, filt_w1_2, filt_b1_2, filt_w2_2, filt_b2_2, filt_w3_2, filt_b3_2, filt_w4_2,
    filt_freq_2, hy_bias_2, lambda_q1_2, lambda_k1_2, lambda_q2_2, lambda_k2_2, subln_g_2,
    w_hy_out_2, w_da_out_2, w_o_2,
):
    x = first_block(
        x, positions, attn_norm, w_in, mix_norm_a, mix_norm_b, sinks, w_out, ffn_norm,
        dense_w_gate, dense_w_up, dense_w_down, router, moe_w_gate, moe_w_up, moe_w_down,
        final_norm,
    )
    return second_block(
        x, c_2, ctx_2, c_ctx_2, w_ada_2, b_ada_2, norm_g_2, w_ff_in_2, w_ff_out_2, w_in_2,
        hy_conv_w_2, hy_conv_b_2, filt_w1_2, filt_b1_2, filt_w2_2, filt_b2_2, filt_w3_2,
        filt_b3_2, filt_w4_2, filt_freq_2, hy_bias_2, lambda_q1_2, lambda_k1_2, lambda_q2_2,
        lambda_k2_2, subln_g_2, w_hy_out_2, w_da_out_2, w_o_2,
    )


_drawn_inputs = setup_inputs


def setup_inputs(seed=0):
    import zlib

    import numpy as np

    out = dict(_drawn_inputs(seed))
    spreads = {}
    factors = {'mix_norm_a': 3.757,
     'mix_norm_b': 3.913,
     'sinks': 4.783,
     'ffn_norm': 3.191,
     'final_norm': 2.795,
     'b_ada_2': 3.733,
     'norm_g_2': 4.8,
     'hy_conv_b_2': 36.881,
     'filt_b1_2': 4.479,
     'filt_b2_2': 4.377,
     'filt_b3_2': 3.135,
     'filt_freq_2': 8.0,
     'lambda_k1_2': 24.632,
     'subln_g_2': 64.0,
     'lambda_q2_2': 3.835,
     'lambda_k2_2': 6.613}
    for name, (base, spread) in spreads.items():
        noise = np.random.default_rng([zlib.crc32(name.encode()), seed]).standard_normal(out[name].shape)
        drawn = base * np.exp(spread * noise) if base else spread * noise
        out[name] = jnp.asarray(drawn.astype(out[name].dtype))
    for name, factor in factors.items():
        out[name] = (out[name] * factor).astype(out[name].dtype)
    return out
```

```python
import math
from contextlib import ExitStack

import numpy as np

import concourse.bass as bass
from concourse import mybir

F32 = mybir.dt.float32
I32 = mybir.dt.int32
U32 = mybir.dt.uint32
ALU = mybir.AluOpType
ACT = mybir.ActivationFunctionType
X = mybir.AxisListType.X

P = 128
SEQ = 256
D = 1024
KC = D // P
TILES = SEQ // P
HD = 64
THETA = 10000.0
FF = 3584
FF2 = 2816
NE = 8
QKV = 2304
BW = 512
FB = 256
NB1 = FF // FB
NB2 = FF2 // FB
NADA = 9 * D // BW
SCALE = HD ** -0.5
LAM_INIT = 0.8 - 0.6 * math.exp(-0.3 * 0)
NEG = -1.0e30
MAGIC = 1.5 * 2.0 ** 23
C1, C2 = 6.28125, float(np.float32(2 * math.pi - 6.28125))
C3 = float(2 * math.pi - C1 - C2)
PI_IN = 3.1415925
CAP = P


def shape_constants():
    L = SEQ
    parts = {}
    parts["ident"] = np.eye(P)
    parts["ones"] = np.ones((P, P))
    i = np.arange(L)[:, None]
    j = np.arange(L)[None, :]
    dist = i - j
    dil = ((dist >= 0) & (dist <= 128)).astype(np.float64)
    dil += (dist >= 0) & (dist % 4 == 0) & (dist <= 512)
    dil += (dist >= 0) & (dist % 16 == 0) & (dist <= 2048)
    win = ((dist >= 0) & (dist <= 127)).astype(np.float64)
    for name, m in (("dil", dil), ("win", win)):
        packed = np.concatenate([m[:P, :P], m[P:, :]], axis=1)
        parts[name + "_count"] = packed
        parts[name + "_bias"] = np.where(packed > 0, 0.0, NEG)
    inv = np.float32(THETA) ** (-np.arange(0, HD, 2, dtype=np.float32) / np.float32(HD))
    parts["inv"] = np.broadcast_to(inv, (P, HD // 2))
    sel = np.zeros((P, 2 * P))
    sel[0, :P] = 1
    sel[1, P:] = 1
    parts["pick"] = sel
    parts["iota"] = np.broadcast_to(np.arange(P), (P, P))
    parts["before"] = np.triu(np.ones((P, P)), 1)
    first = {k: v for k, v in parts.items()}
    parts = {}
    half = HD // 2
    inv2 = np.float32(THETA) ** (-np.arange(0, half, 2, dtype=np.float32) / np.float32(half))
    t = np.arange(L)
    ang = np.stack([(t // 64).astype(np.float32)[:, None] * inv2, (t % 64).astype(np.float32)[:, None] * inv2], 1)
    c, s = np.cos(ang.astype(np.float64)), np.sin(ang.astype(np.float64))
    cc = np.stack([c, c], 2).reshape(L, HD)
    ss = np.stack([-s, s], 2).reshape(L, HD)
    tok = lambda m: m.reshape(TILES, P, -1).transpose(1, 0, 2).reshape(P, -1)
    parts["cos2"], parts["sin2"] = tok(cc), tok(ss)
    f = np.arange(L)[None, :]
    tt = t[:, None]
    w = 2 * math.pi * ((tt * f) % (2 * L)) / (2 * L)
    nyq = (-1.0) ** t
    cos, sin = np.cos(w), np.sin(w)
    sin_u = sin.copy()
    sin_u[:, 0] = nyq
    cos_n = cos[:, :P].copy()
    cos_n[:, 0] = nyq
    parts["dft"] = tok(np.concatenate([cos, sin_u, sin[:, :P], cos_n], 1))
    wt = np.full(L, 2.0)
    wt[0] = 1.0
    ic = (cos * wt[None, :]).T / (2 * L)
    isn = (sin * wt[None, :]).T / (2 * L)
    isn[0] = nyq / (2 * L)
    parts["idft"] = np.concatenate([ic, isn], 0).reshape(4, P, L).transpose(1, 0, 2).reshape(P, -1)
    z = np.zeros((P, L))
    tl = np.linspace(0.0, 1.0, L, dtype=np.float32)
    wl = (2.0 * math.pi * t / L).astype(np.float32)
    fl = np.linspace(1e-4, 15, 16, dtype=np.float32)
    z[0] = tl
    z[1:17] = np.cos((fl[:, None] * wl[None, :]).astype(np.float64))
    z[17:33] = -np.sin((fl[:, None] * wl[None, :]).astype(np.float64))
    parts["zT"] = z
    parts["negt"] = -tl.reshape(TILES, P).T
    rm = np.ones((P, TILES))
    rm[0, 0] = 0.0
    parts["notfirst"] = rm
    dl = np.linspace(math.log(1e-2) / 1.5, math.log(1e-2) / 0.3, D, dtype=np.float32)
    parts["absdelta"] = np.broadcast_to(np.abs(dl), (P, D))

    def pack(ps):
        at, cols, off = {}, [], 0
        for n, m in ps.items():
            m = np.asarray(m, np.float32)
            at[n] = (off, m.shape[1])
            cols.append(m)
            off += m.shape[1]
        return at, np.ascontiguousarray(np.concatenate(cols, 1))
    return pack(first) + pack(parts)


def build(nc, t, out, AT1, N1, AT2, N2):
    ctx = ExitStack()
    with ctx:
        def sb(name, shape, dt=F32):
            return ctx.enter_context(nc.sbuf_tensor(name, shape, dt))

        def sem(name):
            return ctx.enter_context(nc.semaphore(name))

        x = sb("x", [P, TILES, D])
        cs = sb("cs", [P, TILES, D])
        hT = sb("hT", [P, KC, SEQ])
        hcT = sb("hcT", [P, KC, SEQ])
        xn = sb("xn", [P, TILES, D])
        ringA = sb("ringA", [P, 2, KC, BW])
        ringB = sb("ringB", [P, 2, FB // P, D])
        gateG = sb("gateG", [P, 4, D])
        fnrow = sb("fnrow", [P, D])
        c1 = sb("c1", [P, N1])
        vst = sb("vst", [P, 3, P])
        vcol = sb("vcol", [P, 3, P])
        modT = sb("modT", [P, 6, KC, 2])
        adaS = sb("adaS", [P, 3, 2, KC])
        cT = sb("cT", [P, KC, 2])
        sinkr = sb("sinkr", [P, 2, 8])
        rout = sb("rout", [P, KC, NE])
        sg = sb("sg", [P, 2, FB])
        hh = sb("hh", [P, 2, FB])
        hdT = sb("hdT", [P, 2, 2, P])
        ss = sb("ss", [P, 4])
        std = sb("std", [P, 4])
        rr = sb("rr", [P, 4])
        posi = sb("posi", [P, TILES], I32)
        posf = sb("posf", [P, TILES])
        cosT = sb("cosT", [P, TILES, HD])
        sinT = sb("sinT", [P, TILES, HD])
        small = sb("small", [P, 512])
        idx8 = sb("idx8", [P, TILES, 8], U32)
        gates = sb("gates", [P, NE, TILES])
        slots = sb("slots", [P, NE, TILES])
        most = sb("most", [P, 1], I32)
        AR_N = 18688
        arena = sb("arena", [P, AR_N])

        def ar(off, *shape):
            n = int(np.prod(shape))
            assert off + n <= AR_N, (off, n)
            v = arena[:, off:off + n]
            if len(shape) == 1:
                return v
            if len(shape) == 2:
                return v.rearrange("p (a b) -> p a b", a=shape[0])
            return v.rearrange("p (a b c) -> p a b c", a=shape[0], b=shape[1])

        modrow = ar(0, 9 * D)
        grow = ar(9216, 3, D)
        brow = ar(9216 + 3072, 3, D)
        qkv = ar(0, TILES, QKV)
        qr = ar(4608, TILES, 14 * P)
        qkT = ar(8192, 14, SEQ)
        S = ar(11776, 4, 384)
        PT = ar(13312, 4, 384)
        O = ar(14848, TILES, D)
        xgT = ar(0, KC, P)
        ye = ar(1024, D)
        sel = ar(2048, TILES, P)
        selg = ar(2304, TILES, P)
        selgT = ar(2560, TILES, P)
        chosen = ar(2816, TILES, NE)
        KF = ar(0, 5, D)
        c2 = ar(5120, N2)
        H0 = 5120 + N2
        hs, hd, ha = ar(H0, TILES, D), ar(H0 + 2048, TILES, D), ar(H0 + 4096, TILES, D)
        flt = ar(H0 + 6144, 1024)
        decay = ar(H0 + 6144 + 1024, D)
        H0 -= D
        x0T, uT = ar(H0, KC, SEQ), ar(H0 + 2048, KC, SEQ)
        utok = ar(H0 + 4096, TILES, D)
        Y = ar(H0 + 6144, 4, D)
        assert H0 + 6144 + 4096 <= AR_N
        YH = ar(0, TILES, D)
        V2 = ar(2048, 4, D)
        qT2 = ar(6144 + 256, KC, SEQ)
        kT2 = ar(8192 + 256, KC, 2 * SEQ)
        kraw = ar(12288 + 256, 4, D)
        qraw = ar(16384 + 256, TILES, D)
        E2 = ar(12288 + 256, 2, 2, 512)
        PT2 = ar(12288 + 256 + 2048, 2, 512)
        O2 = qraw
        SG = ar(8192 + 256, TILES, 2 * D)
        YD = ar(2048, TILES, D)

        def kv_dst(tt, n, cols):
            return kraw[:, tt, n * BW:n * BW + cols] if n < 2 else V2[:, tt, (n - 2) * BW:(n - 2) * BW + cols]

        def qk_dst(q):
            c, who = q // 3, q % 3
            return qT2[:, c, :] if who == 0 else kT2[:, c, (who - 1) * SEQ:who * SEQ]

        ps = ctx.enter_context(nc.psum_tensor("ps", [P, 8, 512], F32))

        def k1(name):
            o, n = AT1[name]
            return c1[:, o:o + n]

        def k2(name):
            o, n = AT2[name]
            return c2[:, o:o + n]
        ident = k1("ident")
        ones = k1("ones")

        consts_in, vecs_in, x_in, ctx_in, rows_in = (sem(n) for n in ("consts_in", "vecs_in", "x_in", "ctx_in", "rows_in"))
        c2_in, w4_in, filt_in, rope2_in = (sem(n) for n in ("c2_in", "w4_in", "filt_in", "rope2_in"))
        A_full = [[sem(f"A_full{s}{h}") for h in range(2)] for s in range(2)]
        B_full = [sem(f"B_full{s}") for s in range(2)]
        A_lo_free = sem("A_lo_free")
        tile_done = sem("tile_done")
        vt_done, vt_copied, c_silu = sem("vt_done"), sem("vt_copied"), sem("c_silu")
        ada_copied, mt_done, gb_done, gb_used = (sem(n) for n in ("ada_copied", "mt_done", "gb_done", "gb_used"))
        act_step, dve_step = sem("act_step"), sem("dve_step")
        ang_ready, table_ready = sem("ang_ready"), sem("table_ready")
        x_ready = sem("x_ready")
        nrm_std, nrm_xn, nt_tp, nt_act, nt_dve = (sem(n) for n in ("nrm_std", "nrm_xn", "nt_tp", "nt_act", "nt_dve"))
        pj_act, pj_dve = sem("pj_act"), sem("pj_dve")
        silu_done, h_ready, tp_done, hdT_ready, down_done, acc_free = (sem(n) for n in ("silu_done", "h_ready", "tp_done", "hdT_ready", "down_done", "acc_free"))
        gcol_ready = sem("gcol_ready")
        rope_ready, qt_tp, qt_act, qt_dve = (sem(n) for n in ("rope_ready", "qt_tp", "qt_act", "qt_dve"))
        sc_done, nm_ready, e_ready, p_ready = (sem(n) for n in ("sc_done", "nm_ready", "e_ready", "p_ready"))
        pt_done, pt_act, pt_dve, pv_done, o_done = (sem(n) for n in ("pt_done", "pt_act", "pt_dve", "pv_done", "o_done"))
        rt_done, rt_ready, rt_exp = sem("rt_done"), sem("rt_ready"), sem("rt_exp")
        slot_mm, most_ready, col_ready, sel_ready, selg_ready = (sem(n) for n in ("slot_mm", "most_ready", "col_ready", "sel_ready", "selg_ready"))
        gathered, xg_ready, selg_tp, selgT_ready, mixed_back, added = (sem(n) for n in ("gathered", "xg_ready", "selg_tp", "selgT_ready", "mixed_back", "added"))
        f_mm, f_arg, f_sin, f_dec, f_h = (sem(n) for n in ("f_mm", "f_arg", "f_sin", "f_dec", "f_h"))
        k_mm, k_copied, rn_mm = sem("k_mm"), sem("k_copied"), sem("rn_mm")
        z_used, ut_tp, ut_copied, u_mm, y_ready, i_mm, i_used = (sem(n) for n in ("z_used", "ut_tp", "ut_copied", "u_mm", "y_ready", "i_mm", "i_used"))
        lam_ready, sl_sq, sl_std = sem("lam_ready"), sem("sl_sq"), sem("sl_std")
        s2_mm, s2_max, s2_exp, s2_p, s2_tp, s2_pt, s2_pv, s2_o = (sem(n) for n in ("s2_mm", "s2_max", "s2_exp", "s2_p", "s2_tp", "s2_pt", "s2_pv", "s2_o"))
        y_mixed = sem("y_mixed")
        out_done = sem("out_done")

        a, b, s, f, ja, jd = 0, 0, 0, 0, 0, 0
        ph = {}
        A_LANDED, TILES_THROUGH, landed, through = [], [], [[0, 0], [0, 0]], 0

        def take(nb, loads, tiles):
            nonlocal a, through
            for _ in range(nb):
                landed[a % 2][0] += 16 * loads
                A_LANDED.append(landed[a % 2][0])
                through += tiles
                TILES_THROUGH.append(through)
                a += 1

        def proj(name, nb, tiles=2, by="both"):
            nonlocal ja, jd
            ph[name] = dict(a=a, nb=nb, ja=ja, jd=jd, td=through, tiles=tiles, by=by)
            take(nb, 1, tiles)
            ja += {"both": nb * tiles // 2, "act": nb * tiles, "dve": 0}[by]
            jd += {"both": nb * tiles // 2, "dve": nb * tiles, "act": 0}[by]

        def ffn(name, nb, times=1):
            nonlocal b, s, f
            ph[name] = dict(a=a, b=b, s=s, f=f, nb=nb, td=through)
            take(nb * times, 2, TILES)
            b += nb * times
            s += nb * TILES * times
            f += times
        ph["ada"] = dict(a=0, nb=NADA, td=0)
        take(NADA, 1, 1)
        proj("in0", 5)
        proj("out0", 2, by="dve")
        ffn("dense", NB1)
        proj("in1", 5)
        proj("out1", 2, by="dve")
        ffn("moe", NB1, NE)
        ffn("ff0x", NB2)
        ffn("ff0c", NB2)
        ph["z"] = dict(a=a, nb=6, td=through)
        take(6, 1, 4)
        proj("hyo", 2)
        proj("q2", 2)
        proj("kv2", 4, 4)
        proj("dao", 2)
        proj("gt2", 4, by="act")
        proj("wo", 2)
        ffn("ff1", NB2)
        NORMS = ["attn0", "mix0", "ffn0", "attn1", "mix1", "ffn1", "ff0x", "ff0c", "mixx", "mixc", "ff1"]
        call = {n: i for i, n in enumerate(NORMS)}
        XR = {n: i + 1 for i, n in enumerate(["out0", "dense", "out1", "moe", "final", "ff0x", "ff0c", "mixer", "ff1"])}
        SQ = {n: i + 1 for i, n in enumerate(["attn0", "mix0", "ffn0", "attn1", "mix1", "ffn1", "final", "ff0x", "ff0x_out", "ff0c", "ff0c_out",
                                              "mixx", "mixc", "wo_out", "ff1", "ff1_out"])}
        VROWS = (120, 96, 72)

        def pairs(eng, nb, first=0, straight=False):
            lo, hi = first // 2, nb // 2
            if straight:
                for n in range(2 * lo, 2 * hi):
                    yield n, n // 2, n % 2
            elif hi - lo > 1:
                with eng.Fori(lo, hi) as i:
                    for u in range(2):
                        yield i * 2 + u, i, u
            elif hi - lo == 1:
                for u in range(2):
                    yield 2 * lo + u, lo, u
            if nb % 2:
                yield nb - 1, nb // 2, 0

        def emptied(p, i, u, tt):
            T = p["tiles"]
            if p["by"] == "both":
                return (pj_act, i * T + (T // 2 * u + tt // 2 + 1 + p["ja"])) if tt % 2 == 0 else (pj_dve, i * T + (T // 2 * u + tt // 2 + 1 + p["jd"]))
            if p["by"] == "act":
                return pj_act, i * (2 * T) + (T * u + tt + 1 + p["ja"])
            return pj_dve, i * (2 * T) + (T * u + tt + 1 + p["jd"])

        class Chain:

            def __init__(self, eng, sm):
                self.eng, self.sm, self.n = eng, sm, 0

            def done(self, ins):
                ins.then_inc(self.sm, 1)
                self.n += 1
                self.eng.wait_ge(self.sm, self.n)

        block = ctx.enter_context(nc.Block())

        @block.sync
        def _(sp):
            w2d = lambda ap: ap.rearrange("(k p) n -> p k n", p=P)

            def half_free(a, h, i=0, e=0, per=TILES, nb=0):
                if h == 0:
                    sp.wait_ge(A_lo_free, e * nb + i * 2 + (a - 1))
                else:
                    sp.wait_ge(tile_done, e * (nb * per) + i * (2 * per) + TILES_THROUGH[a - 2])

            def load_A(a, n, w, width=BW, first=0, i=0, per=TILES):
                v = w2d(w)
                for h in range(2):
                    if a >= 2:
                        half_free(a, h, i, per=per)
                    sl = slice(4 * h, 4 * h + 4)
                    sp.dma_start(ringA[:, a % 2, sl, 0:width], v[:, sl, bass.ds(n * BW + first, width)]).then_inc(A_full[a % 2][h], 16)

            def load_proj(p, w, first=0):
                for n in range(p["nb"]):
                    load_A(p["a"] + n, n, w, first=first)

            def load_ffn(p, wg, wu, wd, e=0):
                nb = p["nb"]
                vd = wd.rearrange("(k p) n -> p k n", p=P)

                def A(n, i, u):
                    a0 = p["a"] + u
                    for h in range(2):
                        if isinstance(i, int):
                            half_free(a0 + 2 * i, h, 0, e, nb=nb)
                        else:
                            half_free(a0 + 2, h, i - 1, e, nb=nb)
                        sl = slice(4 * h, 4 * h + 4)
                        sp.dma_start(ringA[:, a0 % 2, sl, 0:FB], w2d(wg)[:, sl, bass.ds(n * FB, FB)]).then_inc(A_full[a0 % 2][h], 16)
                        sp.dma_start(ringA[:, a0 % 2, sl, FB:BW], w2d(wu)[:, sl, bass.ds(n * FB, FB)]).then_inc(A_full[a0 % 2][h], 16)

                def B(n, i, u):
                    b0 = p["b"] + u
                    if b0 >= 2 or not isinstance(i, int) or i > 0:
                        sp.wait_ge(down_done, e * (nb * TILES) + i * (2 * TILES) + TILES * (b0 - 1))
                    sp.dma_start(ringB[:, b0 % 2, :, :], vd[:, bass.ds(n * 2, 2), :]).then_inc(B_full[b0 % 2], 16)

                A(0, 0, 0)
                A(1, 0, 1)
                B(0, 0, 0)
                A(2, 1, 0)
                B(1, 0, 1)
                A(3, 1, 1)
                B(2, 1, 0)
                with sp.Fori(2, nb // 2) as i:
                    A(i * 2, i, 0)
                    B(i * 2 - 1, i - 1, 1)
                    A(i * 2 + 1, i, 1)
                    B(i * 2, i, 0)
                m = nb // 2
                if nb % 2:
                    A(nb - 1, m, 0)
                    B(nb - 2, m - 1, 1)
                    B(nb - 1, m, 0)
                else:
                    B(nb - 1, m - 1, 1)

            rows = [("attn_norm", 16), ("ffn_norm", 16), ("mix_norm_a", 8), ("mix_norm_b", 8), ("norm_g_2", 48),
                    ("c_2", 8), ("c_ctx_2", 8), ("hy_bias_2", 8)]
            at = 0
            for n, r in rows:
                sp.dma_start(vst[at:at + r, 0, :], t[n].rearrange("(r q) -> r q", q=P)).then_inc(vecs_in, 16)
                at += r
            sp.dma_start(vst[0:72, 1, :], t["hy_conv_w_2"].rearrange("(r q) -> r q", q=P)).then_inc(vecs_in, 16)
            sp.dma_start(vst[72:96, 1, :], t["hy_conv_b_2"].rearrange("(r q) -> r q", q=P)).then_inc(vecs_in, 16)
            sp.dma_start(vst[0:72, 2, :], t["b_ada_2"].rearrange("(r q) -> r q", q=P)).then_inc(vecs_in, 16)
            sp.dma_start(c1[:, :], t["const1"]).then_inc(consts_in, 16)
            for n in range(2):
                load_A(n, n, t["w_ada_2"])
            sp.dma_start(x[:, :, :], t["x"].rearrange("(t p) n -> p t n", p=P)).then_inc(x_in, 16)
            sp.dma_start(posi[:, :], t["positions"].rearrange("(t p) -> p t", p=P), allow_slow_non_contiguous=True).then_inc(x_in, 16)
            for g, (w, off) in enumerate(((1, 2), (3, 5), (5, 8))):
                sp.dma_start(grow[:, g, :], t["norm_g_2"][w * D:(w + 1) * D].partition_broadcast(P)).then_inc(rows_in, 16)
                sp.dma_start(brow[:, g, :], t["b_ada_2"][off * D:(off + 1) * D].partition_broadcast(P)).then_inc(rows_in, 16)
            sp.dma_start(fnrow[:, :], t["final_norm"].partition_broadcast(P)).then_inc(rows_in, 16)
            sp.dma_start(sinkr[:, :, :].rearrange("p a b -> p (a b)"), t["sinks"].partition_broadcast(P)).then_inc(rows_in, 16)
            sp.dma_start(rout[:, :, :], w2d(t["router"])).then_inc(rows_in, 16)
            sp.dma_start(cs[:, :, :], t["ctx_2"].rearrange("(t p) n -> p t n", p=P)).then_inc(ctx_in, 16)
            with sp.Fori(1, NADA // 2) as i:
                for u in range(2):
                    load_A(2 + u, i * 2 + u, t["w_ada_2"], i=i - 1, per=1)
            for l in range(2):
                wi = t["w_in"][l * D:(l + 1) * D, :]
                p = ph[f"in{l}"]
                for n in range(5):
                    load_A(p["a"] + n, n, wi, FB if n == 4 else BW)
                load_proj(ph[f"out{l}"], t["w_out"][l * D:(l + 1) * D, :])
                if l == 0:
                    load_ffn(ph["dense"], t["dense_w_gate"], t["dense_w_up"], t["dense_w_down"])
            with sp.Fori(0, NE) as e:
                one = lambda w: w[bass.ds(e, 1), :, :].rearrange("o k n -> (o k) n")
                load_ffn(ph["moe"], one(t["moe_w_gate"]), one(t["moe_w_up"]), one(t["moe_w_down"]), e)
            g0 = t["w_ff_in_2"][0:D, 0:FF2], t["w_ff_in_2"][0:D, FF2:2 * FF2], t["w_ff_out_2"][0:FF2, :]
            load_ffn(ph["ff0x"], *g0)
            load_ffn(ph["ff0c"], *g0)
            sp.wait_ge(x_ready, XR["moe"])
            sp.dma_start(c2[:, :], t["const2"]).then_inc(c2_in, 16)
            sp.dma_start(flt[0:33, 0:64], t["filt_w1_2"]).then_inc(filt_in, 16)
            sp.dma_start(flt[0:64, 64:128], t["filt_w2_2"]).then_inc(filt_in, 16)
            sp.dma_start(flt[0:64, 128:192], t["filt_w3_2"]).then_inc(filt_in, 16)
            for n, nm in enumerate(("filt_b1_2", "filt_b2_2", "filt_b3_2", "filt_freq_2")):
                sp.dma_start(flt[0:64, 192 + n:193 + n], t[nm].rearrange("(p o) -> p o", o=1), allow_slow_non_contiguous=True).then_inc(filt_in, 16)
            sp.wait_ge(x_ready, XR["ff0c"])
            sp.dma_start(xn[0:64, :, :].rearrange("p a b -> p (a b)"), t["filt_w4_2"]).then_inc(w4_in, 16)
            load_proj(ph["z"], t["w_in_2"])
            load_proj(ph["hyo"], t["w_hy_out_2"])
            sp.wait_ge(i_used, KC)
            for n, nm in enumerate(("lambda_q1_2", "lambda_k1_2", "lambda_q2_2", "lambda_k2_2")):
                sp.dma_start(small[:, 64 * n:64 * n + 64], t[nm].partition_broadcast(P)).then_inc(rope2_in, 16)
            sp.dma_start(small[:, 256:384], t["subln_g_2"].partition_broadcast(P)).then_inc(rope2_in, 16)
            o = AT2["cos2"][0]
            sp.dma_start(arena[:, 6144:6400], t["const2"][:, o:o + 256]).then_inc(rope2_in, 16)
            load_proj(ph["q2"], t["w_in_2"], 3 * D)
            load_proj(ph["kv2"], t["w_in_2"], 4 * D)
            load_proj(ph["dao"], t["w_da_out_2"])
            load_proj(ph["gt2"], t["w_in_2"], 6 * D)
            load_proj(ph["wo"], t["w_o_2"])
            load_ffn(ph["ff1"], t["w_ff_in_2"][D:2 * D, 0:FF2], t["w_ff_in_2"][D:2 * D, FF2:2 * FF2], t["w_ff_out_2"][FF2:2 * FF2, :])
            sp.wait_ge(x_ready, XR["ff1"])
            sp.dma_start(out.rearrange("(t p) n -> p t n", p=P), x[:, :, :]).then_inc(out_done, 16)
            sp.wait_ge(out_done, 16)

        @block.tensor
        def _(pe):
            mm = nc.tensor.matmul
            tr = nc.tensor.transpose

            def norm(c):
                for k in range(KC):
                    if k == 0:
                        pe.wait_ge(nrm_xn, c + 1)
                    if k >= 2:
                        ev = nt_act if k % 2 == 0 else nt_dve
                        pe.wait_ge(ev, 4 * c + k // 2)
                    for tt in range(TILES):
                        last = tr(ps[:, 2 + k % 2, tt * P:(tt + 1) * P], xn[:, tt, k * P:(k + 1) * P], ident)
                    last.then_inc(nt_tp, 1)

            def norm_ready(c):
                pe.wait_ge(nt_act, 4 * (c + 1))
                pe.wait_ge(nt_dve, 4 * (c + 1))

            def project(p, lhs, bank=lambda u, tt: 4 + 2 * u + tt, last_cols=BW):
                nb, T = p["nb"], p["tiles"]
                if p["ja"]:
                    pe.wait_ge(pj_act, p["ja"])
                    pe.wait_ge(pj_dve, p["jd"])
                for n, i, u in pairs(pe, nb, straight=not p["ja"]):
                    a0 = p["a"] + u
                    cols = last_cols if nb % 2 and isinstance(n, int) and n == nb - 1 else BW
                    for tt in range(T):
                        if not (isinstance(n, int) and n < 2):
                            pe.wait_ge(*emptied(p, i - 1, u, tt))
                        for k in range(KC):
                            if tt == 0 and k % 4 == 0:
                                pe.wait_ge(A_full[a0 % 2][k // 4], i * 16 + A_LANDED[a0])
                            m = mm(ps[:, bank(u, tt), 0:cols], lhs(tt, k), ringA[:, a0 % 2, k, 0:cols], start=k == 0, stop=k == KC - 1)
                            if tt == T - 1 and k == 3:
                                m.then_inc(A_lo_free, 1)
                        m.then_inc(tile_done, 1)

            def feed(p, lhs, e=0):
                nb = p["nb"]
                es = e * (nb * TILES)

                def gu(n, i, u, tt, ks, s):
                    a0 = p["a"] + u
                    for k in ks:
                        if tt == 0 and k % 4 == 0:
                            pe.wait_ge(A_full[a0 % 2][k // 4], e * (16 * nb) + i * 32 + A_LANDED[a0])
                        m = mm(ps[:, tt, :], lhs(tt, k), ringA[:, a0 % 2, k, :], start=k == 0, stop=k == KC - 1)
                        if tt == TILES - 1 and k == 3:
                            m.then_inc(A_lo_free, 1)
                    return m

                def turn(tt, s):
                    pe.wait_ge(h_ready, es + s + 1)
                    if not (isinstance(s, int) and s < 2):
                        pe.wait_ge(hdT_ready, es + s - 1)
                    for q in range(2):
                        m = tr(ps[:, 2 + tt, q * P:(q + 1) * P], hh[:, tt, q * P:(q + 1) * P], ident)
                    m.then_inc(tp_done, 1)

                def down(n, i, u, tt, s, firstblock):
                    b0 = p["b"] + u
                    pe.wait_ge(hdT_ready, es + s + 1)
                    if tt == 0:
                        pe.wait_ge(B_full[b0 % 2], e * (8 * nb) + i * 16 + 16 * (b0 // 2 + 1))
                    for q in range(2):
                        for half in range(2):
                            m = mm(ps[:, 4 + 2 * tt + half, :], hdT[:, tt, q, :], ringB[:, b0 % 2, q, half * 512:(half + 1) * 512],
                                   start=firstblock and q == 0, stop=q == 1, skip_group_check=True)
                    m.then_inc(down_done, 1)
                    return m

                def step(n, i, u, tt, prev, peeled):
                    s = i * 4 + 2 * u + tt + p["s"]
                    if not (isinstance(s, int) and s < 2):
                        pe.wait_ge(h_ready, es + s - 1)
                    gu(n, i, u, tt, range(0, 4), s)
                    if prev:
                        pn, pi, pu, pt, pf = prev
                        sp_ = pi * 4 + 2 * pu + pt + p["s"]
                        turn(pt, sp_)
                    m = gu(n, i, u, tt, range(4, 8), s)
                    m.then_inc(tile_done, 1)
                    if prev:
                        if pf == 1:
                            if p["f"] or not isinstance(e, int):
                                pe.wait_ge(acc_free, e + p["f"])
                        down(pn, pi, pu, pt, sp_, bool(pf))

                step(0, 0, 0, 0, None, True)
                step(0, 0, 0, 1, (0, 0, 0, 0, 1), True)
                step(1, 0, 1, 0, (0, 0, 0, 1, 2), True)
                step(1, 0, 1, 1, (1, 0, 1, 0, 0), True)
                with pe.Fori(1, nb // 2) as i:
                    step(i * 2, i, 0, 0, (i * 2 - 1, i - 1, 1, 1, 0), False)
                    step(i * 2, i, 0, 1, (i * 2, i, 0, 0, 0), False)
                    step(i * 2 + 1, i, 1, 0, (i * 2, i, 0, 1, 0), False)
                    step(i * 2 + 1, i, 1, 1, (i * 2 + 1, i, 1, 0, 0), False)
                m = nb // 2
                tail = (nb - 1, m - 1, 1, 1, 0)
                if nb % 2:
                    step(nb - 1, m, 0, 0, (nb - 2, m - 1, 1, 1, 0), True)
                    step(nb - 1, m, 0, 1, (nb - 1, m, 0, 0, 0), True)
                    tail = (nb - 1, m, 0, 1, 0)
                pn, pi, pu, pt, pf = tail
                sl = pi * 4 + 2 * pu + pt + p["s"]
                turn(pt, sl)
                down(pn, pi, pu, pt, sl, False)

            moe = ph["moe"]
            PER = TILES * NB1

            def gather(e):
                pe.wait_ge(sel_ready, e + 1)
                if not isinstance(e, int) or e >= 2:
                    pe.wait_ge(added, 2 * e - 2)
                for half in range(2):
                    for k in range(4):
                        for tt in range(TILES):
                            o = (4 * half + k) * P
                            last = mm(ps[:, 6 + half, k * P:(k + 1) * P], xn[:, tt, o:o + P], sel[:, tt, :], start=tt == 0, stop=tt == TILES - 1)
                    last.then_inc(gathered, 1)

            def scatter(e, tt):
                if tt == 0:
                    pe.wait_ge(selgT_ready, e + 1)
                    pe.wait_ge(acc_free, e + (moe["f"] + 1))
                    if not isinstance(e, int) or e < NE - 1:
                        pe.wait_ge(xg_ready, 2 * e + 4)
                if tt or isinstance(e, int) and e == NE - 1:
                    pe.wait_ge(added, 2 * e + tt)
                for half in range(2):
                    last = mm(ps[:, 6 + half, :], selgT[:, tt, :], ye[:, half * 512:(half + 1) * 512], start=True, stop=True)
                last.then_inc(mixed_back, 1)

            def expert(e):
                p = moe

                def gu(u, i, ks):
                    a0 = p["a"] + u
                    for k in ks:
                        if k % 4 == 0:
                            pe.wait_ge(A_full[a0 % 2][k // 4], e * (16 * NB1) + i * 32 + A_LANDED[a0])
                        m = mm(ps[:, u, :], xgT[:, k, :], ringA[:, a0 % 2, k, :], start=k == 0, stop=k == KC - 1)
                        if k == 3:
                            m.then_inc(A_lo_free, 1)
                    return m

                def turn(u, i):
                    pe.wait_ge(h_ready, e * PER + i * 4 + (2 * u + 2 + p["s"]))
                    pe.wait_ge(hdT_ready, e * PER + i * 4 + (2 * u + p["s"]))
                    for q in range(2):
                        m = tr(ps[:, 2, q * P:(q + 1) * P], hh[:, u, q * P:(q + 1) * P], ident)
                    m.then_inc(tp_done, 2)

                def down(u, i, first):
                    b0 = p["b"] + u
                    if first:
                        pe.wait_ge(acc_free, e + p["f"])
                    pe.wait_ge(hdT_ready, e * PER + i * 4 + (2 * u + 2 + p["s"]))
                    pe.wait_ge(B_full[b0 % 2], e * (8 * NB1) + i * 16 + 16 * (b0 // 2 + 1))
                    for q in range(2):
                        for half in range(2):
                            m = mm(ps[:, 4 + half, :], hdT[:, u, q, :], ringB[:, b0 % 2, q, half * 512:(half + 1) * 512],
                                   start=first and q == 0, stop=q == 1, skip_group_check=True)
                    m.then_inc(down_done, 2)

                def step(u, i, prev):
                    pe.wait_ge(h_ready, e * PER + i * 4 + (2 * u - 2 + p["s"]))
                    gu(u, i, range(0, 4))
                    if prev:
                        turn(*prev)
                    gu(u, i, range(4, 8)).then_inc(tile_done, 2)
                    if prev:
                        down(*prev, isinstance(i, int) and i == 0)

                pe.wait_ge(xg_ready, 2 * e + 2)
                step(0, 0, None)
                if not isinstance(e, int) or e:
                    scatter(e - 1, 0)
                step(1, 0, (0, 0))
                if not isinstance(e, int) or e:
                    scatter(e - 1, 1)
                with pe.Fori(1, NB1 // 2) as i:
                    step(0, i, (1, i - 1))
                    step(1, i, (0, i))
                if not isinstance(e, int) or e < NE - 1:
                    gather(e + 1)
                pe.wait_ge(selg_ready, e + 1)
                for tt in range(TILES):
                    last = tr(ps[:, 3, tt * P:(tt + 1) * P], selg[:, tt, :], ident)
                last.then_inc(selg_tp, 1)
                turn(1, NB1 // 2 - 1)
                down(1, NB1 // 2 - 1, False)

            def heads(l):
                def head(h):
                    if h < 8:
                        return h // 2, 4 + h // 2, HD * (h % 2), 1024 + HD * h
                    hb = h - 8
                    return 8 + hb // 2, 12 + hb // 4, HD * (hb % 2), 2176 + HD * (hb // 4)
                pe.wait_ge(rope_ready, 2 * l + 1)
                for c in range(14):
                    if c >= 2:
                        pe.wait_ge(qt_act if c % 2 == 0 else qt_dve, 7 * l + c // 2)
                    for tt in range(TILES):
                        if c == 8:
                            pe.wait_ge(rope_ready, 2 * l + 2)
                        last = tr(ps[:, 2 + c % 2, tt * P:(tt + 1) * P], qr[:, tt, c * P:(c + 1) * P], ident)
                    last.then_inc(qt_tp, 1)
                pe.wait_ge(qt_act, 7 * (l + 1))
                pe.wait_ge(qt_dve, 7 * (l + 1))
                for g in range(4):
                    gi = 4 * l + g
                    if gi:
                        pe.wait_ge(nm_ready, gi)
                    for j in range(4):
                        cq, ck, o, _ = head(4 * g + j)
                        mm(ps[:, 4 + j, 0:P], qkT[o:o + HD, cq, 0:P], qkT[o:o + HD, ck, 0:P], start=True, stop=True)
                        last = mm(ps[:, 4 + j, P:384], qkT[o:o + HD, cq, P:SEQ], qkT[o:o + HD, ck, :], start=True, stop=True)
                    last.then_inc(sc_done, 1)
                    pe.wait_ge(p_ready, gi + 1)
                    for j in range(4):
                        if 4 * gi + j >= 2:
                            pe.wait_ge(pt_act if j % 2 == 0 else pt_dve, 2 * gi + j // 2)
                        for q in range(3):
                            last = tr(ps[:, 2 + j % 2, q * P:(q + 1) * P], S[:, j, q * P:(q + 1) * P], ident)
                        last.then_inc(pt_done, 1)
                    if gi:
                        pe.wait_ge(o_done, gi)
                    for j in range(4):
                        v = head(4 * g + j)[3]
                        pe.wait_ge(pt_act if j % 2 == 0 else pt_dve, 2 * gi + j // 2 + 1)
                        mm(ps[:, 0, j * P:j * P + HD], PT[:, j, 0:P], qkv[:, 0, v:v + HD], start=True, stop=True)
                        mm(ps[:, 0, j * P + HD:j * P + P], PT[:, j, P:2 * P], qkv[:, 0, v:v + HD], start=True, stop=False)
                        last = mm(ps[:, 0, j * P + HD:j * P + P], PT[:, j, 2 * P:3 * P], qkv[:, 1, v:v + HD], start=False, stop=True)
                    last.then_inc(pv_done, 1)

            stream = lambda tt, k: hT[:, k, tt * P:(tt + 1) * P]
            both = lambda tt, k: (hT if tt < 2 else hcT)[:, k, (tt % 2) * P:(tt % 2 + 1) * P]

            pe.wait_ge(vecs_in, 16 * 11)
            pe.wait_ge(consts_in, 16)
            for g in range(3):
                r = VROWS[g]
                last = tr(ps[:, 2, g * P:g * P + r], vst[0:r, g, :], ident[0:r, 0:r])
            last.then_inc(vt_done, 1)
            pe.wait_ge(c_silu, 1)
            p = ph["ada"]

            def ada(n, i, u):
                if not (isinstance(i, int) and i == 0):
                    pe.wait_ge(ada_copied, i * 2 + u - 1)
                for k in range(KC):
                    if k % 4 == 0:
                        pe.wait_ge(A_full[u][k // 4], i * 16 + 16)
                    m = mm(ps[0:2, 4 + u, :], cT[:, k, :], ringA[:, u, k, :], start=k == 0, stop=k == KC - 1)
                    if k == 3:
                        m.then_inc(A_lo_free, 1)
                m.then_inc(tile_done, 1)
            ada(0, 0, 0)
            ada(1, 0, 1)
            with pe.Fori(1, NADA // 2) as i:
                ada(i * 2, i, 0)
                ada(i * 2 + 1, i, 1)
            pe.wait_ge(ada_copied, NADA)
            for j, m in enumerate((0, 1, 3, 4, 6, 7)):
                for k in range(KC):
                    o = m * D + k * P
                    last = tr(ps[:, 3, (j * KC + k) * 2:(j * KC + k) * 2 + 2], modrow[0:2, o:o + P], ident[0:2, 0:2])
            last.then_inc(mt_done, 1)
            for g, (m, who) in enumerate(((2, 0), (2, 1), (5, 0), (8, 0))):
                for half in range(2):
                    q = 2 * g + half
                    if q >= 4:
                        pe.wait_ge(gb_used, q - 3)
                    o = m * D + half * 512
                    pk = k1("pick")
                    mm(ps[:, 4 + q % 4, :], pk[0:2, who * P:(who + 1) * P], modrow[0:2, o:o + 512], start=True, stop=True).then_inc(gb_done, 1)

            for l in range(2):
                if l == 0:
                    pe.wait_ge(gb_used, 8)
                norm(call[f"attn{l}"])
                norm_ready(call[f"attn{l}"])
                project(ph[f"in{l}"], stream, last_cols=FB)
                heads(l)
                norm(call[f"mix{l}"])
                norm_ready(call[f"mix{l}"])
                project(ph[f"out{l}"], stream)
                norm(call[f"ffn{l}"])
                norm_ready(call[f"ffn{l}"])
                if l == 0:
                    feed(ph["dense"], stream)
            pe.wait_ge(rows_in, 16 * 9)
            for tt in range(TILES):
                for k in range(KC):
                    last = mm(ps[:, 0, tt * NE:(tt + 1) * NE], stream(tt, k), rout[:, k, :], start=k == 0, stop=k == KC - 1)
            last.then_inc(rt_done, 1)
            pe.wait_ge(rt_ready, 1)
            before, c0 = k1("before"), 2 * NE
            mm(ps[:, 0, c0:c0 + NE], before, chosen[:, 0, :], start=True, stop=True)
            mm(ps[:, 0, c0 + NE:c0 + 2 * NE], before, chosen[:, 1, :], start=True, stop=False)
            mm(ps[:, 0, c0 + NE:c0 + 2 * NE], ones, chosen[:, 0, :], start=False, stop=True)
            for tt in range(TILES):
                last = mm(ps[:, 0, c0 + 2 * NE:c0 + 3 * NE], ones, chosen[:, tt, :], start=tt == 0, stop=tt == TILES - 1)
            last.then_inc(slot_mm, 1)
            pe.wait_ge(most_ready, 2)
            with pe.If(pe.value_load(most[0:1, 0:1], min_val=0, max_val=SEQ) < CAP + 1):
                gather(0)
                expert(0)
                with pe.Fori(1, NE - 1) as e:
                    expert(e)
                expert(NE - 1)
                for tt in range(TILES):
                    scatter(NE - 1, tt)
            with pe.Else():
                with pe.Fori(0, NE) as e:
                    feed(ph["moe"], stream, e)
            norm(call["ff0x"])
            norm_ready(call["ff0x"])
            feed(ph["ff0x"], stream)
            norm(call["ff0c"])
            norm_ready(call["ff0c"])
            feed(ph["ff0c"], lambda tt, k: hcT[:, k, tt * P:(tt + 1) * P])
            pe.wait_ge(c2_in, 16)
            pe.wait_ge(filt_in, 16 * 7)
            pe.wait_ge(w4_in, 16)
            pe.wait_ge(acc_free, ph["ff1"]["f"])
            for j in range(3):
                if j:
                    pe.wait_ge(f_sin, j)
                rhs = k2("zT")[0:33, :] if j == 0 else flt[0:64, 256:512]
                kk = 33 if j == 0 else 64
                mm(ps[0:64, 0, 0:SEQ], flt[0:kk, 64 * j:64 * j + 64], rhs, start=True, stop=True).then_inc(f_mm, 1)
            pe.wait_ge(f_sin, 3)
            for tt in range(TILES):
                if tt:
                    pe.wait_ge(f_h, tt)
                for q in range(4):
                    last = mm(ps[:, 4 + q, :], flt[0:64, 256 + tt * P:256 + (tt + 1) * P],
                              xn[0:64, q // 2, (q % 2) * 512:(q % 2 + 1) * 512], start=True, stop=True)
                last.then_inc(f_mm, 1)
            pe.wait_ge(f_h, 2)
            for c in range(KC):
                for tt in range(TILES):
                    last = mm(ps[:, 0, c:c + 1], ha[:, tt, c * P:(c + 1) * P], ones[:, 0:1], start=tt == 0, stop=tt == TILES - 1)
            last.then_inc(rn_mm, 1)
            dft = k2("dft").rearrange("p (t f) -> p t f", t=TILES)
            colof = [0, P, 4 * P, 3 * P, 5 * P]
            for q in range(10):
                fc, half = q // 2, q % 2
                src = hd if fc in (2, 3) else hs
                if q >= 4:
                    pe.wait_ge(k_copied, q - 3)
                for tt in range(TILES):
                    last = mm(ps[:, 4 + q % 4, :], dft[:, tt, colof[fc]:colof[fc] + P], src[:, tt, half * 512:(half + 1) * 512],
                              start=tt == 0, stop=tt == TILES - 1)
                last.then_inc(k_mm, 1)
            for nm in ("mixx", "mixc"):
                norm(call[nm])
                norm_ready(call[nm])
            pe.wait_ge(k_copied, 10)
            p = ph["z"]
            for n, i, u in pairs(pe, 6, straight=True):
                a0 = p["a"] + u
                for j in range(4):
                    if not (isinstance(n, int) and n == 0):
                        pe.wait_ge(z_used, i * 8 + (4 * u + j - 3))
                    for k in range(KC):
                        if j == 0 and k % 4 == 0:
                            pe.wait_ge(A_full[a0 % 2][k // 4], i * 16 + A_LANDED[a0])
                        m = mm(ps[:, 4 + j, 0:SEQ], ringA[:, a0 % 2, k, j * P:(j + 1) * P], hT[:, k, :], start=k == 0, stop=k == KC - 1)
                        if j == 3 and k == 3:
                            m.then_inc(A_lo_free, 1)
                    m.then_inc(tile_done, 1)
            pe.wait_ge(z_used, 24)
            for tt in range(TILES):
                for half in range(2):
                    q = 2 * tt + half
                    if q >= 2:
                        pe.wait_ge(ut_copied, q - 1)
                    for c in range(4):
                        last = tr(ps[:, 2 + q % 2, c * P:(c + 1) * P], uT[:, 4 * half + c, tt * P:(tt + 1) * P], ident)
                    last.then_inc(ut_tp, 1)
            pe.wait_ge(ut_copied, 4)
            for half in range(2):
                if half:
                    pe.wait_ge(y_ready, 1)
                for fc in range(4):
                    for tt in range(TILES):
                        last = mm(ps[:, 4 + fc, :], dft[:, tt, fc * P:(fc + 1) * P], utok[:, tt, half * 512:(half + 1) * 512],
                                  start=tt == 0, stop=tt == TILES - 1)
                last.then_inc(u_mm, 1)
            idft = k2("idft").rearrange("p (f t) -> p f t", f=4)
            for c in range(KC):
                if c % 4 == 0:
                    pe.wait_ge(y_ready, c // 4 + 1)
                if c >= 2:
                    pe.wait_ge(i_used, c - 1)
                for fc in range(4):
                    last = mm(ps[:, c % 2, 0:SEQ], Y[:, fc, c * P:(c + 1) * P], idft[:, fc, :], start=fc == 0, stop=fc == 3)
                last.then_inc(i_mm, 1)
            pe.wait_ge(i_used, KC)
            project(ph["hyo"], lambda tt, k: uT[:, k, tt * P:(tt + 1) * P])
            project(ph["q2"], stream)
            project(ph["kv2"], both, bank=lambda u, tt: 4 * (1 - u) + tt)
            pe.wait_ge(pj_act, ph["dao"]["ja"])
            pe.wait_ge(pj_dve, ph["dao"]["jd"])
            for c in range(KC):
                for who in range(3):
                    q = 3 * c + who
                    pe.wait_ge(rope_ready, 5 + (0 if who == 0 else 1))
                    if q >= 2:
                        pe.wait_ge(qt_act if q % 2 == 0 else qt_dve, 14 + q // 2)
                    for tt in range(TILES):
                        src = qraw[:, tt, c * P:(c + 1) * P] if who == 0 else kraw[:, 2 * (who - 1) + tt, c * P:(c + 1) * P]
                        last = tr(ps[:, 2 + q % 2, tt * P:(tt + 1) * P], src, ident)
                    last.then_inc(qt_tp, 1)
            pe.wait_ge(qt_act, 14 + 12)
            pe.wait_ge(qt_dve, 14 + 12)

            def scores(n):
                h, tt = n // 2, n % 2
                if n >= 2:
                    pe.wait_ge(s2_exp, n - 1)
                for m in range(2):
                    last = mm(ps[:, 4 + 2 * (n % 2) + m, :], qT2[HD * m:HD * m + HD, h, tt * P:(tt + 1) * P], kT2[HD * m:HD * m + HD, h, :], start=True, stop=True)
                last.then_inc(s2_mm, 1)
            NU = 16
            scores(0)
            for n in range(NU):
                if n + 1 < NU:
                    scores(n + 1)
                h = n // 2
                pe.wait_ge(s2_p, n + 1)
                if n >= 2:
                    pe.wait_ge(s2_pt, n - 1)
                for q in range(4):
                    last = tr(ps[:, 2 + n % 2, q * P:(q + 1) * P], E2[:, n % 2, 0, q * P:(q + 1) * P], ident)
                last.then_inc(s2_tp, 1)
                pe.wait_ge(s2_pt, n + 1)
                if n >= 2:
                    pe.wait_ge(s2_o, n - 1)
                for q in range(4):
                    last = mm(ps[:, n % 2, 0:P], PT2[:, n % 2, q * P:(q + 1) * P], V2[:, q, h * P:(h + 1) * P], start=q == 0, stop=q == 3)
                last.then_inc(s2_pv, 1)
            for c in range(KC):
                if c == 0:
                    pe.wait_ge(sl_std, 2)
                q = 24 + c
                pe.wait_ge(qt_act if q % 2 == 0 else qt_dve, 14 + q // 2)
                for tt in range(TILES):
                    last = tr(ps[:, 2 + q % 2, tt * P:(tt + 1) * P], O2[:, tt, c * P:(c + 1) * P], ident)
                last.then_inc(qt_tp, 1)
            pe.wait_ge(qt_act, 30)
            pe.wait_ge(qt_dve, 30)
            project(ph["dao"], lambda tt, k: hcT[:, k, tt * P:(tt + 1) * P])
            project(ph["gt2"], stream)
            for c in range(KC):
                if c == 0:
                    pe.wait_ge(y_mixed, 1)
                q = 32 + c
                pe.wait_ge(qt_act if q % 2 == 0 else qt_dve, 14 + q // 2)
                for tt in range(TILES):
                    last = tr(ps[:, 2 + q % 2, tt * P:(tt + 1) * P], YH[:, tt, c * P:(c + 1) * P], ident)
                last.then_inc(qt_tp, 1)
            pe.wait_ge(qt_act, 34)
            pe.wait_ge(qt_dve, 34)
            project(ph["wo"], lambda tt, k: hcT[:, k, tt * P:(tt + 1) * P])
            norm(call["ff1"])
            norm_ready(call["ff1"])
            feed(ph["ff1"], stream)

        @block.scalar
        def _(act):
            A = nc.scalar.activation
            ch = Chain(act, act_step)

            def squares(src, nparts, eps, dst=None):
                n = D // nparts
                for tt in range(TILES):
                    for q in range(nparts):
                        j = tt * nparts + q
                        ch.done(A(xn[:, tt, q * n:(q + 1) * n] if dst is None else dst(tt, q), src(tt)[:, q * n:(q + 1) * n], ACT.Square, accum_out=ss[:, j:j + 1]))
                A(std[:, 0:2 * nparts], ss[:, 0:2 * nparts], ACT.Sqrt, bias=epsc[eps], scale=1.0 / n).then_inc(nrm_std, 1)

            epsc = {1e-5: small[:, 500:501], 1e-6: small[:, 501:502]}

            def norm(c, wait, src, scale, bias=None, dst=None, nparts=1, eps=1e-5):
                for sm, v in wait:
                    act.wait_ge(sm, v)
                if c:
                    act.wait_ge(nt_tp, 8 * c)
                squares(src, nparts, eps)
                for k in range(0, KC, 2):
                    act.wait_ge(nt_tp, 8 * c + k + 1)
                    kw = {} if bias is None else dict(bias=bias(k))
                    A(dst[:, k, :], ps[:, 2 + k % 2, 0:SEQ], ACT.Copy if bias is None else ACT.Identity, scale=scale(k), **kw).then_inc(nt_act, 1)

            def copy_out(p, dst, func=ACT.Copy, last_cols=BW, bank=lambda u, tt: 4 + 2 * u + tt, straight=True):
                nb, T = p["nb"], p["tiles"]
                for n, i, u in pairs(act, nb, straight=straight):
                    cols = last_cols if nb % 2 and isinstance(n, int) and n == nb - 1 else BW
                    for tt in range(0, T, 2 if p["by"] == "both" else 1):
                        act.wait_ge(tile_done, i * (2 * T) + (u * T + tt + 1 + p["td"]))
                        A(dst(tt, n, cols), ps[:, bank(u, tt), 0:cols], func).then_inc(pj_act, 1)

            def feed(p, e=0):
                nb = p["nb"]
                es = e * (nb * TILES)

                def step(i, u, tt):
                    s = i * 4 + 2 * u + tt + p["s"]
                    act.wait_ge(tile_done, es + i * 4 + (2 * u + tt + 1 + p["td"]))
                    if not (isinstance(s, int) and s < 2):
                        act.wait_ge(h_ready, es + s - 1)
                    A(sg[:, tt, :], ps[:, tt, 0:FB], ACT.Silu).then_inc(silu_done, 1)
                for u in range(2):
                    for tt in range(TILES):
                        step(0, u, tt)
                with act.Fori(1, nb // 2) as i:
                    for u in range(2):
                        for tt in range(TILES):
                            step(i, u, tt)
                if nb % 2:
                    for tt in range(TILES):
                        step(nb // 2, 0, tt)

            def expert(e):
                p, per = ph["moe"], TILES * NB1
                with act.Fori(0, NB1 // 2) as i:
                    for u in range(2):
                        act.wait_ge(tile_done, e * per + i * 4 + (2 * u + 2 + p["td"]))
                        act.wait_ge(h_ready, e * per + i * 4 + (2 * u - 2 + p["s"]))
                        A(sg[:, u, :], ps[:, u, 0:FB], ACT.Silu).then_inc(silu_done, 2)
                act.wait_ge(selg_tp, e + 1)
                A(selgT[:, :, :].rearrange("p a b -> p (a b)"), ps[:, 3, 0:TILES * P], ACT.Copy).then_inc(selgT_ready, 1)
                act.wait_ge(down_done, e * per + (p["s"] + per))
                A(ye[:, :], ps[:, 4:6, :].rearrange("p a b -> p (a b)"), ACT.Copy).then_inc(acc_free, 1)

            col = lambda r: (lambda k: vcol[:, 0, r + k:r + k + 1])
            act.wait_ge(vt_copied, 1)
            A(cT[:, :, :].rearrange("p k w -> p w k"), vcol[:, 0, 96:112].rearrange("p (w k) -> p w k", w=2), ACT.Silu).then_inc(c_silu, 1)
            act.wait_ge(ang_ready, 1)
            a4 = small[:, 0:128].rearrange("p (t f) -> p t f", t=TILES)
            for tt in range(TILES):
                A(sinT[:, tt, 32:64], a4[:, tt, 0:32], ACT.Sin)
                A(sinT[:, tt, 0:32], a4[:, tt, 0:32], ACT.Sin, scale=-1.0)
                A(cosT[:, tt, 0:32], a4[:, tt, 32:64], ACT.Sin)
                A(cosT[:, tt, 32:64], a4[:, tt, 32:64], ACT.Sin).then_inc(table_ready, 1)

            for l in range(2):
                norm(call[f"attn{l}"], [(x_in, 32)] if l == 0 else [(x_ready, XR["dense"])], lambda tt: x[:, tt, :], col(8 * l), dst=hT)
                copy_out(ph[f"in{l}"], lambda tt, n, cols: qkv[:, tt, n * BW:n * BW + cols], last_cols=FB)
                for c in range(0, 14, 2):
                    act.wait_ge(qt_tp, 14 * l + c + 1)
                    A(qkT[:, c, :], ps[:, 2 + c % 2, 0:SEQ], ACT.Copy).then_inc(qt_act, 1)
                for g in range(4):
                    gi = 4 * l + g
                    act.wait_ge(nm_ready, gi + 1)
                    for j in range(4):
                        for tt in range(TILES):
                            cols = slice(0, P) if tt == 0 else slice(P, 384)
                            last = A(S[:, j, cols], S[:, j, cols], ACT.Exp, bias=small[:, 128 + 2 * j + tt:129 + 2 * j + tt])
                    if g >= 2:
                        last = A(small[:, 144:152], small[:, 136:144], ACT.Exp)
                    last.then_inc(e_ready, 1)
                    for j in (0, 2):
                        act.wait_ge(pt_done, 4 * gi + j + 1)
                        A(PT[:, j, :], ps[:, 2, 0:384], ACT.Copy).then_inc(pt_act, 1)
                mixc = lambda k, l=l: vcol[:, 0, (32 + 4 * l + k if k < 4 else 40 + 4 * l + k - 4):][:, 0:1]
                norm(call[f"mix{l}"], [(o_done, 4 * (l + 1))], lambda tt: O[:, tt, :], mixc, dst=hT, nparts=2)
                norm(call[f"ffn{l}"], [(x_ready, XR[f"out{l}"])], lambda tt: x[:, tt, :], col(16 + 8 * l), dst=hT)
                if l == 0:
                    feed(ph["dense"])
            act.wait_ge(rt_exp, 1)
            A(small[:, 306:308], small[:, 304:306], ACT.Exp).then_inc(rt_exp, 1)
            act.wait_ge(most_ready, 2)
            with act.If(act.value_load(most[0:1, 0:1], min_val=0, max_val=SEQ) < CAP + 1):
                with act.Fori(0, NE) as e:
                    expert(e)
            with act.Else():
                with act.Fori(0, NE) as e:
                    feed(ph["moe"], e)
            act.wait_ge(x_ready, XR["moe"])
            squares(lambda tt: x[:, tt, :], 1, 1e-5)
            for who, (nm, src, dst) in enumerate((("ff0x", x, hT), ("ff0c", cs, hcT))):
                sc = lambda k, who=who: adaS[:, 0, who, k:k + 1]
                bi = lambda k, who=who: modT[:, 0, k, who:who + 1]
                norm(call[nm], [(x_ready, XR["final"]), (ctx_in, 16)] if who == 0 else [(x_ready, XR["ff0x"])], lambda tt: src[:, tt, :], sc, bi, dst=dst, eps=1e-6)
                feed(ph[nm])
                act.wait_ge(down_done, ph[nm]["s"] + 2 * NB2)
                squares(lambda tt: ps[:, 4 + 2 * tt:6 + 2 * tt, :].rearrange("p a b -> p (a b)"), 1, 1e-6)
            for j in range(3):
                act.wait_ge(f_arg, j + 1)
                A(flt[0:64, 256:512], flt[0:64, 512:768], ACT.Sin).then_inc(f_sin, 1)
            for tt in range(TILES):
                if tt:
                    act.wait_ge(f_h, tt)
                A(decay, k2("absdelta"), ACT.Exp, scale=k2("negt")[:, tt:tt + 1]).then_inc(f_dec, 1)
            for q in range(0, 10, 2):
                act.wait_ge(k_mm, q + 1)
                if q:
                    act.wait_ge(k_copied, q)
                A(KF[:, q // 2, 0:512], ps[:, 4 + q % 4, :], ACT.Copy).then_inc(k_copied, 1)
            for who, (nm, src, dst) in enumerate((("mixx", x, hT), ("mixc", cs, hcT))):
                sc = lambda k, who=who: adaS[:, 1, who, k:k + 1]
                bi = lambda k, who=who: modT[:, 2, k, who:who + 1]
                norm(call[nm], [(x_ready, XR["ff0c"]), (f_mm, 5)], lambda tt: src[:, tt, :], sc, bi, dst=dst, eps=1e-6)
            for q in range(4):
                act.wait_ge(ut_tp, q + 1)
                A(utok[:, q // 2, (q % 2) * 512:(q % 2 + 1) * 512], ps[:, 2 + q % 2, :], ACT.Copy).then_inc(ut_copied, 1)
            act.wait_ge(i_used, KC)
            copy_out(ph["hyo"], lambda tt, n, cols: YH[:, tt, n * BW:(n + 1) * BW])
            copy_out(ph["q2"], lambda tt, n, cols: qraw[:, tt, n * BW:(n + 1) * BW])
            copy_out(ph["kv2"], kv_dst, bank=lambda u, tt: 4 * (1 - u) + tt)
            for q in range(0, 24, 2):
                act.wait_ge(qt_tp, 28 + q + 1)
                A(qk_dst(q), ps[:, 2, 0:SEQ], ACT.Copy).then_inc(qt_act, 1)
            act.wait_ge(lam_ready, 1)
            A(small[:, 388:390], small[:, 384:386], ACT.Exp).then_inc(lam_ready, 1)
            def weigh(n):
                act.wait_ge(s2_max, n + 1)
                if n >= 2:
                    act.wait_ge(s2_tp, n - 1)
                for m in range(2):
                    last = A(E2[:, n % 2, m, :], ps[:, 4 + 2 * (n % 2) + m, :], ACT.Exp, bias=small[:, 400 + 2 * (n % 2) + m:401 + 2 * (n % 2) + m],
                             scale=SCALE, accum_out=small[:, 404 + 2 * (n % 2) + m:405 + 2 * (n % 2) + m])
                last.then_inc(s2_exp, 1)
            weigh(0)
            for n in range(16):
                if n < 15:
                    weigh(n + 1)
                act.wait_ge(s2_tp, n + 1)
                if n >= 2:
                    act.wait_ge(s2_pv, n - 1)
                A(PT2[:, n % 2, :], ps[:, 2 + n % 2, :], ACT.Copy).then_inc(s2_pt, 1)
            act.wait_ge(sl_sq, 1)
            A(small[:, 432:448], small[:, 416:432], ACT.Sqrt, scale=1.0 / P, bias=epsc[1e-6]).then_inc(sl_std, 1)
            for q in range(24, 32, 2):
                act.wait_ge(qt_tp, 28 + q + 1)
                A(hcT[:, q - 24, :], ps[:, 2, 0:SEQ], ACT.Copy).then_inc(qt_act, 1)
            copy_out(ph["dao"], lambda tt, n, cols: YD[:, tt, n * BW:(n + 1) * BW])
            copy_out(ph["gt2"], lambda tt, n, cols: SG[:, tt, n * BW:(n + 1) * BW], ACT.Sigmoid)
            for q in range(32, 40, 2):
                act.wait_ge(qt_tp, 28 + q + 1)
                A(hcT[:, q - 32, :], ps[:, 2, 0:SEQ], ACT.Copy).then_inc(qt_act, 1)
            copy_out(ph["wo"], lambda tt, n, cols: YH[:, tt, n * BW:(n + 1) * BW])
            act.wait_ge(pj_dve, ph["wo"]["jd"] + 2)
            act.wait_ge(pj_act, ph["wo"]["ja"] + 2)
            squares(lambda tt: YH[:, tt, :], 1, 1e-6)
            sc = lambda k: adaS[:, 2, 0, k:k + 1]
            bi = lambda k: modT[:, 4, k, 0:1]
            norm(call["ff1"], [(x_ready, XR["mixer"])], lambda tt: x[:, tt, :], sc, bi, dst=hT, eps=1e-6)
            feed(ph["ff1"])
            act.wait_ge(down_done, ph["ff1"]["s"] + 2 * NB2)
            squares(lambda tt: ps[:, 4 + 2 * tt:6 + 2 * tt, :].rearrange("p a b -> p (a b)"), 1, 1e-6)

        @block.vector
        def _(dve):
            V = nc.vector
            ch = Chain(dve, dve_step)

            def wait(*pairs_):
                for sm, v in pairs_:
                    dve.wait_ge(sm, v)

            def norm(c, name, src, scale, dst, bias=None, nparts=1):
                n = D // nparts
                dve.wait_ge(nrm_std, SQ[name])
                ch.done(V.reciprocal(rr[:, 0:2 * nparts], std[:, 0:2 * nparts]))
                for tt in range(TILES):
                    for q in range(nparts):
                        j = tt * nparts + q
                        last = V.tensor_scalar(xn[:, tt, q * n:(q + 1) * n], src[:, tt, q * n:(q + 1) * n], rr[:, j:j + 1], None, ALU.mult)
                last.then_inc(nrm_xn, 1)
                for k in range(1, KC, 2):
                    dve.wait_ge(nt_tp, 8 * c + k + 1)
                    if bias is None:
                        V.tensor_scalar(dst[:, k, :], ps[:, 3, 0:SEQ], scale(k), None, ALU.mult).then_inc(nt_dve, 1)
                    else:
                        V.tensor_scalar(dst[:, k, :], ps[:, 3, 0:SEQ], scale(k), bias(k), ALU.mult, ALU.add).then_inc(nt_dve, 1)

            def copy_out(p, dst, last_cols=BW, bank=lambda u, tt: 4 + 2 * u + tt):
                nb, T = p["nb"], p["tiles"]
                for n, i, u in pairs(dve, nb, straight=True):
                    cols = last_cols if nb % 2 and n == nb - 1 else BW
                    for tt in range(1, T, 2):
                        dve.wait_ge(tile_done, n * T + tt + 1 + p["td"])
                        V.tensor_copy(dst(tt, n, cols), ps[:, bank(u, tt), 0:cols]).then_inc(pj_dve, 1)

            def add_out(p):
                for n in range(p["nb"]):
                    for tt in range(TILES):
                        dve.wait_ge(tile_done, 2 * n + tt + 1 + p["td"])
                        xs = x[:, tt, n * BW:(n + 1) * BW]
                        V.tensor_tensor(xs, xs, ps[:, 4 + 2 * (n % 2) + tt, :], ALU.add).then_inc(pj_dve, 1)
                dve.wait_ge(pj_dve, p["jd"] + 2 * p["nb"])
                dve.sem_inc(x_ready, 1)

            def reduce_angle(src, dst, k):
                ch.done(V.tensor_scalar(k, src, 1.0 / (2 * math.pi), MAGIC, ALU.mult, ALU.add))
                ch.done(V.tensor_scalar(k, k, MAGIC, None, ALU.subtract))
                ch.done(V.scalar_tensor_tensor(dst, k, -C1, src, ALU.mult, ALU.add))
                ch.done(V.scalar_tensor_tensor(dst, k, -C2, dst, ALU.mult, ALU.add))
                ch.done(V.scalar_tensor_tensor(dst, k, -C3, dst, ALU.mult, ALU.add))
                ch.done(V.tensor_scalar(dst, dst, PI_IN, -PI_IN, ALU.min, ALU.max))

            def feed(p, e=0):
                nb = p["nb"]
                es = e * (nb * TILES)

                def step(i, u, tt):
                    s = i * 4 + 2 * u + tt + p["s"]
                    old = not (isinstance(s, int) and s < 2)
                    dve.wait_ge(silu_done, es + s + 1)
                    if old:
                        dve.wait_ge(tp_done, es + s - 1)
                    V.tensor_tensor(hh[:, tt, :], sg[:, tt, :], ps[:, tt, FB:BW], ALU.mult).then_inc(h_ready, 1)
                    dve.wait_ge(tp_done, es + s + 1)
                    if old:
                        dve.wait_ge(down_done, es + s - 1)
                    V.tensor_copy(hdT[:, tt, :, :].rearrange("p a b -> p (a b)"), ps[:, 2 + tt, 0:FB]).then_inc(hdT_ready, 1)
                for u in range(2):
                    for tt in range(TILES):
                        step(0, u, tt)
                with dve.Fori(1, nb // 2) as i:
                    for u in range(2):
                        for tt in range(TILES):
                            step(i, u, tt)
                if nb % 2:
                    for tt in range(TILES):
                        step(nb // 2, 0, tt)
                dve.wait_ge(down_done, es + (p["s"] + nb * TILES))

            def one_hot(e, n, gated):
                flat = lambda v: v[:, bass.ds(e, 1), :].rearrange("p o t -> p (o t)")
                pcol, gcol = (small[:, 346:348], small[:, 348:350]) if gated else (small[:, 350:352], small[:, 352:354])
                V.tensor_copy(pcol, flat(slots))
                V.tensor_copy(gcol, flat(gates)).then_inc(col_ready, 1)
                dve.wait_ge(col_ready, n)
                for tt in range(TILES):
                    if gated:
                        last = V.tensor_scalar(selg[:, tt, :], k1("iota"), pcol[:, tt:tt + 1], gcol[:, tt:tt + 1], ALU.is_equal, ALU.mult)
                    else:
                        last = V.tensor_scalar(sel[:, tt, :], k1("iota"), pcol[:, tt:tt + 1], None, ALU.is_equal)
                last.then_inc(selg_ready if gated else sel_ready, 1)

            def dispatch(e):
                for half in range(2):
                    dve.wait_ge(gathered, 2 * e + (half + 1))
                    g = vcol[:, 0, 24 + 4 * half:28 + 4 * half].unsqueeze(2).broadcast_to([P, 4, P])
                    V.tensor_tensor(xgT[:, 4 * half:4 * half + 4, :], ps[:, 6 + half, :].rearrange("p (k s) -> p k s", k=4), g, ALU.mult).then_inc(xg_ready, 1)

            def add(e, tt):
                dve.wait_ge(mixed_back, 2 * e + (tt + 1))
                V.tensor_tensor(x[:, tt, :], x[:, tt, :], ps[:, 6:8, :].rearrange("p a b -> p (a b)"), ALU.add).then_inc(added, 1)
                dve.wait_ge(added, 2 * e + (tt + 1))

            def expert(e):
                p, per = ph["moe"], TILES * NB1
                first, final = isinstance(e, int) and e == 0, isinstance(e, int) and e == NE - 1

                def gate(u, i):
                    dve.wait_ge(silu_done, e * per + i * 4 + (2 * u + 2 + p["s"]))
                    dve.wait_ge(tp_done, e * per + i * 4 + (2 * u - 2 + p["s"]))
                    V.tensor_tensor(hh[:, u, :], sg[:, u, :], ps[:, u, FB:BW], ALU.mult).then_inc(h_ready, 2)

                def move(u, i):
                    dve.wait_ge(tp_done, e * per + i * 4 + (2 * u + 2 + p["s"]))
                    dve.wait_ge(down_done, e * per + i * 4 + (2 * u - 2 + p["s"]))
                    V.tensor_copy(hdT[:, u, :, :].rearrange("p a b -> p (a b)"), ps[:, 2, 0:FB]).then_inc(hdT_ready, 2)
                for u in range(2):
                    gate(u, 0)
                    move(u, 0)
                    if not first:
                        add(e - 1, u)
                if not first:
                    dve.wait_ge(selg_tp, e)
                one_hot(e, 2 * e + 2, True)
                if not final:
                    dve.wait_ge(gathered, 2 * e + 2)
                    one_hot(e + 1, 2 * e + 3, False)
                with dve.Fori(1, NB1 // 2 - 1) as i:
                    for u in range(2):
                        gate(u, i)
                        move(u, i)
                gate(0, NB1 // 2 - 1)
                move(0, NB1 // 2 - 1)
                gate(1, NB1 // 2 - 1)
                if not final:
                    dispatch(e + 1)
                move(1, NB1 // 2 - 1)

            def acc(tt):
                return ps[:, 4 + 2 * tt:6 + 2 * tt, :].rearrange("p a b -> p (a b)")

            def post(name, src, g, stream, signal):
                dve.wait_ge(nrm_std, SQ[name])
                ch.done(V.reciprocal(rr[:, 0:2], std[:, 0:2]))
                for tt in range(TILES):
                    last = V.scalar_tensor_tensor(xn[:, tt, :], src(tt), rr[:, tt:tt + 1], gateG[:, g, :], ALU.mult, ALU.mult)
                if signal:
                    last.then_inc(acc_free, 1)
                    dve.wait_ge(acc_free, signal)
                else:
                    ch.done(last)
                V.tensor_tensor(stream[:, :, :], stream[:, :, :], xn[:, :, :], ALU.add).then_inc(x_ready, 1)

            col = lambda r: (lambda k: vcol[:, 0, r + k:r + k + 1])
            V.memset(small[:, 500:501], 1e-5)
            V.memset(small[:, 501:502], 1e-6)
            ch.done(V.memset(small[:, 502:503], 0.0))
            wait((vt_done, 1))
            for g in range(3):
                last = V.tensor_copy(vcol[:, g, 0:VROWS[g]], ps[:, 2, g * P:g * P + VROWS[g]])
            last.then_inc(vt_copied, 1)
            wait((x_in, 32))
            ch.done(V.tensor_copy(posf[:, :], posi[:, :]))
            ang = small[:, 0:128].rearrange("p (t f) -> p t f", t=TILES)
            for tt in range(TILES):
                ch.done(V.tensor_scalar(small[:, 128:160], k1("inv"), posf[:, tt:tt + 1], None, ALU.mult))
                reduce_angle(small[:, 128:160], ang[:, tt, 0:32], small[:, 160:192])
                ch.done(V.scalar_tensor_tensor(ang[:, tt, 32:64], ang[:, tt, 0:32], -1.0, ang[:, tt, 0:32], ALU.mult, ALU.max))
                ch.done(V.tensor_scalar(ang[:, tt, 32:64], ang[:, tt, 32:64], -1.0, math.pi / 2, ALU.mult, ALU.add))
            dve.sem_inc(ang_ready, 1)
            def ada(n, i, u):
                dve.wait_ge(tile_done, i * 2 + u + 1)
                V.tensor_copy(modrow[0:2, bass.ds(n * BW, BW)], ps[0:2, 4 + u, :]).then_inc(ada_copied, 1)
            for n, i, u in pairs(dve, NADA):
                ada(n, i, u)
            wait((mt_done, 1))
            for j, m in enumerate((0, 1, 3, 4, 6, 7)):
                last = V.tensor_tensor(modT[:, j, :, :], ps[:, 3, j * 16:(j + 1) * 16].rearrange("p (k w) -> p k w", w=2),
                                       vcol[:, 2, 8 * m:8 * m + 8].unsqueeze(2).broadcast_to([P, KC, 2]), ALU.add)
            ch.done(last)
            for j in range(3):
                for who in range(2):
                    last = V.scalar_tensor_tensor(adaS[:, j, who, :], modT[:, 2 * j + 1, :, who], 1.0, vcol[:, 0, 48 + 16 * j:56 + 16 * j], ALU.add, ALU.mult)
            ch.done(last)
            wait((rows_in, 16 * 9))
            for g, (w, fac) in enumerate(((0, 0.5), (0, 0.5), (1, 1.0), (2, 0.5))):
                for half in range(2):
                    c = slice(half * 512, (half + 1) * 512)
                    dve.wait_ge(gb_done, 2 * g + half + 1)
                    V.tensor_tensor(gateG[:, g, c], ps[:, 4 + (2 * g + half) % 4, :], brow[:, w, c], ALU.add).then_inc(gb_used, 1)
                    dve.wait_ge(gb_used, 2 * g + half + 1)
                    ch.done(V.scalar_tensor_tensor(gateG[:, g, c], gateG[:, g, c], fac, grow[:, w, c], ALU.mult, ALU.mult))

            def rotate(dst, src, G, Ax, cos, sin, dup=False):
                hw = HD // (2 * Ax)
                n = G * HD
                a1, a2 = xn[:, 0, 0:n], xn[:, 1, 0:n]
                g2 = lambda v: v.rearrange("p (g d) -> p g d", g=G)
                V.tensor_tensor(g2(a1), g2(src), cos.unsqueeze(1).broadcast_to([P, G, HD]), ALU.mult)
                for h in range(2):
                    v = lambda z, hh_: z.rearrange("p (g a h w) -> p g a h w", g=G, a=Ax, h=2)[:, :, :, hh_, :]
                    sv = sin.rearrange("p (a h w) -> p a h w", a=Ax, h=2)[:, :, h, :].unsqueeze(1).broadcast_to([P, G, Ax, hw])
                    last = V.tensor_tensor(v(a2, h), v(src, 1 - h), sv, ALU.mult)
                ch.done(last)
                if dup:
                    b_ = lambda z: g2(z).unsqueeze(2).broadcast_to([P, G, 2, HD])
                    return V.tensor_tensor(dst.rearrange("p (g u d) -> p g u d", g=G, u=2), b_(a1), b_(a2), ALU.add)
                return V.tensor_tensor(dst, a1, a2, ALU.add)

            for l in range(2):
                norm(call[f"attn{l}"], f"attn{l}", x, col(8 * l), hT)
                copy_out(ph[f"in{l}"], lambda tt, n, cols: qkv[:, tt, n * BW:n * BW + cols], last_cols=FB)
                if l == 0:
                    wait((table_ready, 2))
                wait((pj_act, ph[f"in{l}"]["ja"] + 5), (pj_dve, ph[f"in{l}"]["jd"] + 5))
                for tt in range(TILES):
                    ch.done(rotate(qr[:, tt, 0:D], qkv[:, tt, 0:D], 16, 1, cosT[:, tt, :], sinT[:, tt, :]))
                dve.sem_inc(rope_ready, 1)
                for tt in range(TILES):
                    ch.done(rotate(qr[:, tt, D:D + 512], qkv[:, tt, 1536:2048], 8, 1, cosT[:, tt, :], sinT[:, tt, :]))
                    ch.done(rotate(qr[:, tt, D + 512:D + 768], qkv[:, tt, 2048:2176], 2, 1, cosT[:, tt, :], sinT[:, tt, :], dup=True))
                dve.sem_inc(rope_ready, 1)
                for c in range(1, 14, 2):
                    dve.wait_ge(qt_tp, 14 * l + c + 1)
                    V.tensor_copy(qkT[:, c, :], ps[:, 3, 0:SEQ]).then_inc(qt_dve, 1)
                nm2 = lambda o: small[:, o:o + 8].rearrange("p (j t) -> p j t", t=TILES)
                for g in range(4):
                    gi = 4 * l + g
                    kind = "dil" if g < 2 else "win"
                    rep = lambda m: k1(m).unsqueeze(1).broadcast_to([P, 4, 384])
                    dve.wait_ge(sc_done, gi + 1)
                    if gi:
                        dve.wait_ge(pt_done, 4 * gi)
                    ch.done(V.scalar_tensor_tensor(S[:, :, :], ps[:, 4:8, 0:384], SCALE, rep(kind + "_bias"), ALU.mult, ALU.add))
                    V.tensor_reduce(nm2(168)[:, :, 0], S[:, :, 0:P], X, ALU.max)
                    ch.done(V.tensor_reduce(nm2(168)[:, :, 1], S[:, :, P:384], X, ALU.max))
                    if g >= 2:
                        sk = sinkr[:, l, 4 * (g - 2):4 * (g - 2) + 4].unsqueeze(2).broadcast_to([P, 4, 2])
                        ch.done(V.tensor_tensor(nm2(168), nm2(168), sk, ALU.max))
                        ch.done(V.tensor_tensor(nm2(136), sk, nm2(168), ALU.subtract))
                    V.tensor_scalar(small[:, 128:136], small[:, 168:176], -1.0, None, ALU.mult).then_inc(nm_ready, 1)
                    dve.wait_ge(e_ready, gi + 1)
                    V.tensor_tensor(S[:, :, :], S[:, :, :], rep(kind + "_count"), ALU.mult).then_inc(p_ready, 1)
                    dve.wait_ge(p_ready, gi + 1)
                    V.tensor_reduce(nm2(152)[:, :, 0], S[:, :, 0:P], X, ALU.add)
                    ch.done(V.tensor_reduce(nm2(152)[:, :, 1], S[:, :, P:384], X, ALU.add))
                    if g >= 2:
                        ch.done(V.tensor_tensor(small[:, 152:160], small[:, 152:160], small[:, 144:152], ALU.add))
                    ch.done(V.reciprocal(small[:, 160:168], small[:, 152:160]))
                    for j in (1, 3):
                        dve.wait_ge(pt_done, 4 * gi + j + 1)
                        V.tensor_copy(PT[:, j, :], ps[:, 3, 0:384]).then_inc(pt_dve, 1)
                    dve.wait_ge(pv_done, gi + 1)
                    for tt in range(TILES):
                        last = V.tensor_tensor(O[:, tt, g * SEQ:(g + 1) * SEQ].rearrange("p (j d) -> p j d", j=4),
                                               ps[:, 0, :].rearrange("p (j t d) -> p j t d", j=4, t=TILES)[:, :, tt, :],
                                               nm2(160)[:, :, tt:tt + 1].broadcast_to([P, 4, HD]), ALU.mult)
                    last.then_inc(o_done, 1)
                mixc = lambda k, l=l: vcol[:, 0, (32 + 4 * l + k if k < 4 else 40 + 4 * l + k - 4):][:, 0:1]
                norm(call[f"mix{l}"], f"mix{l}", O, mixc, hT, nparts=2)
                add_out(ph[f"out{l}"])
                norm(call[f"ffn{l}"], f"ffn{l}", x, col(16 + 8 * l), hT)
                if l == 0:
                    feed(ph["dense"])
                    for tt in range(TILES):
                        last = V.tensor_tensor(x[:, tt, :], x[:, tt, :], acc(tt), ALU.add)
                    last.then_inc(acc_free, 1)
                    dve.wait_ge(acc_free, 1)
                    dve.sem_inc(x_ready, 1)
            wait((rt_done, 1))
            lg = small[:, 256:272].rearrange("p (t e) -> p t e", t=TILES)
            top = small[:, 272:288].rearrange("p (t e) -> p t e", t=TILES)
            ixf = small[:, 288:304].rearrange("p (t e) -> p t e", t=TILES)
            ch.done(V.tensor_copy(small[:, 256:272], ps[:, 0, 0:16]))
            for tt in range(TILES):
                ch.done(V.max(top[:, tt, :], lg[:, tt, :]))
                ch.done(V.max_index(idx8[:, tt, :], top[:, tt, :], lg[:, tt, :]))
                ch.done(V.tensor_copy(ixf[:, tt, :], idx8[:, tt, :]))
            V.tensor_tensor(small[:, 304:306], top[:, :, 1], top[:, :, 0], ALU.subtract).then_inc(rt_exp, 1)
            wait((rt_exp, 2))
            ch.done(V.tensor_scalar(small[:, 308:310], small[:, 306:308], 1.0, None, ALU.add))
            ch.done(V.reciprocal(small[:, 310:312], small[:, 308:310]))
            ch.done(V.tensor_tensor(small[:, 312:314], small[:, 306:308], small[:, 310:312], ALU.mult))
            for tt in range(TILES):
                V.tensor_scalar(small[:, 320:328], k1("iota")[:, 0:NE], ixf[:, tt, 0:1], small[:, 310 + tt:311 + tt], ALU.is_equal, ALU.mult)
                ch.done(V.tensor_scalar(small[:, 328:336], k1("iota")[:, 0:NE], ixf[:, tt, 1:2], small[:, 312 + tt:313 + tt], ALU.is_equal, ALU.mult))
                ch.done(V.tensor_tensor(gates[:, :, tt], small[:, 320:328], small[:, 328:336], ALU.add))
                ch.done(V.tensor_scalar(chosen[:, tt, :], k1("iota")[:, 0:NE], ixf[:, tt, 0:1], None, ALU.is_equal))
                ch.done(V.scalar_tensor_tensor(chosen[:, tt, :], k1("iota")[:, 0:NE], ixf[:, tt, 1:2], chosen[:, tt, :], ALU.is_equal, ALU.add))
            dve.sem_inc(rt_ready, 1)
            dve.wait_ge(slot_mm, 1)
            c0 = 2 * NE
            for tt in range(TILES):
                ch.done(V.scalar_tensor_tensor(slots[:, :, tt], ps[:, 0, c0 + tt * NE:c0 + (tt + 1) * NE], 1.0, chosen[:, tt, :], ALU.add, ALU.mult))
            ch.done(V.tensor_scalar(slots[:, :, :], slots[:, :, :], 1.0, None, ALU.subtract))
            V.tensor_reduce(small[:, 344:345], ps[:, 0, c0 + 2 * NE:c0 + 3 * NE], X, ALU.max).then_inc(most_ready, 1)
            dve.wait_ge(most_ready, 1)
            V.tensor_copy(most[:, :], small[:, 344:345]).then_inc(most_ready, 1)
            dve.wait_ge(most_ready, 2)
            p = ph["moe"]
            gcol = small[:, 340:342]
            with dve.If(dve.value_load(most[0:1, 0:1], min_val=0, max_val=SEQ) < CAP + 1):
                one_hot(0, 1, False)
                dispatch(0)
                expert(0)
                with dve.Fori(1, NE - 1) as e:
                    expert(e)
                expert(NE - 1)
                for tt in range(TILES):
                    add(NE - 1, tt)
                dve.wait_ge(added, TILES * NE)
            with dve.Else():
                with dve.Fori(0, NE) as e:
                    feed(p, e)
                    dve.wait_ge(acc_free, e + 1)
                    V.tensor_copy(gcol, gates[:, bass.ds(e, 1), :].rearrange("p o t -> p (o t)")).then_inc(gcol_ready, 1)
                    dve.wait_ge(gcol_ready, e + 1)
                    for tt in range(TILES):
                        last = V.scalar_tensor_tensor(x[:, tt, :], acc(tt), gcol[:, tt:tt + 1], x[:, tt, :], ALU.mult, ALU.add)
                    last.then_inc(acc_free, 1)
                dve.wait_ge(acc_free, 1 + NE)
            dve.sem_inc(x_ready, 1)
            dve.wait_ge(nrm_std, SQ["final"])
            ch.done(V.reciprocal(rr[:, 0:2], std[:, 0:2]))
            for tt in range(TILES):
                last = V.scalar_tensor_tensor(x[:, tt, :], x[:, tt, :], rr[:, tt:tt + 1], fnrow[:, :], ALU.mult, ALU.mult)
            last.then_inc(x_ready, 1)
            for who, (nm, src, dst) in enumerate((("ff0x", x, hT), ("ff0c", cs, hcT))):
                sc = lambda k, who=who: adaS[:, 0, who, k:k + 1]
                bi = lambda k, who=who: modT[:, 0, k, who:who + 1]
                if who == 0:
                    wait((x_ready, XR["final"]))
                norm(call[nm], nm, src, sc, dst, bi)
                feed(ph[nm])
                post(nm + "_out", acc, who, src, ph[nm]["f"] + 1)
            wait((c2_in, 16), (filt_in, 16 * 7))
            fa, fk, fr = flt[0:64, 512:768], flt[0:64, 768:1024], decay[0:64, 0:256]
            for j in range(3):
                dve.wait_ge(f_mm, j + 1)
                ch.done(V.tensor_scalar(fr, ps[0:64, 0, 0:SEQ], flt[0:64, 192 + j:193 + j], flt[0:64, 195:196], ALU.add, ALU.mult))
                reduce_angle(fr, fa, fk)
                dve.sem_inc(f_arg, 1)
            nf = k2("notfirst")
            for tt in range(TILES):
                wait((f_mm, 4 + tt), (f_dec, tt + 1))
                two = lambda o: ps[:, o:o + 2, :].rearrange("p a b -> p (a b)")
                V.tensor_tensor(hs[:, tt, :], two(4), decay, ALU.mult)
                ch.done(V.scalar_tensor_tensor(hd[:, tt, :], two(6), nf[:, tt:tt + 1], decay, ALU.mult, ALU.mult))
                V.scalar_tensor_tensor(ha[:, tt, :], hd[:, tt, :], -1.0, hd[:, tt, :], ALU.mult, ALU.max)
                ch.done(V.scalar_tensor_tensor(decay, hs[:, tt, :], -1.0, hs[:, tt, :], ALU.mult, ALU.max))
                ch.done(V.tensor_tensor(ha[:, tt, :], ha[:, tt, :], decay, ALU.add))
                ch.done(V.tensor_tensor(decay, hs[:, tt, :], hd[:, tt, :], ALU.add))
                ch.done(V.tensor_tensor(hd[:, tt, :], hs[:, tt, :], hd[:, tt, :], ALU.subtract))
                V.tensor_copy(hs[:, tt, :], decay).then_inc(f_h, 1)
            wait((rn_mm, 1))
            rn = small[:, 460:468]
            ch.done(V.tensor_scalar(rn, ps[:, 0, 0:KC], 1e-6, None, ALU.add))
            ch.done(V.reciprocal(rn, rn))
            for q in range(1, 10, 2):
                wait((k_mm, q + 1), (k_copied, q))
                V.tensor_copy(KF[:, q // 2, 512:D], ps[:, 4 + q % 4, :]).then_inc(k_copied, 1)
            for who, (nm, src, dst) in enumerate((("mixx", x, hT), ("mixc", cs, hcT))):
                sc = lambda k, who=who: adaS[:, 1, who, k:k + 1]
                bi = lambda k, who=who: modT[:, 2, k, who:who + 1]
                norm(call[nm], nm, src, sc, dst, bi)
            w = lambda j, c: vcol[:, 1, 24 * j + c:24 * j + c + 1]
            for c in range(24):
                bk = ps[:, 4 + c % 4, :]
                dst = x0T[:, c, :] if c < 8 else uT[:, c - 8, :] if c < 16 else xn[:, 0, 0:SEQ]
                dve.wait_ge(tile_done, ph["z"]["td"] + c + 1)
                ch.done(V.tensor_scalar(dst, bk[:, 0:SEQ], w(1, c), vcol[:, 1, 72 + c:73 + c], ALU.mult, ALU.add))
                ch.done(V.scalar_tensor_tensor(dst[:, 1:SEQ], bk[:, 0:SEQ - 1], w(0, c), dst[:, 1:SEQ], ALU.mult, ALU.add))
                last = V.scalar_tensor_tensor(dst[:, 0:SEQ - 1], bk[:, 1:SEQ], w(2, c), dst[:, 0:SEQ - 1], ALU.mult, ALU.add)
                if c >= 16:
                    ch.done(last)
                    last = V.tensor_tensor(uT[:, c - 16, :], uT[:, c - 16, :], dst, ALU.mult)
                last.then_inc(z_used, 1)
                dve.wait_ge(z_used, c + 1)
            for half in range(2):
                cs_ = slice(half * 512, (half + 1) * 512)
                t1, t2 = xn[:, 0, 0:512], xn[:, 0, 512:D]
                dve.wait_ge(u_mm, half + 1)
                for fc in range(2):
                    re, im = ps[:, 4 + fc, :], ps[:, 6 + fc, :]
                    V.tensor_tensor(Y[:, fc, cs_], re, KF[:, fc, cs_], ALU.mult)
                    V.tensor_tensor(t1, im, KF[:, 2 + fc, cs_], ALU.mult)
                    V.tensor_tensor(Y[:, 2 + fc, cs_], re, KF[:, 2 + fc, cs_], ALU.mult)
                    ch.done(V.tensor_tensor(t2, im, KF[:, 4 if fc == 0 else 1, cs_], ALU.mult))
                    V.tensor_tensor(Y[:, fc, cs_], Y[:, fc, cs_], t1, ALU.subtract)
                    last = V.tensor_tensor(Y[:, 2 + fc, cs_], Y[:, 2 + fc, cs_], t2, ALU.add)
                    if fc == 0:
                        ch.done(last)
                last.then_inc(y_ready, 1)
                dve.wait_ge(y_ready, half + 1)
            for c in range(KC):
                tmp = xn[:, 0, 0:SEQ]
                ch.done(V.tensor_scalar(tmp, uT[:, c, :], vcol[:, 0, 112 + c:113 + c], None, ALU.mult))
                dve.wait_ge(i_mm, c + 1)
                ch.done(V.scalar_tensor_tensor(tmp, ps[:, c % 2, 0:SEQ], rn[:, c:c + 1], tmp, ALU.mult, ALU.add))
                V.tensor_tensor(uT[:, c, :], tmp, x0T[:, c, :], ALU.mult).then_inc(i_used, 1)
                dve.wait_ge(i_used, c + 1)
            copy_out(ph["hyo"], lambda tt, n, cols: YH[:, tt, n * BW:(n + 1) * BW])
            copy_out(ph["q2"], lambda tt, n, cols: qraw[:, tt, n * BW:(n + 1) * BW])
            wait((rope2_in, 16 * 6), (pj_act, ph["kv2"]["ja"]), (pj_dve, ph["kv2"]["jd"]))
            cos2 = arena[:, 6144:6272].rearrange("p (t d) -> p t d", t=TILES)
            sin2 = arena[:, 6272:6400].rearrange("p (t d) -> p t d", t=TILES)
            for tt in range(TILES):
                ch.done(rotate(qraw[:, tt, :], qraw[:, tt, :], 16, 2, cos2[:, tt, :], sin2[:, tt, :]))
            dve.sem_inc(rope_ready, 1)
            copy_out(ph["kv2"], kv_dst, bank=lambda u, tt: 4 * (1 - u) + tt)
            wait((pj_act, ph["dao"]["ja"]), (pj_dve, ph["dao"]["jd"]))
            for tt in range(TILES):
                ch.done(rotate(kraw[:, tt, :], kraw[:, tt, :], 16, 2, cos2[:, tt, :], sin2[:, tt, :]))
            dve.sem_inc(rope_ready, 1)
            for j in range(2):
                o = 128 * j
                ch.done(V.tensor_tensor(small[:, o:o + 64], small[:, o:o + 64], small[:, o + 64:o + 128], ALU.mult))
                ch.done(V.tensor_reduce(small[:, 384 + j:385 + j], small[:, o:o + 64], X, ALU.add))
            dve.sem_inc(lam_ready, 1)
            for q in range(1, 24, 2):
                dve.wait_ge(qt_tp, 28 + q + 1)
                V.tensor_copy(qk_dst(q), ps[:, 3, 0:SEQ]).then_inc(qt_dve, 1)
            wait((lam_ready, 2))
            lam = small[:, 390:391]
            ch.done(V.tensor_tensor(lam, small[:, 388:389], small[:, 389:390], ALU.subtract))
            ch.done(V.tensor_scalar(lam, lam, LAM_INIT, None, ALU.add))

            def rowmax(n):
                m = 2 * (n % 2)
                dve.wait_ge(s2_mm, n + 1)
                ch.done(V.tensor_reduce(small[:, 396 + m:398 + m], ps[:, 4 + m:6 + m, :], X, ALU.max))
                V.tensor_scalar(small[:, 400 + m:402 + m], small[:, 396 + m:398 + m], -SCALE, None, ALU.mult).then_inc(s2_max, 1)

            def gather_out(n):
                h, tt = n // 2, n % 2
                dve.wait_ge(s2_pv, n + 1)
                V.tensor_copy(O2[:, tt, h * P:(h + 1) * P], ps[:, n % 2, 0:P]).then_inc(s2_o, 1)
            rowmax(0)
            for n in range(16):
                m = 2 * (n % 2)
                if n < 15:
                    rowmax(n + 1)
                dve.wait_ge(s2_exp, n + 1)
                ri = small[:, 408 + m:410 + m]
                ch.done(V.reciprocal(ri, small[:, 404 + m:406 + m]))
                ch.done(V.tensor_tensor(ri[:, 1:2], ri[:, 1:2], lam, ALU.mult))
                e0, e1 = E2[:, n % 2, 0, :], E2[:, n % 2, 1, :]
                ch.done(V.tensor_scalar(e1, e1, ri[:, 1:2], None, ALU.mult))
                V.scalar_tensor_tensor(e0, e0, ri[:, 0:1], e1, ALU.mult, ALU.subtract).then_inc(s2_p, 1)
                if n:
                    gather_out(n - 1)
            gather_out(15)
            dve.wait_ge(s2_o, 16)
            ch.done(V.tensor_tensor(xn[:, :, :], O2[:, :, :], O2[:, :, :], ALU.mult))
            V.tensor_reduce(small[:, 416:432], xn[:, :, :].rearrange("p t (h d) -> p (t h) d", d=P), X, ALU.add).then_inc(sl_sq, 1)
            dve.wait_ge(sl_std, 1)
            ch.done(V.reciprocal(small[:, 416:432], small[:, 432:448]))
            o16 = O2[:, :, :].rearrange("p t (h d) -> p (t h) d", d=P)
            ch.done(V.tensor_tensor(o16, o16, small[:, 416:432].unsqueeze(2).broadcast_to([P, 16, P]), ALU.mult))
            V.scalar_tensor_tensor(o16, o16, 1.0 - LAM_INIT, small[:, 256:384].unsqueeze(1).broadcast_to([P, 16, P]), ALU.mult, ALU.mult).then_inc(sl_std, 1)
            for q in range(25, 32, 2):
                dve.wait_ge(qt_tp, 28 + q + 1)
                V.tensor_copy(hcT[:, q - 24, :], ps[:, 3, 0:SEQ]).then_inc(qt_dve, 1)
            copy_out(ph["dao"], lambda tt, n, cols: YD[:, tt, n * BW:(n + 1) * BW])
            wait((pj_act, ph["wo"]["ja"]), (pj_dve, ph["wo"]["jd"]))
            V.tensor_tensor(YD[:, :, :], YD[:, :, :], SG[:, :, D:2 * D], ALU.mult)
            ch.done(V.tensor_tensor(YH[:, :, :], YH[:, :, :], SG[:, :, 0:D], ALU.mult))
            V.tensor_tensor(YH[:, :, :], YH[:, :, :], YD[:, :, :], ALU.add).then_inc(y_mixed, 1)
            for q in range(33, 40, 2):
                dve.wait_ge(qt_tp, 28 + q + 1)
                V.tensor_copy(hcT[:, q - 32, :], ps[:, 3, 0:SEQ]).then_inc(qt_dve, 1)
            copy_out(ph["wo"], lambda tt, n, cols: YH[:, tt, n * BW:(n + 1) * BW])
            post("wo_out", lambda tt: YH[:, tt, :], 2, x, 0)
            sc = lambda k: adaS[:, 2, 0, k:k + 1]
            bi = lambda k: modT[:, 4, k, 0:1]
            norm(call["ff1"], "ff1", x, sc, hT, bi)
            feed(ph["ff1"])
            post("ff1_out", acc, 3, x, ph["ff1"]["f"] + 1)


LAYOUT = {
    "x": (SEQ, D), "positions": (SEQ,), "attn_norm": (-1,), "w_in": (2 * D, QKV), "mix_norm_a": (-1,), "mix_norm_b": (-1,),
    "sinks": (-1,), "w_out": (2 * D, D), "ffn_norm": (-1,), "dense_w_gate": (D, FF), "dense_w_up": (D, FF), "dense_w_down": (FF, D),
    "router": (D, NE), "moe_w_gate": (NE, D, FF), "moe_w_up": (NE, D, FF), "moe_w_down": (NE, FF, D), "final_norm": (D,),
    "c_2": (D,), "ctx_2": (SEQ, D), "c_ctx_2": (D,), "w_ada_2": (D, 9 * D), "b_ada_2": (-1,), "norm_g_2": (-1,),
    "w_ff_in_2": (2 * D, 2 * FF2), "w_ff_out_2": (2 * FF2, D), "w_in_2": (D, 8 * D), "hy_conv_w_2": (-1,), "hy_conv_b_2": (-1,),
    "filt_w1_2": (33, 64), "filt_b1_2": (64,), "filt_w2_2": (64, 64), "filt_b2_2": (64,), "filt_w3_2": (64, 64), "filt_b3_2": (64,),
    "filt_w4_2": (64, 2 * D), "filt_freq_2": (64,), "hy_bias_2": (-1,), "lambda_q1_2": (64,), "lambda_k1_2": (64,),
    "lambda_q2_2": (64,), "lambda_k2_2": (64,), "subln_g_2": (P,), "w_hy_out_2": (D, D), "w_da_out_2": (D, D), "w_o_2": (D, D),
}


def kernel(**inputs):
    import concourse.bacc as bacc
    from concourse.bass_utils import run_bass_kernel_spmd as run

    nc = bacc.Bacc("TRN2", target_bir_lowering=False, num_devices=1)
    at1, const1, at2, const2 = shape_constants()
    arrays = {n: np.ascontiguousarray(inputs[n]).reshape(s) for n, s in LAYOUT.items()}
    arrays["const1"], arrays["const2"] = const1, const2
    t = {n: nc.dram_tensor(f"in_{n}", a.shape, mybir.dt.from_np(a.dtype), kind="ExternalInput").ap() for n, a in arrays.items()}
    out = nc.dram_tensor("out", (SEQ, D), F32, kind="ExternalOutput").ap()
    build(nc, t, out, at1, const1.shape[1], at2, const2.shape[1])
    r = run(nc, [{f"in_{n}": a for n, a in arrays.items()}], core_ids=[0])
    return r.results[0]["out"].reshape(1, SEQ, D)
```

```python
import math
from contextlib import ExitStack

import numpy as np

import concourse.bass as bass
from concourse import mybir

F32 = mybir.dt.float32
F32R = mybir.dt.float32r
I32 = mybir.dt.int32
U32 = mybir.dt.uint32
ALU = mybir.AluOpType
ACT = mybir.ActivationFunctionType
X = mybir.AxisListType.X

P = 128
SEQ = 256
D = 1024
KC = D // P
TILES = SEQ // P
HD = 64
THETA = 10000.0
FF = 3584
FF2 = 2816
NE = 8
QKV = 2304
BW = 512
FB = 256
NB1 = FF // FB
NB2 = FF2 // FB
NADA = 9 * D // BW
SCALE = HD ** -0.5
LAM_INIT = 0.8 - 0.6 * math.exp(-0.3 * 0)
NEG = -1.0e30
MAGIC = 1.5 * 2.0 ** 23
C1, C2 = 6.28125, float(np.float32(2 * math.pi - 6.28125))
C3 = float(2 * math.pi - C1 - C2)
PI_IN = 3.1415925
CAP = P


def shape_constants():
    L = SEQ
    parts = {}
    parts["ident"] = np.eye(P)
    parts["ones"] = np.ones((P, P))
    i = np.arange(L)[:, None]
    j = np.arange(L)[None, :]
    dist = i - j
    dil = ((dist >= 0) & (dist <= 128)).astype(np.float64)
    dil += (dist >= 0) & (dist % 4 == 0) & (dist <= 512)
    dil += (dist >= 0) & (dist % 16 == 0) & (dist <= 2048)
    win = ((dist >= 0) & (dist <= 127)).astype(np.float64)
    for name, m in (("dil", dil), ("win", win)):
        packed = np.concatenate([m[:P, :P], m[P:, :]], axis=1)
        parts[name + "_count"] = packed
        parts[name + "_bias"] = np.where(packed > 0, 0.0, NEG)
    inv = np.float32(THETA) ** (-np.arange(0, HD, 2, dtype=np.float32) / np.float32(HD))
    parts["inv"] = np.broadcast_to(inv, (P, HD // 2))
    sel = np.zeros((P, 2 * P))
    sel[0, :P] = 1
    sel[1, P:] = 1
    parts["pick"] = sel
    parts["iota"] = np.broadcast_to(np.arange(P), (P, P))
    parts["before"] = np.triu(np.ones((P, P)), 1)
    first = {k: v for k, v in parts.items()}
    parts = {}
    half = HD // 2
    inv2 = np.float32(THETA) ** (-np.arange(0, half, 2, dtype=np.float32) / np.float32(half))
    t = np.arange(L)
    ang = np.stack([(t // 64).astype(np.float32)[:, None] * inv2, (t % 64).astype(np.float32)[:, None] * inv2], 1)
    c, s = np.cos(ang.astype(np.float64)), np.sin(ang.astype(np.float64))
    cc = np.stack([c, c], 2).reshape(L, HD)
    ss = np.stack([-s, s], 2).reshape(L, HD)
    tok = lambda m: m.reshape(TILES, P, -1).transpose(1, 0, 2).reshape(P, -1)
    parts["cos2"], parts["sin2"] = tok(cc), tok(ss)
    f = np.arange(L)[None, :]
    tt = t[:, None]
    w = 2 * math.pi * ((tt * f) % (2 * L)) / (2 * L)
    nyq = (-1.0) ** t
    cos, sin = np.cos(w), np.sin(w)
    sin_u = sin.copy()
    sin_u[:, 0] = nyq
    cos_n = cos[:, :P].copy()
    cos_n[:, 0] = nyq
    parts["dft"] = tok(np.concatenate([cos, sin_u, sin[:, :P], cos_n], 1))
    wt = np.full(L, 2.0)
    wt[0] = 1.0
    ic = (cos * wt[None, :]).T / (2 * L)
    isn = (sin * wt[None, :]).T / (2 * L)
    isn[0] = nyq / (2 * L)
    parts["idft"] = np.concatenate([ic, isn], 0).reshape(4, P, L).transpose(1, 0, 2).reshape(P, -1)
    z = np.zeros((P, L))
    tl = np.linspace(0.0, 1.0, L, dtype=np.float32)
    wl = (2.0 * math.pi * t / L).astype(np.float32)
    fl = np.linspace(1e-4, 15, 16, dtype=np.float32)
    z[0] = tl
    z[1:17] = np.cos((fl[:, None] * wl[None, :]).astype(np.float64))
    z[17:33] = -np.sin((fl[:, None] * wl[None, :]).astype(np.float64))
    parts["zT"] = z
    parts["negt"] = -tl.reshape(TILES, P).T
    rm = np.ones((P, TILES))
    rm[0, 0] = 0.0
    parts["notfirst"] = rm
    dl = np.linspace(math.log(1e-2) / 1.5, math.log(1e-2) / 0.3, D, dtype=np.float32)
    parts["absdelta"] = np.broadcast_to(np.abs(dl), (P, D))

    def pack(ps):
        at, cols, off = {}, [], 0
        for n, m in ps.items():
            m = np.asarray(m, np.float32)
            at[n] = (off, m.shape[1])
            cols.append(m)
            off += m.shape[1]
        return at, np.ascontiguousarray(np.concatenate(cols, 1))
    return pack(first) + pack(parts)


def build(nc, t, out, AT1, N1, AT2, N2):
    ctx = ExitStack()
    with ctx:
        def sb(name, shape, dt=F32):
            return ctx.enter_context(nc.sbuf_tensor(name, shape, dt))

        def sem(name):
            return ctx.enter_context(nc.semaphore(name))

        x = sb("x", [P, TILES, D])
        cs = sb("cs", [P, TILES, D])
        hT = sb("hT", [P, KC, SEQ])
        hcT = sb("hcT", [P, KC, SEQ])
        xn = sb("xn", [P, TILES, D])
        ringA = sb("ringA", [P, 2, KC, BW])
        ringB = sb("ringB", [P, 2, FB // P, D])
        gateG = sb("gateG", [P, 4, D])
        fnrow = sb("fnrow", [P, D])
        c1 = sb("c1", [P, N1])
        vst = sb("vst", [P, 3, P])
        vcol = sb("vcol", [P, 3, P])
        modT = sb("modT", [P, 6, KC, 2])
        adaS = sb("adaS", [P, 3, 2, KC])
        cT = sb("cT", [P, KC, 2])
        arow = sb("arow", [P, 2, BW])
        sinkr = sb("sinkr", [P, 2, 8])
        rout = sb("rout", [P, KC, NE])
        sg = sb("sg", [P, 2, FB])
        hh = sb("hh", [P, 2, FB])
        ss = sb("ss", [P, 4])
        std = sb("std", [P, 4])
        rr = sb("rr", [P, 4])
        posi = sb("posi", [P, TILES], I32)
        posf = sb("posf", [P, TILES])
        cosT = sb("cosT", [P, TILES, HD])
        sinT = sb("sinT", [P, TILES, HD])
        small = sb("small", [P, 512])
        idx8 = sb("idx8", [P, TILES, 8], U32)
        gates = sb("gates", [P, NE, TILES])
        slots = sb("slots", [P, NE, TILES])
        most = sb("most", [P, 1], I32)
        AR_N = 18688
        with nc.sbuf_tensor("arena", [P, AR_N], F32) as arena:
            pass
        with nc.sbuf_tensor("xs", [P, 2, KC, SEQ], F32R) as xs:
            pass
        SHARED = 2 * KC * P + TILES * P * 3 + TILES * NE
        sb("below", [P, SHARED])
        xgs = sb("xgs", [P, 2, KC, P], F32R)
        As = sb("As", [P, 2, 2, KC // 2, BW], F32R)
        Bs = sb("Bs", [P, FB // P, 2, D], F32R)
        hds = sb("hds", [P, 2, 2, FB // P, P], F32R)
        f32 = lambda v: v.bitcast(F32)

        def ar(off, *shape):
            n = int(np.prod(shape))
            assert off + n <= AR_N, (off, n)
            v = arena[:, off:off + n]
            if len(shape) == 1:
                return v
            if len(shape) == 2:
                return v.rearrange("p (a b) -> p a b", a=shape[0])
            return v.rearrange("p (a b c) -> p a b c", a=shape[0], b=shape[1])

        vec_row = arow[:, :, :].rearrange("p w n -> p (w n)")
        qkv = ar(0, TILES, QKV)
        qr = ar(4608, TILES, 14 * P)
        qkT = ar(8192, 14, SEQ)
        S = ar(11776, 4, 384)
        PT = ar(13312, 4, 384)
        O = ar(14848, TILES, D)
        xgT = ar(0, KC, P)
        ye = ar(1024, D)
        sel = ar(2048, TILES, P)
        selg = ar(2304, TILES, P)
        selgT = ar(2560, TILES, P)
        chosen = ar(2816, TILES, NE)
        KF = ar(0, 5, D)
        c2 = ar(5120, N2)
        H0 = 5120 + N2
        hs, hd, ha = ar(H0, TILES, D), ar(H0 + 2048, TILES, D), ar(H0 + 4096, TILES, D)
        flt = ar(H0 + 6144, 1024)
        decay = ar(H0 + 6144 + 1024, D)
        H0 -= D
        x0T, uT = ar(H0, KC, SEQ), ar(H0 + 2048, KC, SEQ)
        utok = ar(H0 + 4096, TILES, D)
        Y = ar(H0 + 6144, 4, D)
        assert H0 + 6144 + 4096 <= AR_N
        YH = ar(0, TILES, D)
        V2 = ar(2048, 4, D)
        qT2 = ar(6144 + 256, KC, SEQ)
        kT2 = ar(8192 + 256, KC, 2 * SEQ)
        kraw = ar(12288 + 256, 4, D)
        qraw = ar(16384 + 256, TILES, D)
        E2 = ar(12288 + 256, 2, 2, 512)
        PT2 = ar(12288 + 256 + 2048, 2, 512)
        O2 = qraw
        SGh, SGd = gateG[:, 0:2, :], cs
        YD = ar(2048, TILES, D)

        def kv_dst(tt, n, cols):
            return kraw[:, tt, n * BW:n * BW + cols] if n < 2 else V2[:, tt, (n - 2) * BW:(n - 2) * BW + cols]

        def qk_dst(q):
            c, who = q // 3, q % 3
            return qT2[:, c, :] if who == 0 else kT2[:, c, (who - 1) * SEQ:who * SEQ]

        ps = ctx.enter_context(nc.psum_tensor("ps", [P, 8, 512], F32))

        def k1(name):
            o, n = AT1[name]
            return c1[:, o:o + n]

        def k2(name):
            o, n = AT2[name]
            return c2[:, o:o + n]
        ident = k1("ident")
        ones = k1("ones")

        consts_in, vecs_in, x_in, ctx_in, rows_in = (sem(n) for n in ("consts_in", "vecs_in", "x_in", "ctx_in", "rows_in"))
        c2_in, w4_in, filt_in, rope2_in = (sem(n) for n in ("c2_in", "w4_in", "filt_in", "rope2_in"))
        A_full = [[sem(f"A_full{s}{h}") for h in range(2)] for s in range(2)]
        B_full = [sem(f"B_full{s}") for s in range(2)]
        A_lo_free = sem("A_lo_free")
        tile_done = sem("tile_done")
        vt_done, vt_copied, c_silu = sem("vt_done"), sem("vt_copied"), sem("c_silu")
        row_copied, spread, spread_copied, gain_in, pool_step, mods_ready = (sem(n) for n in ("row_copied", "spread", "spread_copied", "gain_in", "pool_step", "mods_ready"))
        act_step, dve_step = sem("act_step"), sem("dve_step")
        ang_ready, table_ready = sem("ang_ready"), sem("table_ready")
        x_ready = sem("x_ready")
        nrm_std, nrm_xn, nt_tp, nt_act, nt_dve = (sem(n) for n in ("nrm_std", "nrm_xn", "nt_tp", "nt_act", "nt_dve"))
        pj_act, pj_dve = sem("pj_act"), sem("pj_dve")
        silu_done, h_ready, tp_done, hdT_ready, down_done, acc_free = (sem(n) for n in ("silu_done", "h_ready", "tp_done", "hdT_ready", "down_done", "acc_free"))
        A_high, A_split = sem("A_high"), sem("A_split")
        B_high, B_low0, B_low1 = sem("B_high"), sem("B_low0"), sem("B_low1")
        hd_high = sem("hd_high")
        xs_high, xs_split, xr_high, xr_split, xg_high, xg_split = (sem(n) for n in ("xs_high", "xs_split", "xr_high", "xr_split", "xg_high", "xg_split"))
        gcol_ready = sem("gcol_ready")
        rope_ready, qt_tp, qt_act, qt_dve = (sem(n) for n in ("rope_ready", "qt_tp", "qt_act", "qt_dve"))
        sc_done, nm_ready, e_ready, p_ready = (sem(n) for n in ("sc_done", "nm_ready", "e_ready", "p_ready"))
        pt_done, pt_act, pt_dve, pv_done, o_done = (sem(n) for n in ("pt_done", "pt_act", "pt_dve", "pv_done", "o_done"))
        rt_done, rt_ready, rt_exp = sem("rt_done"), sem("rt_ready"), sem("rt_exp")
        slot_mm, most_ready, col_ready, sel_ready, selg_ready = (sem(n) for n in ("slot_mm", "most_ready", "col_ready", "sel_ready", "selg_ready"))
        gathered, xg_ready, selg_tp, selgT_ready, mixed_back, added = (sem(n) for n in ("gathered", "xg_ready", "selg_tp", "selgT_ready", "mixed_back", "added"))
        f_mm, f_arg, f_sin, f_dec, f_h = (sem(n) for n in ("f_mm", "f_arg", "f_sin", "f_dec", "f_h"))
        k_mm, k_copied, rn_mm = sem("k_mm"), sem("k_copied"), sem("rn_mm")
        z_used, ut_tp, ut_copied, u_mm, y_ready, i_mm, i_used = (sem(n) for n in ("z_used", "ut_tp", "ut_copied", "u_mm", "y_ready", "i_mm", "i_used"))
        lam_ready, sl_sq, sl_std = sem("lam_ready"), sem("sl_sq"), sem("sl_std")
        s2_mm, s2_max, s2_exp, s2_p, s2_tp, s2_pt, s2_pv, s2_o = (sem(n) for n in ("s2_mm", "s2_max", "s2_exp", "s2_p", "s2_tp", "s2_pt", "s2_pv", "s2_o"))
        gates_open = sem("gates_open")
        y_mixed = sem("y_mixed")
        out_done = sem("out_done")

        a, b, s, f, ja, jd, q, xc = 0, 0, 0, 0, 0, 0, 0, 0
        ph = {}
        A_LANDED, TILES_THROUGH, landed, through = [], [], [[0, 0], [0, 0]], 0
        SPLIT = {}

        def take(nb, loads, tiles):
            nonlocal a, through
            for _ in range(nb):
                landed[a % 2][0] += 16 * loads
                A_LANDED.append(landed[a % 2][0])
                through += tiles
                TILES_THROUGH.append(through)
                a += 1

        def proj(name, nb, tiles=2, by="both"):
            nonlocal ja, jd
            ph[name] = dict(a=a, nb=nb, ja=ja, jd=jd, td=through, tiles=tiles, by=by)
            take(nb, 1, tiles)
            ja += {"both": nb * tiles // 2, "act": nb * tiles, "dve": 0}[by]
            jd += {"both": nb * tiles // 2, "dve": nb * tiles, "act": 0}[by]

        def ffn(name, nb, times=1):
            nonlocal b, s, f, q, xc
            ph[name] = dict(a=a, b=b, s=s, f=f, nb=nb, td=through, q=q, xc=xc)
            SPLIT.update((a + n, q + n) for n in range(nb * times))
            take(nb * times, 2, TILES)
            q += nb * times
            xc += 1 if times == 1 else 0
            b += nb * times
            s += nb * TILES * times
            f += times
        def ada(l):
            ph[f"ada{l}"] = dict(a=a, td=through)
            take(NADA // 2, 1, 1)
        proj("in0", 5)
        ada(0)
        proj("out0", 2, by="dve")
        ffn("dense", NB1)
        proj("in1", 5)
        ada(1)
        proj("out1", 2, by="dve")
        ffn("moe", NB1, NE)
        ffn("ff0c", NB2)
        ffn("ff0x", NB2)
        ph["z"] = dict(a=a, nb=6, td=through)
        take(6, 1, 4)
        proj("hyo", 2)
        proj("q2", 2)
        proj("kv2", 4, 4)
        proj("gt2", 4, by="act")
        proj("dao", 2, by="dve")
        proj("wo", 2)
        ffn("ff1", NB2)
        NORMS = ["attn0", "mix0", "ffn0", "attn1", "mix1", "ff0c", "ffn1", "ff0x", "mixc", "mixx", "ff1"]
        call = {n: i for i, n in enumerate(NORMS)}
        XR = {n: i + 1 for i, n in enumerate(["out0", "dense", "out1", "moe", "final", "ff0c", "ff0x", "mixer", "ff1"])}
        SQ = {n: i + 1 for i, n in enumerate(["attn0", "mix0", "ffn0", "attn1", "mix1", "ff0c", "ffn1", "final", "ff0x", "ff0c_out", "mixc",
                                              "ff0x_out", "mixx", "wo_out", "ff1", "ff1_out"])}
        COL_OF = {m: j for j, m in enumerate((0, 1, 3, 4, 6, 7))}
        GATE_OF = {2: ((0, 0), (1, 1)), 5: ((2, 0),), 8: ((3, 0),)}
        UNITS = [1 if n // 2 in COL_OF else len(GATE_OF[n // 2]) for n in range(NADA)]

        def units_before(n):
            return sum(UNITS[:n])
        VROWS = (120, 96, 72)

        def pairs(eng, nb, first=0, straight=False):
            lo, hi = first // 2, nb // 2
            if straight:
                for n in range(2 * lo, 2 * hi):
                    yield n, n // 2, n % 2
            elif hi - lo > 1:
                with eng.Fori(lo, hi) as i:
                    for u in range(2):
                        yield i * 2 + u, i, u
            elif hi - lo == 1:
                for u in range(2):
                    yield 2 * lo + u, lo, u
            if nb % 2:
                yield nb - 1, nb // 2, 0

        def blocks(eng, nb, body):
            m = (nb - 1) // 2
            body(0, 0, False)
            body(0, 1, False)
            with eng.Fori(1, m) as i:
                body(i, 0, False)
                body(i, 1, False)
            for n in range(2 * m, nb):
                body(m, n % 2, n == nb - 1)

        def ffn_count(p, T, e, i, u, tt, back=0):
            return e * (2 * p["nb"]) + i * 4 + (2 * u + (tt + 1) * (2 // T) - 2 * back + p["s"])

        def thru(p, T, e, i, u, tt, back=0):
            return ffn_count(p, T, e, i, u, tt, back) + (p["td"] - p["s"])

        def started(v):
            return not isinstance(v, int) or v > 0

        def emptied(p, i, u, tt):
            T = p["tiles"]
            if p["by"] == "both":
                return (pj_act, i * T + (T // 2 * u + tt // 2 + 1 + p["ja"])) if tt % 2 == 0 else (pj_dve, i * T + (T // 2 * u + tt // 2 + 1 + p["jd"]))
            if p["by"] == "act":
                return pj_act, i * (2 * T) + (T * u + tt + 1 + p["ja"])
            return pj_dve, i * (2 * T) + (T * u + tt + 1 + p["jd"])

        class Chain:

            def __init__(self, eng, sm):
                self.eng, self.sm, self.n = eng, sm, 0

            def done(self, ins):
                ins.then_inc(self.sm, 1)
                self.n += 1
                self.eng.wait_ge(self.sm, self.n)

        block = ctx.enter_context(nc.Block())

        @block.sync
        def _(sp):
            w2d = lambda ap: ap.rearrange("(k p) n -> p k n", p=P)

            def half_free(a, h):
                if a - 2 in SPLIT:
                    sp.wait_ge(A_split, 2 * SPLIT[a - 2] + h + 1)
                elif h == 0:
                    sp.wait_ge(A_lo_free, a - 1)
                else:
                    sp.wait_ge(tile_done, TILES_THROUGH[a - 2])

            def load_A(a, n, w, width=BW, first=0):
                v = w2d(w)
                for h in range(2):
                    if a >= 2:
                        half_free(a, h)
                    sl = slice(4 * h, 4 * h + 4)
                    sp.dma_start(ringA[:, a % 2, sl, 0:width], v[:, sl, bass.ds(n * BW + first, width)]).then_inc(A_full[a % 2][h], 16)

            def load_proj(p, w, first=0):
                for n in range(p["nb"]):
                    load_A(p["a"] + n, n, w, first=first)

            def load_ffn(p, wg, wu, wd, e=0):
                nb = p["nb"]
                vd = wd.rearrange("(k p) n -> p k n", p=P)

                def A(n, i, u):
                    a0 = p["a"] + u
                    for h in range(2):
                        if isinstance(i, int) and i == 0 and a0 - 2 not in SPLIT:
                            half_free(a0, h)
                            if not isinstance(e, int):
                                sp.wait_ge(A_split, e * (2 * nb) + (2 * (p["q"] + u) - 3 + h))
                        else:
                            sp.wait_ge(A_split, e * (2 * nb) + i * 4 + (2 * (p["q"] + u) - 3 + h))
                        sl = slice(4 * h, 4 * h + 4)
                        sp.dma_start(ringA[:, a0 % 2, sl, 0:FB], w2d(wg)[:, sl, bass.ds(n * FB, FB)]).then_inc(A_full[a0 % 2][h], 16)
                        sp.dma_start(ringA[:, a0 % 2, sl, FB:BW], w2d(wu)[:, sl, bass.ds(n * FB, FB)]).then_inc(A_full[a0 % 2][h], 16)

                def B(n, i, u):
                    b0 = p["b"] + u
                    for sm in (B_low0, B_low1):
                        v = e * nb + i * 2 + (b0 - 1)
                        if started(v):
                            sp.wait_ge(sm, v)
                    sp.dma_start(ringB[:, b0 % 2, :, :], vd[:, bass.ds(n * 2, 2), :]).then_inc(B_full[b0 % 2], 16)

                A(0, 0, 0)
                A(1, 0, 1)
                B(0, 0, 0)
                A(2, 1, 0)
                B(1, 0, 1)
                A(3, 1, 1)
                B(2, 1, 0)
                with sp.Fori(2, nb // 2) as i:
                    A(i * 2, i, 0)
                    B(i * 2 - 1, i - 1, 1)
                    A(i * 2 + 1, i, 1)
                    B(i * 2, i, 0)
                m = nb // 2
                if nb % 2:
                    A(nb - 1, m, 0)
                    B(nb - 2, m - 1, 1)
                    B(nb - 1, m, 0)
                else:
                    B(nb - 1, m - 1, 1)

            rows = [("attn_norm", 16), ("ffn_norm", 16), ("mix_norm_a", 8), ("mix_norm_b", 8), ("norm_g_2", 48),
                    ("c_2", 8), ("c_ctx_2", 8), ("hy_bias_2", 8)]
            at = 0
            for n, r in rows:
                sp.dma_start(vst[at:at + r, 0, :], t[n].rearrange("(r q) -> r q", q=P)).then_inc(vecs_in, 16)
                at += r
            sp.dma_start(vst[0:72, 1, :], t["hy_conv_w_2"].rearrange("(r q) -> r q", q=P)).then_inc(vecs_in, 16)
            sp.dma_start(vst[72:96, 1, :], t["hy_conv_b_2"].rearrange("(r q) -> r q", q=P)).then_inc(vecs_in, 16)
            sp.dma_start(vst[0:72, 2, :], t["b_ada_2"].rearrange("(r q) -> r q", q=P)).then_inc(vecs_in, 16)
            sp.dma_start(c1[:, :], t["const1"]).then_inc(consts_in, 16)
            sp.dma_start(x[:, :, :], t["x"].rearrange("(t p) n -> p t n", p=P)).then_inc(x_in, 16)
            sp.dma_start(posi[:, :], t["positions"].rearrange("(t p) -> p t", p=P), allow_slow_non_contiguous=True).then_inc(x_in, 16)
            for l in range(2):
                wi = t["w_in"][l * D:(l + 1) * D, :]
                p = ph[f"in{l}"]
                for n in range(5):
                    load_A(p["a"] + n, n, wi, FB if n == 4 else BW)
                    if l == 0 and n == 1:
                        sp.dma_start(fnrow[:, :], t["final_norm"].partition_broadcast(P)).then_inc(rows_in, 16)
                        sp.dma_start(sinkr[:, :, :].rearrange("p a b -> p (a b)"), t["sinks"].partition_broadcast(P)).then_inc(rows_in, 16)
                        sp.dma_start(rout[:, :, :], w2d(t["router"])).then_inc(rows_in, 16)
                        sp.dma_start(cs[:, :, :], t["ctx_2"].rearrange("(t p) n -> p t n", p=P)).then_inc(ctx_in, 16)
                for n in range(NADA // 2):
                    load_A(ph[f"ada{l}"]["a"] + n, NADA // 2 * l + n, t["w_ada_2"])
                load_proj(ph[f"out{l}"], t["w_out"][l * D:(l + 1) * D, :])
                if l == 0:
                    load_ffn(ph["dense"], t["dense_w_gate"], t["dense_w_up"], t["dense_w_down"])
            with sp.Fori(0, NE) as e:
                one = lambda w: w[bass.ds(e, 1), :, :].rearrange("o k n -> (o k) n")
                load_ffn(ph["moe"], one(t["moe_w_gate"]), one(t["moe_w_up"]), one(t["moe_w_down"]), e)
            g0 = t["w_ff_in_2"][0:D, 0:FF2], t["w_ff_in_2"][0:D, FF2:2 * FF2], t["w_ff_out_2"][0:FF2, :]
            load_ffn(ph["ff0c"], *g0)
            load_ffn(ph["ff0x"], *g0)
            sp.wait_ge(x_ready, XR["ff0x"])
            sp.dma_start(c2[:, :], t["const2"]).then_inc(c2_in, 16)
            sp.dma_start(flt[0:33, 0:64], t["filt_w1_2"]).then_inc(filt_in, 16)
            sp.dma_start(flt[0:64, 64:128], t["filt_w2_2"]).then_inc(filt_in, 16)
            sp.dma_start(flt[0:64, 128:192], t["filt_w3_2"]).then_inc(filt_in, 16)
            for n, nm in enumerate(("filt_b1_2", "filt_b2_2", "filt_b3_2", "filt_freq_2")):
                sp.dma_start(flt[0:64, 192 + n:193 + n], t[nm].rearrange("(p o) -> p o", o=1), allow_slow_non_contiguous=True).then_inc(filt_in, 16)
            sp.wait_ge(nt_tp, 8 * (call["mixx"] + 1))
            sp.dma_start(xn[0:64, :, :].rearrange("p a b -> p (a b)"), t["filt_w4_2"]).then_inc(w4_in, 16)
            load_proj(ph["z"], t["w_in_2"])
            load_proj(ph["hyo"], t["w_hy_out_2"])
            sp.wait_ge(i_used, KC)
            for n, nm in enumerate(("lambda_q1_2", "lambda_k1_2", "lambda_q2_2", "lambda_k2_2")):
                sp.dma_start(small[:, 64 * n:64 * n + 64], t[nm].partition_broadcast(P)).then_inc(rope2_in, 16)
            sp.dma_start(small[:, 256:384], t["subln_g_2"].partition_broadcast(P)).then_inc(rope2_in, 16)
            o = AT2["cos2"][0]
            sp.dma_start(arena[:, 6144:6400], t["const2"][:, o:o + 256]).then_inc(rope2_in, 16)
            load_proj(ph["q2"], t["w_in_2"], 3 * D)
            load_proj(ph["kv2"], t["w_in_2"], 4 * D)
            load_proj(ph["gt2"], t["w_in_2"], 6 * D)
            load_proj(ph["dao"], t["w_da_out_2"])
            load_proj(ph["wo"], t["w_o_2"])
            load_ffn(ph["ff1"], t["w_ff_in_2"][D:2 * D, 0:FF2], t["w_ff_in_2"][D:2 * D, FF2:2 * FF2], t["w_ff_out_2"][FF2:2 * FF2, :])
            sp.wait_ge(x_ready, XR["ff1"])
            sp.dma_start(out.rearrange("(t p) n -> p t n", p=P), x[:, :, :]).then_inc(out_done, 16)
            sp.wait_ge(out_done, 16)

        @block.tensor
        def _(pe):
            mm = nc.tensor.matmul
            tr = nc.tensor.transpose

            def norm(c):
                for k in range(KC):
                    if k == 0:
                        pe.wait_ge(nrm_xn, c + 1)
                    if k >= 2:
                        ev = nt_act if k % 2 == 0 else nt_dve
                        pe.wait_ge(ev, 4 * c + k // 2)
                    for tt in range(TILES):
                        last = tr(ps[:, 2 + k % 2, tt * P:(tt + 1) * P], xn[:, tt, k * P:(k + 1) * P], ident)
                    last.then_inc(nt_tp, 1)

            def norm_ready(c):
                pe.wait_ge(nt_act, 4 * (c + 1))
                pe.wait_ge(nt_dve, 4 * (c + 1))

            def project(p, lhs, bank=lambda u, tt: 4 + 2 * u + tt, last_cols=BW, between=None):
                nb, T = p["nb"], p["tiles"]
                if p["ja"]:
                    pe.wait_ge(pj_act, p["ja"])
                    pe.wait_ge(pj_dve, p["jd"])
                for n, i, u in pairs(pe, nb, straight=not p["ja"]):
                    a0 = p["a"] + u
                    cols = last_cols if nb % 2 and isinstance(n, int) and n == nb - 1 else BW
                    for tt in range(T):
                        if not (isinstance(n, int) and n < 2):
                            pe.wait_ge(*emptied(p, i - 1, u, tt))
                        for k in range(KC):
                            if tt == 0 and k % 4 == 0:
                                pe.wait_ge(A_full[a0 % 2][k // 4], i * 16 + A_LANDED[a0])
                            m = mm(ps[:, bank(u, tt), 0:cols], lhs(tt, k), ringA[:, a0 % 2, k, 0:cols], start=k == 0, stop=k == KC - 1)
                            if tt == T - 1 and k == 3:
                                m.then_inc(A_lo_free, 1)
                        m.then_inc(tile_done, 1)
                    if between and n == 0:
                        between()

            def feed(p, lhs, T, e=0, ready=None, xsm=None, after=None, before_last=None):
                nb = p["nb"]

                def gu(i, u, h):
                    a_ = e * (2 * nb) + i * 4 + (2 * (p["q"] + u) + h + 1)
                    for tt in range(T):
                        bank = tt if T == 2 else u
                        if h == 0:
                            v = ffn_count(p, T, e, i, u, tt, 3 - T)
                            if started(v):
                                pe.wait_ge(h_ready, v)
                        if tt == 0:
                            pe.wait_ge(A_split, a_)
                            if isinstance(i, int) and i == 0 and u == 0:
                                pe.wait_ge(xsm, ready + h)
                        for k in range(4 * h, 4 * h + 4):
                            for n, (l, r) in enumerate(((0, 0), (0, 1), (1, 0))):
                                m = mm(ps[:, bank, :], lhs(l, tt, k), As[:, h, r, k % 4, :], start=k == 0 and n == 0, stop=k == KC - 1 and n == 2)
                        if h == 1:
                            m.then_inc(tile_done, 2 // T)
                    if h == 0:
                        m.then_inc(A_lo_free, 1)

                def turn(i, u):
                    for tt in range(T):
                        pe.wait_ge(h_ready, ffn_count(p, T, e, i, u, tt))
                        v = ffn_count(p, T, e, i, u, tt, 1)
                        if started(v):
                            pe.wait_ge(hdT_ready, v)
                        for q in range(2):
                            m = tr(ps[:, 2 + tt, q * P:(q + 1) * P], hh[:, tt if T == 2 else u, q * P:(q + 1) * P], ident)
                        m.then_inc(tp_done, 2 // T)

                def down(i, u):
                    first = isinstance(i, int) and i == 0 and u == 0
                    for tt in range(T):
                        buf = tt if T == 2 else u
                        if first and tt == 0 and (p["f"] or not isinstance(e, int)):
                            pe.wait_ge(acc_free, e + p["f"])
                        pe.wait_ge(hdT_ready, ffn_count(p, T, e, i, u, tt))
                        if tt == 0:
                            for sm in (B_low0, B_low1):
                                pe.wait_ge(sm, e * nb + i * 2 + (p["b"] + u + 1))
                        for q in range(2):
                            for n, (l, r) in enumerate(((0, 0), (0, 1), (1, 0))):
                                for half in range(2):
                                    m = mm(ps[:, 4 + 2 * tt + half, :], hds[:, buf, l, q, :], Bs[:, q, r, half * 512:(half + 1) * 512],
                                           start=first and q == 0 and n == 0, stop=q == 1 and n == 2, skip_group_check=True)
                        m.then_inc(down_done, 2 // T)

                def body(i, u, last):
                    lead = isinstance(i, int) and i == 0 and u == 0
                    prev = (i, 0) if u else (i - 1, 1)
                    gu(i, u, 0)
                    if not lead:
                        turn(*prev)
                    gu(i, u, 1)
                    if not lead:
                        down(*prev)
                    if after and isinstance(i, int) and i == 0:
                        after(u)
                    if last:
                        if before_last:
                            before_last()
                        turn(i, u)
                        down(i, u)
                blocks(pe, nb, body)

            moe = ph["moe"]

            def gather(e):
                pe.wait_ge(sel_ready, e + 1)
                if not isinstance(e, int) or e >= 2:
                    pe.wait_ge(added, 2 * e - 2)
                for half in range(2):
                    for k in range(4):
                        for tt in range(TILES):
                            o = (4 * half + k) * P
                            last = mm(ps[:, 6 + half, k * P:(k + 1) * P], xn[:, tt, o:o + P], sel[:, tt, :], start=tt == 0, stop=tt == TILES - 1)
                    last.then_inc(gathered, 1)

            def scatter(e, tt):
                if tt == 0:
                    pe.wait_ge(selgT_ready, e + 1)
                    pe.wait_ge(acc_free, e + (moe["f"] + 1))
                    if not isinstance(e, int) or e < NE - 1:
                        pe.wait_ge(xg_ready, 2 * e + 4)
                if tt or isinstance(e, int) and e == NE - 1:
                    pe.wait_ge(added, 2 * e + tt)
                for half in range(2):
                    last = mm(ps[:, 6 + half, :], selgT[:, tt, :], ye[:, half * 512:(half + 1) * 512], start=True, stop=True)
                last.then_inc(mixed_back, 1)

            def expert(e):
                first, final = isinstance(e, int) and e == 0, isinstance(e, int) and e == NE - 1

                def next_rows():
                    if not final:
                        gather(e + 1)
                    pe.wait_ge(selg_ready, e + 1)
                    for tt in range(TILES):
                        last = tr(ps[:, 3, tt * P:(tt + 1) * P], selg[:, tt, :], ident)
                    last.then_inc(selg_tp, 1)
                feed(moe, lambda l, tt, k: xgs[:, l, k, :], 1, e, 2 * e + 1, xg_split,
                     after=None if first else lambda u: scatter(e - 1, u), before_last=next_rows)

            def spread_row(n):
                m, half = n // 2, n % 2
                pe.wait_ge(row_copied, n + 1)
                if m in COL_OF:
                    if n:
                        pe.wait_ge(spread_copied, units_before(n))
                    for k in range(4):
                        last = tr(ps[:, 1, 2 * k:2 * k + 2], arow[0:2, n % 2, k * P:(k + 1) * P], ident[0:2, 0:2])
                    last.then_inc(spread, 1)
                else:
                    for q, (g, who) in enumerate(GATE_OF[m]):
                        pe.wait_ge(spread_copied, units_before(n) + q)
                        mm(ps[:, 1, :], k1("pick")[0:2, who * P:(who + 1) * P], arow[0:2, n % 2, :], start=True, stop=True).then_inc(spread, 1)

            def modulation(l, j):
                n = NADA // 2 * l + j
                if n:
                    spread_row(n - 1)
                    pe.wait_ge(spread_copied, units_before(n))
                else:
                    pe.wait_ge(c_silu, 1)
                a0 = ph[f"ada{l}"]["a"] + j
                for k in range(KC):
                    if k % 4 == 0:
                        pe.wait_ge(A_full[a0 % 2][k // 4], A_LANDED[a0])
                    m = mm(ps[0:2, 1, :], cT[:, k, :], ringA[:, a0 % 2, k, :], start=k == 0, stop=k == KC - 1)
                    if k == 3:
                        m.then_inc(A_lo_free, 1)
                m.then_inc(tile_done, 1)

            def heads(l):
                def head(h):
                    if h < 8:
                        return h // 2, 4 + h // 2, HD * (h % 2), 1024 + HD * h
                    hb = h - 8
                    return 8 + hb // 2, 12 + hb // 4, HD * (hb % 2), 2176 + HD * (hb // 4)
                modulation(l, 0)
                pe.wait_ge(rope_ready, 2 * l + 1)
                for c in range(14):
                    if c >= 2:
                        pe.wait_ge(qt_act if c % 2 == 0 else qt_dve, 7 * l + c // 2)
                    for tt in range(TILES):
                        if c == 8:
                            pe.wait_ge(rope_ready, 2 * l + 2)
                        last = tr(ps[:, 2 + c % 2, tt * P:(tt + 1) * P], qr[:, tt, c * P:(c + 1) * P], ident)
                    last.then_inc(qt_tp, 1)
                pe.wait_ge(qt_act, 7 * (l + 1))
                pe.wait_ge(qt_dve, 7 * (l + 1))

                def scores(g):
                    gi = 4 * l + g
                    if gi:
                        pe.wait_ge(nm_ready, gi)
                    for j in range(4):
                        cq, ck, o, _ = head(4 * g + j)
                        mm(ps[:, 4 + j, 0:P], qkT[o:o + HD, cq, 0:P], qkT[o:o + HD, ck, 0:P], start=True, stop=True)
                        last = mm(ps[:, 4 + j, P:384], qkT[o:o + HD, cq, P:SEQ], qkT[o:o + HD, ck, :], start=True, stop=True)
                    last.then_inc(sc_done, 1)

                def turn_weights(g):
                    gi = 4 * l + g
                    pe.wait_ge(p_ready, gi + 1)
                    for j in range(4):
                        if 4 * gi + j >= 2:
                            pe.wait_ge(pt_act if j % 2 == 0 else pt_dve, 2 * gi + j // 2)
                        for q in range(3):
                            last = tr(ps[:, 2 + j % 2, q * P:(q + 1) * P], S[:, j, q * P:(q + 1) * P], ident)
                        last.then_inc(pt_done, 1)

                def values(g):
                    gi = 4 * l + g
                    if gi:
                        pe.wait_ge(o_done, gi)
                    for j in range(4):
                        v = head(4 * g + j)[3]
                        pe.wait_ge(pt_act if j % 2 == 0 else pt_dve, 2 * gi + j // 2 + 1)
                        mm(ps[:, 0, j * P:j * P + HD], PT[:, j, 0:P], qkv[:, 0, v:v + HD], start=True, stop=True)
                        mm(ps[:, 0, j * P + HD:j * P + P], PT[:, j, P:2 * P], qkv[:, 0, v:v + HD], start=True, stop=False)
                        last = mm(ps[:, 0, j * P + HD:j * P + P], PT[:, j, 2 * P:3 * P], qkv[:, 1, v:v + HD], start=False, stop=True)
                    last.then_inc(pv_done, 1)
                scores(0)
                modulation(l, 1)
                for g in range(4):
                    turn_weights(g)
                    if g < 3:
                        scores(g + 1)
                        modulation(l, 2 * g + 2)
                    values(g)
                    if g < 3:
                        modulation(l, 2 * g + 3)
                modulation(l, 8)

            stream = lambda tt, k: hT[:, k, tt * P:(tt + 1) * P]
            split_stream = lambda l, tt, k: xs[:, l, k, tt * P:(tt + 1) * P]
            both = lambda tt, k: (hT if tt < 2 else hcT)[:, k, (tt % 2) * P:(tt % 2 + 1) * P]

            pe.wait_ge(vecs_in, 16 * 11)
            pe.wait_ge(consts_in, 16)
            for g in range(3):
                r = VROWS[g]
                last = tr(ps[:, 2, g * P:g * P + r], vst[0:r, g, :], ident[0:r, 0:r])
            last.then_inc(vt_done, 1)
            for l in range(2):
                norm(call[f"attn{l}"])
                norm_ready(call[f"attn{l}"])
                project(ph[f"in{l}"], stream, last_cols=FB)
                heads(l)
                norm(call[f"mix{l}"])
                if l == 1:
                    spread_row(NADA - 1)
                norm_ready(call[f"mix{l}"])
                project(ph[f"out{l}"], stream, between=(lambda: norm(call["ff0c"])) if l == 1 else None)
                norm(call[f"ffn{l}"])
                if l == 1:
                    norm_ready(call[f"ffn{l}"])
                if l == 0:
                    feed(ph["dense"], split_stream, 2, ready=1, xsm=xs_split)
            pe.wait_ge(rows_in, 16 * 3)
            for tt in range(TILES):
                for k in range(KC):
                    last = mm(ps[:, 0, tt * NE:(tt + 1) * NE], stream(tt, k), rout[:, k, :], start=k == 0, stop=k == KC - 1)
            last.then_inc(rt_done, 1)
            pe.wait_ge(rt_ready, 1)
            before, c0 = k1("before"), 2 * NE
            mm(ps[:, 0, c0:c0 + NE], before, chosen[:, 0, :], start=True, stop=True)
            mm(ps[:, 0, c0 + NE:c0 + 2 * NE], before, chosen[:, 1, :], start=True, stop=False)
            mm(ps[:, 0, c0 + NE:c0 + 2 * NE], ones, chosen[:, 0, :], start=False, stop=True)
            for tt in range(TILES):
                last = mm(ps[:, 0, c0 + 2 * NE:c0 + 3 * NE], ones, chosen[:, tt, :], start=tt == 0, stop=tt == TILES - 1)
            last.then_inc(slot_mm, 1)
            pe.wait_ge(most_ready, 2)
            with pe.If(pe.value_load(most[0:1, 0:1], min_val=0, max_val=SEQ) < CAP + 1):
                gather(0)
                expert(0)
                with pe.Fori(1, NE - 1) as e:
                    expert(e)
                expert(NE - 1)
                for tt in range(TILES):
                    scatter(NE - 1, tt)
            with pe.Else():
                with pe.Fori(0, NE - 1) as e:
                    feed(moe, split_stream, 2, e, 1, xr_split)
                feed(moe, split_stream, 2, NE - 1, 1, xr_split)
            feed(ph["ff0c"], split_stream, 2, ready=2 * ph["ff0c"]["xc"] + 1, xsm=xs_split)
            norm(call["ff0x"])
            feed(ph["ff0x"], split_stream, 2, ready=2 * ph["ff0x"]["xc"] + 1, xsm=xs_split)
            for nm in ("mixc", "mixx"):
                norm(call[nm])
            pe.wait_ge(c2_in, 16)
            pe.wait_ge(filt_in, 16 * 7)
            pe.wait_ge(w4_in, 16)
            pe.wait_ge(acc_free, ph["ff1"]["f"])
            for j in range(3):
                if j:
                    pe.wait_ge(f_sin, j)
                rhs = k2("zT")[0:33, :] if j == 0 else flt[0:64, 256:512]
                kk = 33 if j == 0 else 64
                mm(ps[0:64, 0, 0:SEQ], flt[0:kk, 64 * j:64 * j + 64], rhs, start=True, stop=True).then_inc(f_mm, 1)
            pe.wait_ge(f_sin, 3)
            for tt in range(TILES):
                if tt:
                    pe.wait_ge(f_h, tt)
                for q in range(4):
                    last = mm(ps[:, 4 + q, :], flt[0:64, 256 + tt * P:256 + (tt + 1) * P],
                              xn[0:64, q // 2, (q % 2) * 512:(q % 2 + 1) * 512], start=True, stop=True)
                last.then_inc(f_mm, 1)
            pe.wait_ge(f_h, 2)
            for c in range(KC):
                for tt in range(TILES):
                    last = mm(ps[:, 0, c:c + 1], ha[:, tt, c * P:(c + 1) * P], ones[:, 0:1], start=tt == 0, stop=tt == TILES - 1)
            last.then_inc(rn_mm, 1)
            dft = k2("dft").rearrange("p (t f) -> p t f", t=TILES)
            colof = [0, P, 4 * P, 3 * P, 5 * P]
            for q in range(10):
                fc, half = q // 2, q % 2
                src = hd if fc in (2, 3) else hs
                if q >= 4:
                    pe.wait_ge(k_copied, q - 3)
                for tt in range(TILES):
                    last = mm(ps[:, 4 + q % 4, :], dft[:, tt, colof[fc]:colof[fc] + P], src[:, tt, half * 512:(half + 1) * 512],
                              start=tt == 0, stop=tt == TILES - 1)
                last.then_inc(k_mm, 1)
            norm_ready(call["mixx"])
            pe.wait_ge(k_copied, 10)
            p = ph["z"]
            for n, i, u in pairs(pe, 6, straight=True):
                a0 = p["a"] + u
                for j in range(4):
                    if not (isinstance(n, int) and n == 0):
                        pe.wait_ge(z_used, i * 8 + (4 * u + j - 3))
                    for k in range(KC):
                        if j == 0 and k % 4 == 0:
                            pe.wait_ge(A_full[a0 % 2][k // 4], i * 16 + A_LANDED[a0])
                        m = mm(ps[:, 4 + j, 0:SEQ], ringA[:, a0 % 2, k, j * P:(j + 1) * P], hT[:, k, :], start=k == 0, stop=k == KC - 1)
                        if j == 3 and k == 3:
                            m.then_inc(A_lo_free, 1)
                    m.then_inc(tile_done, 1)
            pe.wait_ge(z_used, 24)
            for tt in range(TILES):
                for half in range(2):
                    q = 2 * tt + half
                    if q >= 2:
                        pe.wait_ge(ut_copied, q - 1)
                    for c in range(4):
                        last = tr(ps[:, 2 + q % 2, c * P:(c + 1) * P], uT[:, 4 * half + c, tt * P:(tt + 1) * P], ident)
                    last.then_inc(ut_tp, 1)
            pe.wait_ge(ut_copied, 4)
            for half in range(2):
                if half:
                    pe.wait_ge(y_ready, 1)
                for fc in range(4):
                    for tt in range(TILES):
                        last = mm(ps[:, 4 + fc, :], dft[:, tt, fc * P:(fc + 1) * P], utok[:, tt, half * 512:(half + 1) * 512],
                                  start=tt == 0, stop=tt == TILES - 1)
                last.then_inc(u_mm, 1)
            idft = k2("idft").rearrange("p (f t) -> p f t", f=4)
            for c in range(KC):
                if c % 4 == 0:
                    pe.wait_ge(y_ready, c // 4 + 1)
                if c >= 2:
                    pe.wait_ge(i_used, c - 1)
                for fc in range(4):
                    last = mm(ps[:, c % 2, 0:SEQ], Y[:, fc, c * P:(c + 1) * P], idft[:, fc, :], start=fc == 0, stop=fc == 3)
                last.then_inc(i_mm, 1)
            pe.wait_ge(i_used, KC)
            project(ph["hyo"], lambda tt, k: uT[:, k, tt * P:(tt + 1) * P])
            project(ph["q2"], stream)
            project(ph["kv2"], both, bank=lambda u, tt: 4 * (1 - u) + tt)
            pe.wait_ge(pj_act, ph["gt2"]["ja"])
            pe.wait_ge(pj_dve, ph["gt2"]["jd"])
            for c in range(KC):
                for who in range(3):
                    q = 3 * c + who
                    pe.wait_ge(rope_ready, 5 + (0 if who == 0 else 1))
                    if q >= 2:
                        pe.wait_ge(qt_act if q % 2 == 0 else qt_dve, 14 + q // 2)
                    for tt in range(TILES):
                        src = qraw[:, tt, c * P:(c + 1) * P] if who == 0 else kraw[:, 2 * (who - 1) + tt, c * P:(c + 1) * P]
                        last = tr(ps[:, 2 + q % 2, tt * P:(tt + 1) * P], src, ident)
                    last.then_inc(qt_tp, 1)
            pe.wait_ge(qt_act, 14 + 12)
            pe.wait_ge(qt_dve, 14 + 12)

            def scores(n):
                h, tt = n // 2, n % 2
                if n >= 2:
                    pe.wait_ge(s2_exp, n - 1)
                for m in range(2):
                    last = mm(ps[:, 4 + 2 * (n % 2) + m, :], qT2[HD * m:HD * m + HD, h, tt * P:(tt + 1) * P], kT2[HD * m:HD * m + HD, h, :], start=True, stop=True)
                last.then_inc(s2_mm, 1)
            def gates_part(n):
                p, tile, half = ph["gt2"], n // 2, n % 2
                a0, tt, bank = p["a"] + tile // 2, tile % 2, 1 + 2 * (tile % 2)
                if half == 0 and tile >= 2:
                    pe.wait_ge(pj_act, p["ja"] + tile - 1)
                for k in range(4 * half, 4 * half + 4):
                    if tt == 0 and k % 4 == 0:
                        pe.wait_ge(A_full[a0 % 2][half], A_LANDED[a0])
                    m = mm(ps[:, bank, :], stream(tt, k), ringA[:, a0 % 2, k, :], start=k == 0, stop=k == KC - 1)
                if half:
                    m.then_inc(tile_done, 1)
                elif tt == TILES - 1:
                    m.then_inc(A_lo_free, 1)
            NU = 16
            scores(0)
            for n in range(NU):
                if n + 1 < NU:
                    scores(n + 1)
                h = n // 2
                pe.wait_ge(s2_p, n + 1)
                if n:
                    pe.wait_ge(s2_pt, n)
                for q in range(4):
                    last = tr(ps[:, 2, q * P:(q + 1) * P], E2[:, n % 2, 0, q * P:(q + 1) * P], ident)
                last.then_inc(s2_tp, 1)
                gates_part(n)
                pe.wait_ge(s2_pt, n + 1)
                if n:
                    pe.wait_ge(s2_o, n)
                for q in range(4):
                    last = mm(ps[:, 0, 0:P], PT2[:, n % 2, q * P:(q + 1) * P], V2[:, q, h * P:(h + 1) * P], start=q == 0, stop=q == 3)
                last.then_inc(s2_pv, 1)
            for c in range(KC):
                if c == 0:
                    pe.wait_ge(sl_std, 2)
                q = 24 + c
                pe.wait_ge(qt_act if q % 2 == 0 else qt_dve, 14 + q // 2)
                for tt in range(TILES):
                    last = tr(ps[:, 2 + q % 2, tt * P:(tt + 1) * P], O2[:, tt, c * P:(c + 1) * P], ident)
                last.then_inc(qt_tp, 1)
            pe.wait_ge(qt_act, 30)
            pe.wait_ge(qt_dve, 30)
            project(ph["dao"], lambda tt, k: hcT[:, k, tt * P:(tt + 1) * P])
            for c in range(KC):
                if c % 4 == 0:
                    pe.wait_ge(y_mixed, c // 2 + 2)
                q = 32 + c
                pe.wait_ge(qt_act if q % 2 == 0 else qt_dve, 14 + q // 2)
                for tt in range(TILES):
                    last = tr(ps[:, 2 + q % 2, tt * P:(tt + 1) * P], YH[:, tt, c * P:(c + 1) * P], ident)
                last.then_inc(qt_tp, 1)
            pe.wait_ge(qt_act, 34)
            pe.wait_ge(qt_dve, 34)
            project(ph["wo"], lambda tt, k: hcT[:, k, tt * P:(tt + 1) * P])
            norm(call["ff1"])
            feed(ph["ff1"], split_stream, 2, ready=2 * ph["ff1"]["xc"] + 1, xsm=xs_split)

        @block.gpsimd
        def _(pool):
            G = nc.gpsimd
            ch = Chain(pool, pool_step)

            def low(b):
                u, n = b
                pool.wait_ge(B_high, n + 1)
                G.tensor_tensor(Bs[:, 0, 1, :], ringB[:, u, 0, :], f32(Bs[:, 0, 0, :]), ALU.subtract).then_inc(B_low0, 1)

            with pool.Fori(0, NB1 // 2) as i:
                for u in range(2):
                    low((u, i * 4 + 2 * u))
            pool.wait_ge(vt_copied, 1)
            pool.wait_ge(spread_copied, units_before(NADA))
            for m, j in COL_OF.items():
                last = G.tensor_tensor(modT[:, j, :, :], modT[:, j, :, :], vcol[:, 2, 8 * m:8 * m + 8].unsqueeze(2).broadcast_to([P, KC, 2]), ALU.add)
            ch.done(last)
            for j in range(3):
                for who in range(2):
                    ch.done(G.tensor_scalar(adaS[:, j, who, :], modT[:, 2 * j + 1, :, who], 1.0, None, ALU.add))
                    last = G.tensor_tensor(adaS[:, j, who, :], adaS[:, j, who, :], vcol[:, 0, 48 + 16 * j:56 + 16 * j], ALU.mult)
                ch.done(last)
            pool.sem_inc(mods_ready, 1)
            for w, (gain, bias, rows_, fac) in enumerate(((1, 2, (0, 1), 0.5), (3, 5, (2,), 1.0), (5, 8, (3,), 0.5))):
                pool.dma_start(vec_row, t["b_ada_2"][bias * D:(bias + 1) * D].partition_broadcast(P)).then_inc(gain_in, 16)
                pool.wait_ge(gain_in, 32 * w + 16)
                for g in rows_:
                    ch.done(G.tensor_tensor(gateG[:, g, :], gateG[:, g, :], vec_row, ALU.add))
                pool.dma_start(vec_row, t["norm_g_2"][gain * D:(gain + 1) * D].partition_broadcast(P)).then_inc(gain_in, 16)
                for g in rows_:
                    ch.done(G.tensor_scalar(gateG[:, g, :], gateG[:, g, :], fac, None, ALU.mult))
                pool.wait_ge(gain_in, 32 * w + 32)
                for g in rows_:
                    ch.done(G.tensor_tensor(gateG[:, g, :], gateG[:, g, :], vec_row, ALU.mult))
                pool.sem_inc(mods_ready, 1)
            rest = (NB1 * NE + 3 * NB2) // 2
            with pool.Fori(NB1 // 2, NB1 // 2 + rest) as i:
                for u in range(2):
                    low((u, i * 4 + 2 * u))
            if (NB1 * NE + 3 * NB2) % 2:
                low((0, 4 * (NB1 // 2 + rest)))

        @block.scalar
        def _(act):
            A = nc.scalar.activation
            ch = Chain(act, act_step)

            def squares(src, nparts, eps, dst=None):
                n = D // nparts
                for tt in range(TILES):
                    for q in range(nparts):
                        j = tt * nparts + q
                        ch.done(A(xn[:, tt, q * n:(q + 1) * n] if dst is None else dst(tt, q), src(tt)[:, q * n:(q + 1) * n], ACT.Square, accum_out=ss[:, j:j + 1]))
                A(std[:, 0:2 * nparts], ss[:, 0:2 * nparts], ACT.Sqrt, bias=epsc[eps], scale=1.0 / n).then_inc(nrm_std, 1)

            epsc = {1e-5: small[:, 500:501], 1e-6: small[:, 501:502]}

            def norm(c, wait, src, scale, bias=None, dst=None, nparts=1, eps=1e-5, parts=False):
                for sm, v in wait:
                    act.wait_ge(sm, v)
                stats(c, [], src, nparts, eps)
                chunks(c, scale, bias, dst, parts)

            def stats(c, wait, src, nparts=1, eps=1e-5):
                for sm, v in wait:
                    act.wait_ge(sm, v)
                if c:
                    act.wait_ge(nt_tp, 8 * c)
                squares(src, nparts, eps)

            def chunks(c, scale, bias, dst, parts=False):
                for k in range(0, KC, 2):
                    act.wait_ge(nt_tp, 8 * c + k + 1)
                    kw = {} if bias is None else dict(bias=bias(k))
                    A(dst[:, k, :], ps[:, 2 + k % 2, 0:SEQ], ACT.Copy if bias is None else ACT.Identity, scale=scale(k), **kw).then_inc(nt_act, 1)
                    if parts and k % 4 == 2:
                        h = k // 4
                        act.wait_ge(nt_act, 4 * c + 2 * (h + 1))
                        act.wait_ge(nt_dve, 4 * c + 2 * (h + 1))
                        A(xs[:, 0, 4 * h:4 * h + 4, :], dst[:, 4 * h:4 * h + 4, :], ACT.Copy).then_inc(xs_high, 1)

            def copy_out(p, dst, func=ACT.Copy, last_cols=BW, bank=lambda u, tt: 4 + 2 * u + tt, straight=True):
                nb, T = p["nb"], p["tiles"]
                for n, i, u in pairs(act, nb, straight=straight):
                    cols = last_cols if nb % 2 and isinstance(n, int) and n == nb - 1 else BW
                    for tt in range(0, T, 2 if p["by"] == "both" else 1):
                        act.wait_ge(tile_done, i * (2 * T) + (u * T + tt + 1 + p["td"]))
                        A(dst(tt, n, cols), ps[:, bank(u, tt), 0:cols], func).then_inc(pj_act, 1)

            def A_parts(p, e, i, u, h):
                act.wait_ge(A_full[(p["a"] + u) % 2][h], e * (16 * p["nb"]) + i * 32 + A_LANDED[p["a"] + u])
                if h == 0:
                    act.wait_ge(A_lo_free, e * p["nb"] + i * 2 + (p["a"] + u))
                else:
                    act.wait_ge(tile_done, e * (2 * p["nb"]) + i * 4 + TILES_THROUGH[p["a"] + u - 1])
                A(As[:, h, 0, :, :], ringA[:, (p["a"] + u) % 2, 4 * h:4 * h + 4, :], ACT.Copy).then_inc(A_high, 1)

            def x_parts(src, c, high=xs_high):
                act.wait_ge(nt_act, 4 * (c + 1))
                act.wait_ge(nt_dve, 4 * (c + 1))
                for h in range(2):
                    A(xs[:, 0, 4 * h:4 * h + 4, :], src[:, 4 * h:4 * h + 4, :], ACT.Copy).then_inc(high, 1)

            def feed(p, T, e=0, ahead=False, after=None):
                nb = p["nb"]

                def hidden(i, u):
                    for tt in range(T):
                        act.wait_ge(tp_done, ffn_count(p, T, e, i, u, tt))
                        v = ffn_count(p, T, e, i, u, tt, 1)
                        if started(v):
                            act.wait_ge(down_done, v)
                        A(hds[:, tt if T == 2 else u, 0, :, :].rearrange("p a b -> p (a b)"), ps[:, 2 + tt, 0:FB], ACT.Copy).then_inc(hd_high, 2 // T)

                def body(i, u, last):
                    if not (isinstance(i, int) and i == 0 and u == 0):
                        hidden(*((i, 0) if u else (i - 1, 1)))
                    nxt = (i + 1, 0) if u else (i, 1)
                    if not last or ahead:
                        A_parts(p, e, *nxt, 0)
                    for tt in range(T):
                        act.wait_ge(tile_done, thru(p, T, e, i, u, tt))
                        v = ffn_count(p, T, e, i, u, tt, 3 - T)
                        if started(v):
                            act.wait_ge(h_ready, v)
                        A(sg[:, tt if T == 2 else u, :], ps[:, tt if T == 2 else u, 0:FB], ACT.Silu).then_inc(silu_done, 2 // T)
                    if not last or ahead:
                        A_parts(p, e, *nxt, 1)
                    b0 = p["b"] + u
                    for q in range(2):
                        if q == 0:
                            act.wait_ge(B_full[b0 % 2], e * (8 * nb) + i * 16 + 16 * (b0 // 2 + 1))
                            v = ffn_count(p, 2, e, i, u, 1, 1)
                            if started(v):
                                act.wait_ge(down_done, v)
                        A(Bs[:, q, 0, :], ringB[:, b0 % 2, q, :], ACT.Copy).then_inc(B_high, 1)
                    if last:
                        hidden(i, u)
                        if after:
                            after()
                blocks(act, nb, body)

            def spread_row(n):
                m, half = n // 2, n % 2
                for q in range(UNITS[n]):
                    act.wait_ge(spread, units_before(n) + q + 1)
                    if m in COL_OF:
                        A(modT[:, COL_OF[m], 4 * half:4 * half + 4, :], ps[:, 1, 0:8].rearrange("p (k w) -> p k w", w=2), ACT.Copy).then_inc(spread_copied, 1)
                    else:
                        A(gateG[:, GATE_OF[m][q][0], half * BW:(half + 1) * BW], ps[:, 1, :], ACT.Copy).then_inc(spread_copied, 1)

            def modulation(l, j):
                n = NADA // 2 * l + j
                if j == 0 and n:
                    spread_row(n - 1)
                act.wait_ge(tile_done, ph[f"ada{l}"]["td"] + j + 1)
                if n >= 2:
                    act.wait_ge(spread, units_before(n - 1))
                A(arow[0:2, n % 2, :], ps[0:2, 1, :], ACT.Copy).then_inc(row_copied, 1)

            def rows_parts(e):
                for h in range(2):
                    act.wait_ge(xg_ready, 2 * e + (h + 1))
                    A(xgs[:, 0, 4 * h:4 * h + 4, :], xgT[:, 4 * h:4 * h + 4, :], ACT.Copy).then_inc(xg_high, 1)

            def expert(e):
                final = isinstance(e, int) and e == NE - 1
                p = ph["moe"]

                def after():
                    if not final:
                        rows_parts(e + 1)
                    act.wait_ge(selg_tp, e + 1)
                    A(selgT[:, :, :].rearrange("p a b -> p (a b)"), ps[:, 3, 0:TILES * P], ACT.Copy).then_inc(selgT_ready, 1)
                    act.wait_ge(down_done, e * (2 * NB1) + (p["s"] + 2 * NB1))
                    A(ye[:, :], ps[:, 4:6, :].rearrange("p a b -> p (a b)"), ACT.Copy).then_inc(acc_free, 1)
                feed(p, 1, e, True, after)

            col = lambda r: (lambda k: vcol[:, 0, r + k:r + k + 1])
            act.wait_ge(vt_copied, 1)
            A(cT[:, :, :].rearrange("p k w -> p w k"), vcol[:, 0, 96:112].rearrange("p (w k) -> p w k", w=2), ACT.Silu).then_inc(c_silu, 1)
            act.wait_ge(ang_ready, 1)
            a4 = small[:, 0:128].rearrange("p (t f) -> p t f", t=TILES)
            for tt in range(TILES):
                A(sinT[:, tt, 32:64], a4[:, tt, 0:32], ACT.Sin)
                A(sinT[:, tt, 0:32], a4[:, tt, 0:32], ACT.Sin, scale=-1.0)
                A(cosT[:, tt, 0:32], a4[:, tt, 32:64], ACT.Sin)
                A(cosT[:, tt, 32:64], a4[:, tt, 32:64], ACT.Sin).then_inc(table_ready, 1)

            def mod_cols(j, who):
                return lambda k: adaS[:, j, who, k:k + 1], lambda k: modT[:, 2 * j, k, who:who + 1]

            for l in range(2):
                norm(call[f"attn{l}"], [(x_in, 32)] if l == 0 else [(x_ready, XR["dense"])], lambda tt: x[:, tt, :], col(8 * l), dst=hT)
                copy_out(ph[f"in{l}"], lambda tt, n, cols: qkv[:, tt, n * BW:n * BW + cols], last_cols=FB)
                modulation(l, 0)
                for c in range(0, 14, 2):
                    act.wait_ge(qt_tp, 14 * l + c + 1)
                    A(qkT[:, c, :], ps[:, 2 + c % 2, 0:SEQ], ACT.Copy).then_inc(qt_act, 1)

                def exponentials(g):
                    act.wait_ge(nm_ready, 4 * l + g + 1)
                    for j in range(4):
                        for tt in range(TILES):
                            cols = slice(0, P) if tt == 0 else slice(P, 384)
                            last = A(S[:, j, cols], S[:, j, cols], ACT.Exp, bias=small[:, 128 + 2 * j + tt:129 + 2 * j + tt])
                    if g >= 2:
                        last = A(small[:, 144:152], small[:, 136:144], ACT.Exp)
                    last.then_inc(e_ready, 1)
                spread_row(9 * l)
                exponentials(0)
                modulation(l, 1)
                for g in range(4):
                    for j in (0, 2):
                        act.wait_ge(pt_done, 4 * (4 * l + g) + j + 1)
                        A(PT[:, j, :], ps[:, 2, 0:384], ACT.Copy).then_inc(pt_act, 1)
                    if g < 3:
                        spread_row(9 * l + 2 * g + 1)
                        exponentials(g + 1)
                        modulation(l, 2 * g + 2)
                        spread_row(9 * l + 2 * g + 2)
                        modulation(l, 2 * g + 3)
                spread_row(9 * l + 7)
                modulation(l, 8)
                mixc = lambda k, l=l: vcol[:, 0, (32 + 4 * l + k if k < 4 else 40 + 4 * l + k - 4):][:, 0:1]
                norm(call[f"mix{l}"], [(o_done, 4 * (l + 1))], lambda tt: O[:, tt, :], mixc, dst=hT, nparts=2)
                if l == 1:
                    spread_row(NADA - 1)
                    stats(call["ff0c"], [(ctx_in, 16)], lambda tt: cs[:, tt, :], eps=1e-6)
                    act.wait_ge(mods_ready, 1)
                    chunks(call["ff0c"], *mod_cols(0, 1), hcT)
                p = ph["dense"] if l == 0 else ph["moe"]
                for h in range(2):
                    A_parts(p, 0, 0, 0, h)
                norm(call[f"ffn{l}"], [(x_ready, XR[f"out{l}"])], lambda tt: x[:, tt, :], col(16 + 8 * l), dst=hT, parts=l == 0)
                if l == 0:
                    feed(ph["dense"], 2)
            act.wait_ge(rt_exp, 1)
            A(small[:, 306:308], small[:, 304:306], ACT.Exp).then_inc(rt_exp, 1)
            act.wait_ge(most_ready, 2)
            with act.If(act.value_load(most[0:1, 0:1], min_val=0, max_val=SEQ) < CAP + 1):
                rows_parts(0)
                with act.Fori(0, NE - 1) as e:
                    expert(e)
                expert(NE - 1)
            with act.Else():
                x_parts(hT, call["ffn1"], xr_high)
                with act.Fori(0, NE - 1) as e:
                    feed(ph["moe"], 2, e, True)
                feed(ph["moe"], 2, NE - 1, True)
            act.wait_ge(x_ready, XR["moe"])
            x_parts(hcT, call["ff0c"])
            squares(lambda tt: x[:, tt, :], 1, 1e-5)
            stats(call["ff0x"], [(x_ready, XR["final"])], lambda tt: x[:, tt, :], eps=1e-6)

            def acc_squares(nm, c):
                act.wait_ge(nt_tp, 8 * (call[c] + 1))
                act.wait_ge(down_done, ph[nm]["s"] + 2 * NB2)
                squares(lambda tt: ps[:, 4 + 2 * tt:6 + 2 * tt, :].rearrange("p a b -> p (a b)"), 1, 1e-6)
            feed(ph["ff0c"], 2, ahead=True)
            chunks(call["ff0x"], *mod_cols(0, 0), hT, parts=True)
            acc_squares("ff0c", "ff0x")
            stats(call["mixc"], [(x_ready, XR["ff0c"])], lambda tt: cs[:, tt, :], eps=1e-6)
            feed(ph["ff0x"], 2)
            chunks(call["mixc"], *mod_cols(1, 1), hcT)
            acc_squares("ff0x", "mixc")
            norm(call["mixx"], [(x_ready, XR["ff0x"])], lambda tt: x[:, tt, :], *mod_cols(1, 0), dst=hT, eps=1e-6)
            for j in range(3):
                act.wait_ge(f_arg, j + 1)
                A(flt[0:64, 256:512], flt[0:64, 512:768], ACT.Sin).then_inc(f_sin, 1)
            for tt in range(TILES):
                if tt:
                    act.wait_ge(f_h, tt)
                A(decay, k2("absdelta"), ACT.Exp, scale=k2("negt")[:, tt:tt + 1]).then_inc(f_dec, 1)
            for q in range(0, 10, 2):
                act.wait_ge(k_mm, q + 1)
                if q:
                    act.wait_ge(k_copied, q)
                A(KF[:, q // 2, 0:512], ps[:, 4 + q % 4, :], ACT.Copy).then_inc(k_copied, 1)
            for q in range(4):
                act.wait_ge(ut_tp, q + 1)
                A(utok[:, q // 2, (q % 2) * 512:(q % 2 + 1) * 512], ps[:, 2 + q % 2, :], ACT.Copy).then_inc(ut_copied, 1)
            act.wait_ge(i_used, KC)
            copy_out(ph["hyo"], lambda tt, n, cols: YH[:, tt, n * BW:(n + 1) * BW])
            copy_out(ph["q2"], lambda tt, n, cols: qraw[:, tt, n * BW:(n + 1) * BW])
            copy_out(ph["kv2"], kv_dst, bank=lambda u, tt: 4 * (1 - u) + tt)
            for q in range(0, 24, 2):
                act.wait_ge(qt_tp, 28 + q + 1)
                A(qk_dst(q), ps[:, 2, 0:SEQ], ACT.Copy).then_inc(qt_act, 1)
            act.wait_ge(lam_ready, 1)
            A(small[:, 388:390], small[:, 384:386], ACT.Exp).then_inc(lam_ready, 1)
            def weigh(n):
                act.wait_ge(s2_max, n + 1)
                if n >= 2:
                    act.wait_ge(s2_tp, n - 1)
                for m in range(2):
                    last = A(E2[:, n % 2, m, :], ps[:, 4 + 2 * (n % 2) + m, :], ACT.Exp, bias=small[:, 400 + 2 * (n % 2) + m:401 + 2 * (n % 2) + m],
                             scale=SCALE, accum_out=small[:, 404 + 2 * (n % 2) + m:405 + 2 * (n % 2) + m])
                last.then_inc(s2_exp, 1)
            weigh(0)
            for n in range(16):
                act.wait_ge(s2_tp, n + 1)
                if n >= 2:
                    act.wait_ge(s2_pv, n - 1)
                A(PT2[:, n % 2, :], ps[:, 2, :], ACT.Copy).then_inc(s2_pt, 1)
                if n < 15:
                    weigh(n + 1)
                if n % 2:
                    tile, p = n // 2, ph["gt2"]
                    act.wait_ge(tile_done, p["td"] + tile + 1)
                    b, tt = tile // 2, tile % 2
                    A((SGh if b < 2 else SGd)[:, tt, (b % 2) * BW:(b % 2 + 1) * BW], ps[:, 1 + 2 * tt, :], ACT.Copy).then_inc(pj_act, 1)
            act.wait_ge(sl_sq, 1)
            A(small[:, 432:448], small[:, 416:432], ACT.Sqrt, scale=1.0 / P, bias=epsc[1e-6]).then_inc(sl_std, 1)
            for q in range(24, 32, 2):
                act.wait_ge(qt_tp, 28 + q + 1)
                A(hcT[:, q - 24, :], ps[:, 2, 0:SEQ], ACT.Copy).then_inc(qt_act, 1)
            act.wait_ge(pj_act, ph["gt2"]["ja"] + 8)
            for v in (SGh, SGd):
                for tt in range(TILES):
                    A(v[:, tt, :], v[:, tt, :], ACT.Sigmoid).then_inc(gates_open, 1)
            for q in range(32, 40, 2):
                act.wait_ge(qt_tp, 28 + q + 1)
                A(hcT[:, q - 32, :], ps[:, 2, 0:SEQ], ACT.Copy).then_inc(qt_act, 1)
            copy_out(ph["wo"], lambda tt, n, cols: YH[:, tt, n * BW:(n + 1) * BW])
            act.wait_ge(pj_dve, ph["wo"]["jd"] + 2)
            act.wait_ge(pj_act, ph["wo"]["ja"] + 2)
            squares(lambda tt: YH[:, tt, :], 1, 1e-6)
            for h in range(2):
                A_parts(ph["ff1"], 0, 0, 0, h)
            norm(call["ff1"], [(x_ready, XR["mixer"])], lambda tt: x[:, tt, :], *mod_cols(2, 0), dst=hT, eps=1e-6, parts=True)
            feed(ph["ff1"], 2)
            acc_squares("ff1", "ff1")

        @block.vector
        def _(dve):
            V = nc.vector
            ch = Chain(dve, dve_step)

            def wait(*pairs_):
                for sm, v in pairs_:
                    dve.wait_ge(sm, v)

            def norm(c, name, src, scale, dst, bias=None, nparts=1, parts=None):
                scaled(name, src, nparts)
                chunks(c, scale, dst, bias, parts)

            def scaled(name, src, nparts=1):
                n = D // nparts
                dve.wait_ge(nrm_std, SQ[name])
                ch.done(V.reciprocal(rr[:, 0:2 * nparts], std[:, 0:2 * nparts]))
                for tt in range(TILES):
                    for q in range(nparts):
                        j = tt * nparts + q
                        last = V.tensor_scalar(xn[:, tt, q * n:(q + 1) * n], src[:, tt, q * n:(q + 1) * n], rr[:, j:j + 1], None, ALU.mult)
                last.then_inc(nrm_xn, 1)

            def chunks(c, scale, dst, bias=None, parts=None):
                for k in range(1, KC, 2):
                    dve.wait_ge(nt_tp, 8 * c + k + 1)
                    if bias is None:
                        V.tensor_scalar(dst[:, k, :], ps[:, 3, 0:SEQ], scale(k), None, ALU.mult).then_inc(nt_dve, 1)
                    else:
                        V.tensor_scalar(dst[:, k, :], ps[:, 3, 0:SEQ], scale(k), bias(k), ALU.mult, ALU.add).then_inc(nt_dve, 1)
                    if parts is not None and k % 4 == 3:
                        x_low(dst, parts, k // 4, xs_high, xs_split)

            def x_low(src, done, h, high, split):
                dve.wait_ge(high, 2 * done + h + 1)
                V.tensor_tensor(xs[:, 1, 4 * h:4 * h + 4, :], src[:, 4 * h:4 * h + 4, :], f32(xs[:, 0, 4 * h:4 * h + 4, :]), ALU.subtract).then_inc(split, 1)

            def copy_out(p, dst, last_cols=BW, bank=lambda u, tt: 4 + 2 * u + tt):
                nb, T = p["nb"], p["tiles"]
                for n, i, u in pairs(dve, nb, straight=True):
                    cols = last_cols if nb % 2 and n == nb - 1 else BW
                    for tt in range(1, T, 2):
                        dve.wait_ge(tile_done, n * T + tt + 1 + p["td"])
                        V.tensor_copy(dst(tt, n, cols), ps[:, bank(u, tt), 0:cols]).then_inc(pj_dve, 1)

            def add_out(p, between):
                for n in range(p["nb"]):
                    for tt in range(TILES):
                        dve.wait_ge(tile_done, 2 * n + tt + 1 + p["td"])
                        x_ = x[:, tt, n * BW:(n + 1) * BW]
                        V.tensor_tensor(x_, x_, ps[:, 4 + 2 * (n % 2) + tt, :], ALU.add).then_inc(pj_dve, 1)
                    if n == 0 and between:
                        dve.wait_ge(mods_ready, 1)
                        between()
                dve.wait_ge(pj_dve, p["jd"] + 2 * p["nb"])
                dve.sem_inc(x_ready, 1)

            def reduce_angle(src, dst, k):
                ch.done(V.tensor_scalar(k, src, 1.0 / (2 * math.pi), MAGIC, ALU.mult, ALU.add))
                ch.done(V.tensor_scalar(k, k, MAGIC, None, ALU.subtract))
                ch.done(V.scalar_tensor_tensor(dst, k, -C1, src, ALU.mult, ALU.add))
                ch.done(V.scalar_tensor_tensor(dst, k, -C2, dst, ALU.mult, ALU.add))
                ch.done(V.scalar_tensor_tensor(dst, k, -C3, dst, ALU.mult, ALU.add))
                ch.done(V.tensor_scalar(dst, dst, PI_IN, -PI_IN, ALU.min, ALU.max))

            def A_parts(p, e, i, u, h):
                dve.wait_ge(A_high, e * (2 * p["nb"]) + i * 4 + (2 * (p["q"] + u) + h + 1))
                V.tensor_tensor(As[:, h, 1, :, :], ringA[:, (p["a"] + u) % 2, 4 * h:4 * h + 4, :], f32(As[:, h, 0, :, :]), ALU.subtract).then_inc(A_split, 1)

            def x_parts(src, done, high=xs_high, split=xs_split):
                for h in range(2):
                    x_low(src, done, h, high, split)

            def feed(p, T, e=0, ahead=False, after=None, before_last=None, at_end=None):
                nb = p["nb"]

                def hidden(i, u):
                    for tt in range(T):
                        buf = tt if T == 2 else u
                        dve.wait_ge(hd_high, ffn_count(p, T, e, i, u, tt))
                        flat = lambda v: v.rearrange("p a b -> p (a b)")
                        V.tensor_tensor(flat(hds[:, buf, 1, :, :]), ps[:, 2 + tt, 0:FB], f32(flat(hds[:, buf, 0, :, :])), ALU.subtract).then_inc(hdT_ready, 2 // T)

                def body(i, u, last):
                    if not (isinstance(i, int) and i == 0 and u == 0):
                        hidden(*((i, 0) if u else (i - 1, 1)))
                    nxt = (i + 1, 0) if u else (i, 1)
                    if not last or ahead:
                        A_parts(p, e, *nxt, 0)
                    for tt in range(T):
                        buf = tt if T == 2 else u
                        dve.wait_ge(silu_done, ffn_count(p, T, e, i, u, tt))
                        v = ffn_count(p, T, e, i, u, tt, 3 - T)
                        if started(v):
                            dve.wait_ge(tp_done, v)
                        V.tensor_tensor(hh[:, buf, :], sg[:, buf, :], ps[:, buf, FB:BW], ALU.mult).then_inc(h_ready, 2 // T)
                    if not last or ahead:
                        A_parts(p, e, *nxt, 1)
                    dve.wait_ge(B_high, e * (2 * nb) + i * 4 + (2 * (p["b"] + u) + 2))
                    V.tensor_tensor(Bs[:, 1, 1, :], ringB[:, (p["b"] + u) % 2, 1, :], f32(Bs[:, 1, 0, :]), ALU.subtract).then_inc(B_low1, 1)
                    if after and isinstance(i, int) and i == 0:
                        after(u)
                    if last:
                        if before_last:
                            before_last()
                        hidden(i, u)
                        if at_end:
                            at_end()
                blocks(dve, nb, body)
                dve.wait_ge(down_done, e * (2 * nb) + (p["s"] + 2 * nb))

            def acc(tt):
                return ps[:, 4 + 2 * tt:6 + 2 * tt, :].rearrange("p a b -> p (a b)")

            def one_hot(e, n, gated):
                flat = lambda v: v[:, bass.ds(e, 1), :].rearrange("p o t -> p (o t)")
                pcol, gcol = (small[:, 346:348], small[:, 348:350]) if gated else (small[:, 350:352], small[:, 352:354])
                V.tensor_copy(pcol, flat(slots))
                V.tensor_copy(gcol, flat(gates)).then_inc(col_ready, 1)
                dve.wait_ge(col_ready, n)
                for tt in range(TILES):
                    if gated:
                        last = V.tensor_scalar(selg[:, tt, :], k1("iota"), pcol[:, tt:tt + 1], gcol[:, tt:tt + 1], ALU.is_equal, ALU.mult)
                    else:
                        last = V.tensor_scalar(sel[:, tt, :], k1("iota"), pcol[:, tt:tt + 1], None, ALU.is_equal)
                last.then_inc(selg_ready if gated else sel_ready, 1)

            def dispatch(e):
                for half in range(2):
                    dve.wait_ge(gathered, 2 * e + (half + 1))
                    g = vcol[:, 0, 24 + 4 * half:28 + 4 * half].unsqueeze(2).broadcast_to([P, 4, P])
                    V.tensor_tensor(xgT[:, 4 * half:4 * half + 4, :], ps[:, 6 + half, :].rearrange("p (k s) -> p k s", k=4), g, ALU.mult).then_inc(xg_ready, 1)

            def add(e, tt):
                dve.wait_ge(mixed_back, 2 * e + (tt + 1))
                V.tensor_tensor(x[:, tt, :], x[:, tt, :], ps[:, 6:8, :].rearrange("p a b -> p (a b)"), ALU.add).then_inc(added, 1)
                dve.wait_ge(added, 2 * e + (tt + 1))

            def rows_parts(e):
                for h in range(2):
                    dve.wait_ge(xg_high, 2 * e + (h + 1))
                    V.tensor_tensor(xgs[:, 1, 4 * h:4 * h + 4, :], xgT[:, 4 * h:4 * h + 4, :], f32(xgs[:, 0, 4 * h:4 * h + 4, :]), ALU.subtract).then_inc(xg_split, 1)

            def expert(e):
                first, final = isinstance(e, int) and e == 0, isinstance(e, int) and e == NE - 1

                def after(u):
                    if not first:
                        add(e - 1, u)
                    if u:
                        if not first:
                            dve.wait_ge(selg_tp, e)
                        one_hot(e, 2 * e + 2, True)
                        if not final:
                            dve.wait_ge(gathered, 2 * e + 2)
                            one_hot(e + 1, 2 * e + 3, False)
                feed(ph["moe"], 1, e, True, after,
                     before_last=None if final else lambda: dispatch(e + 1), at_end=None if final else lambda: rows_parts(e + 1))

            def post(name, src, g, stream, signal):
                dve.wait_ge(nrm_std, SQ[name])
                dve.wait_ge(mods_ready, 4)
                ch.done(V.reciprocal(rr[:, 0:2], std[:, 0:2]))
                for tt in range(TILES):
                    last = V.scalar_tensor_tensor(xn[:, tt, :], src(tt), rr[:, tt:tt + 1], gateG[:, g, :], ALU.mult, ALU.mult)
                if signal:
                    last.then_inc(acc_free, 1)
                    dve.wait_ge(acc_free, signal)
                else:
                    ch.done(last)
                V.tensor_tensor(stream[:, :, :], stream[:, :, :], xn[:, :, :], ALU.add).then_inc(x_ready, 1)

            col = lambda r: (lambda k: vcol[:, 0, r + k:r + k + 1])
            V.memset(small[:, 500:501], 1e-5)
            V.memset(small[:, 501:502], 1e-6)
            ch.done(V.memset(small[:, 502:503], 0.0))
            wait((vt_done, 1))
            for g in range(3):
                last = V.tensor_copy(vcol[:, g, 0:VROWS[g]], ps[:, 2, g * P:g * P + VROWS[g]])
            last.then_inc(vt_copied, 1)
            wait((x_in, 32))
            ch.done(V.tensor_copy(posf[:, :], posi[:, :]))
            ang = small[:, 0:128].rearrange("p (t f) -> p t f", t=TILES)
            for tt in range(TILES):
                ch.done(V.tensor_scalar(small[:, 128:160], k1("inv"), posf[:, tt:tt + 1], None, ALU.mult))
                reduce_angle(small[:, 128:160], ang[:, tt, 0:32], small[:, 160:192])
                ch.done(V.scalar_tensor_tensor(ang[:, tt, 32:64], ang[:, tt, 0:32], -1.0, ang[:, tt, 0:32], ALU.mult, ALU.max))
                ch.done(V.tensor_scalar(ang[:, tt, 32:64], ang[:, tt, 32:64], -1.0, math.pi / 2, ALU.mult, ALU.add))
            dve.sem_inc(ang_ready, 1)
            def mod_cols(j, who):
                return dict(scale=lambda k: adaS[:, j, who, k:k + 1], bias=lambda k: modT[:, 2 * j, k, who:who + 1])

            def rotate(dst, src, G, Ax, cos, sin, dup=False):
                hw = HD // (2 * Ax)
                n = G * HD
                a1, a2 = xn[:, 0, 0:n], xn[:, 1, 0:n]
                g2 = lambda v: v.rearrange("p (g d) -> p g d", g=G)
                V.tensor_tensor(g2(a1), g2(src), cos.unsqueeze(1).broadcast_to([P, G, HD]), ALU.mult)
                for h in range(2):
                    v = lambda z, hh_: z.rearrange("p (g a h w) -> p g a h w", g=G, a=Ax, h=2)[:, :, :, hh_, :]
                    sv = sin.rearrange("p (a h w) -> p a h w", a=Ax, h=2)[:, :, h, :].unsqueeze(1).broadcast_to([P, G, Ax, hw])
                    last = V.tensor_tensor(v(a2, h), v(src, 1 - h), sv, ALU.mult)
                ch.done(last)
                if dup:
                    b_ = lambda z: g2(z).unsqueeze(2).broadcast_to([P, G, 2, HD])
                    return V.tensor_tensor(dst.rearrange("p (g u d) -> p g u d", g=G, u=2), b_(a1), b_(a2), ALU.add)
                return V.tensor_tensor(dst, a1, a2, ALU.add)

            for l in range(2):
                norm(call[f"attn{l}"], f"attn{l}", x, col(8 * l), hT)
                copy_out(ph[f"in{l}"], lambda tt, n, cols: qkv[:, tt, n * BW:n * BW + cols], last_cols=FB)
                if l == 0:
                    wait((table_ready, 2))
                wait((pj_act, ph[f"in{l}"]["ja"] + 5), (pj_dve, ph[f"in{l}"]["jd"] + 5))
                for tt in range(TILES):
                    ch.done(rotate(qr[:, tt, 0:D], qkv[:, tt, 0:D], 16, 1, cosT[:, tt, :], sinT[:, tt, :]))
                dve.sem_inc(rope_ready, 1)
                for tt in range(TILES):
                    ch.done(rotate(qr[:, tt, D:D + 512], qkv[:, tt, 1536:2048], 8, 1, cosT[:, tt, :], sinT[:, tt, :]))
                    ch.done(rotate(qr[:, tt, D + 512:D + 768], qkv[:, tt, 2048:2176], 2, 1, cosT[:, tt, :], sinT[:, tt, :], dup=True))
                dve.sem_inc(rope_ready, 1)
                for c in range(1, 14, 2):
                    dve.wait_ge(qt_tp, 14 * l + c + 1)
                    V.tensor_copy(qkT[:, c, :], ps[:, 3, 0:SEQ]).then_inc(qt_dve, 1)
                nm2 = lambda o: small[:, o:o + 8].rearrange("p (j t) -> p j t", t=TILES)
                rep = lambda m: k1(m).unsqueeze(1).broadcast_to([P, 4, 384])
                kind = lambda g: "dil" if g < 2 else "win"

                def maxima(g):
                    gi = 4 * l + g
                    dve.wait_ge(sc_done, gi + 1)
                    if gi:
                        dve.wait_ge(pt_done, 4 * gi)
                    ch.done(V.scalar_tensor_tensor(S[:, :, :], ps[:, 4:8, 0:384], SCALE, rep(kind(g) + "_bias"), ALU.mult, ALU.add))
                    V.tensor_reduce(nm2(168)[:, :, 0], S[:, :, 0:P], X, ALU.max)
                    ch.done(V.tensor_reduce(nm2(168)[:, :, 1], S[:, :, P:384], X, ALU.max))
                    if g >= 2:
                        sk = sinkr[:, l, 4 * (g - 2):4 * (g - 2) + 4].unsqueeze(2).broadcast_to([P, 4, 2])
                        ch.done(V.tensor_tensor(nm2(168), nm2(168), sk, ALU.max))
                        ch.done(V.tensor_tensor(nm2(136), sk, nm2(168), ALU.subtract))
                    V.tensor_scalar(small[:, 128:136], small[:, 168:176], -1.0, None, ALU.mult).then_inc(nm_ready, 1)

                def weights(g):
                    gi = 4 * l + g
                    dve.wait_ge(e_ready, gi + 1)
                    V.tensor_tensor(S[:, :, :], S[:, :, :], rep(kind(g) + "_count"), ALU.mult).then_inc(p_ready, 1)
                    dve.wait_ge(p_ready, gi + 1)
                    V.tensor_reduce(nm2(152)[:, :, 0], S[:, :, 0:P], X, ALU.add)
                    ch.done(V.tensor_reduce(nm2(152)[:, :, 1], S[:, :, P:384], X, ALU.add))
                    if g >= 2:
                        ch.done(V.tensor_tensor(small[:, 152:160], small[:, 152:160], small[:, 144:152], ALU.add))
                    ch.done(V.reciprocal(small[:, 160:168], small[:, 152:160]))
                    for j in (1, 3):
                        dve.wait_ge(pt_done, 4 * gi + j + 1)
                        V.tensor_copy(PT[:, j, :], ps[:, 3, 0:384]).then_inc(pt_dve, 1)

                def outputs(g):
                    dve.wait_ge(pv_done, 4 * l + g + 1)
                    for tt in range(TILES):
                        last = V.tensor_tensor(O[:, tt, g * SEQ:(g + 1) * SEQ].rearrange("p (j d) -> p j d", j=4),
                                               ps[:, 0, :].rearrange("p (j t d) -> p j t d", j=4, t=TILES)[:, :, tt, :],
                                               nm2(160)[:, :, tt:tt + 1].broadcast_to([P, 4, HD]), ALU.mult)
                    last.then_inc(o_done, 1)
                maxima(0)
                for g in range(4):
                    weights(g)
                    if g < 3:
                        maxima(g + 1)
                    outputs(g)
                mixc = lambda k, l=l: vcol[:, 0, (32 + 4 * l + k if k < 4 else 40 + 4 * l + k - 4):][:, 0:1]
                norm(call[f"mix{l}"], f"mix{l}", O, mixc, hT, nparts=2)
                if l == 1:
                    scaled("ff0c", cs)
                add_out(ph[f"out{l}"], between=(lambda: chunks(call["ff0c"], dst=hcT, **mod_cols(0, 1))) if l == 1 else None)
                p = ph["dense"] if l == 0 else ph["moe"]
                A_parts(p, 0, 0, 0, 0)
                norm(call[f"ffn{l}"], f"ffn{l}", x, col(16 + 8 * l), hT, parts=0 if l == 0 else None)
                if l == 0:
                    A_parts(p, 0, 0, 0, 1)
                    feed(p, 2)
                    for tt in range(TILES):
                        last = V.tensor_tensor(x[:, tt, :], x[:, tt, :], acc(tt), ALU.add)
                    last.then_inc(acc_free, 1)
                    dve.wait_ge(acc_free, 1)
                    dve.sem_inc(x_ready, 1)
            A_parts(ph["moe"], 0, 0, 0, 1)
            wait((rt_done, 1))
            lg = small[:, 256:272].rearrange("p (t e) -> p t e", t=TILES)
            top = small[:, 272:288].rearrange("p (t e) -> p t e", t=TILES)
            ixf = small[:, 288:304].rearrange("p (t e) -> p t e", t=TILES)
            ch.done(V.tensor_copy(small[:, 256:272], ps[:, 0, 0:16]))
            for tt in range(TILES):
                ch.done(V.max(top[:, tt, :], lg[:, tt, :]))
                ch.done(V.max_index(idx8[:, tt, :], top[:, tt, :], lg[:, tt, :]))
                ch.done(V.tensor_copy(ixf[:, tt, :], idx8[:, tt, :]))
            V.tensor_tensor(small[:, 304:306], top[:, :, 1], top[:, :, 0], ALU.subtract).then_inc(rt_exp, 1)
            wait((rt_exp, 2))
            ch.done(V.tensor_scalar(small[:, 308:310], small[:, 306:308], 1.0, None, ALU.add))
            ch.done(V.reciprocal(small[:, 310:312], small[:, 308:310]))
            ch.done(V.tensor_tensor(small[:, 312:314], small[:, 306:308], small[:, 310:312], ALU.mult))
            for tt in range(TILES):
                V.tensor_scalar(small[:, 320:328], k1("iota")[:, 0:NE], ixf[:, tt, 0:1], small[:, 310 + tt:311 + tt], ALU.is_equal, ALU.mult)
                ch.done(V.tensor_scalar(small[:, 328:336], k1("iota")[:, 0:NE], ixf[:, tt, 1:2], small[:, 312 + tt:313 + tt], ALU.is_equal, ALU.mult))
                ch.done(V.tensor_tensor(gates[:, :, tt], small[:, 320:328], small[:, 328:336], ALU.add))
                ch.done(V.tensor_scalar(chosen[:, tt, :], k1("iota")[:, 0:NE], ixf[:, tt, 0:1], None, ALU.is_equal))
                ch.done(V.scalar_tensor_tensor(chosen[:, tt, :], k1("iota")[:, 0:NE], ixf[:, tt, 1:2], chosen[:, tt, :], ALU.is_equal, ALU.add))
            dve.sem_inc(rt_ready, 1)
            dve.wait_ge(slot_mm, 1)
            c0 = 2 * NE
            for tt in range(TILES):
                ch.done(V.scalar_tensor_tensor(slots[:, :, tt], ps[:, 0, c0 + tt * NE:c0 + (tt + 1) * NE], 1.0, chosen[:, tt, :], ALU.add, ALU.mult))
            ch.done(V.tensor_scalar(slots[:, :, :], slots[:, :, :], 1.0, None, ALU.subtract))
            V.tensor_reduce(small[:, 344:345], ps[:, 0, c0 + 2 * NE:c0 + 3 * NE], X, ALU.max).then_inc(most_ready, 1)
            dve.wait_ge(most_ready, 1)
            V.tensor_copy(most[:, :], small[:, 344:345]).then_inc(most_ready, 1)
            dve.wait_ge(most_ready, 2)
            p = ph["moe"]
            gcol = small[:, 340:342]
            with dve.If(dve.value_load(most[0:1, 0:1], min_val=0, max_val=SEQ) < CAP + 1):
                one_hot(0, 1, False)
                dispatch(0)
                rows_parts(0)
                expert(0)
                with dve.Fori(1, NE - 1) as e:
                    expert(e)
                expert(NE - 1)
                for tt in range(TILES):
                    add(NE - 1, tt)
                dve.wait_ge(added, TILES * NE)
            with dve.Else():
                def all_tokens(e):
                    feed(p, 2, e, True)
                    dve.wait_ge(acc_free, e + 1)
                    V.tensor_copy(gcol, gates[:, bass.ds(e, 1), :].rearrange("p o t -> p (o t)")).then_inc(gcol_ready, 1)
                    dve.wait_ge(gcol_ready, e + 1)
                    for tt in range(TILES):
                        last = V.scalar_tensor_tensor(x[:, tt, :], acc(tt), gcol[:, tt:tt + 1], x[:, tt, :], ALU.mult, ALU.add)
                    last.then_inc(acc_free, 1)
                x_parts(hT, 0, xr_high, xr_split)
                with dve.Fori(0, NE - 1) as e:
                    all_tokens(e)
                all_tokens(NE - 1)
                dve.wait_ge(acc_free, 1 + NE)
            dve.sem_inc(x_ready, 1)
            x_parts(hcT, ph["ff0c"]["xc"])
            dve.wait_ge(nrm_std, SQ["final"])
            ch.done(V.reciprocal(rr[:, 0:2], std[:, 0:2]))
            for tt in range(TILES):
                last = V.scalar_tensor_tensor(x[:, tt, :], x[:, tt, :], rr[:, tt:tt + 1], fnrow[:, :], ALU.mult, ALU.mult)
            last.then_inc(x_ready, 1)
            dve.wait_ge(x_ready, XR["final"])
            scaled("ff0x", x)
            feed(ph["ff0c"], 2, ahead=True)
            chunks(call["ff0x"], dst=hT, parts=ph["ff0x"]["xc"], **mod_cols(0, 0))
            post("ff0c_out", acc, 1, cs, ph["ff0c"]["f"] + 1)
            dve.wait_ge(x_ready, XR["ff0c"])
            scaled("mixc", cs)
            feed(ph["ff0x"], 2)
            chunks(call["mixc"], dst=hcT, **mod_cols(1, 1))
            post("ff0x_out", acc, 0, x, ph["ff0x"]["f"] + 1)
            dve.wait_ge(x_ready, XR["ff0x"])
            norm(call["mixx"], "mixx", x, dst=hT, **mod_cols(1, 0))
            wait((c2_in, 16), (filt_in, 16 * 7))
            fa, fk, fr = flt[0:64, 512:768], flt[0:64, 768:1024], decay[0:64, 0:256]
            for j in range(3):
                dve.wait_ge(f_mm, j + 1)
                ch.done(V.tensor_scalar(fr, ps[0:64, 0, 0:SEQ], flt[0:64, 192 + j:193 + j], flt[0:64, 195:196], ALU.add, ALU.mult))
                reduce_angle(fr, fa, fk)
                dve.sem_inc(f_arg, 1)
            nf = k2("notfirst")
            for tt in range(TILES):
                wait((f_mm, 4 + tt), (f_dec, tt + 1))
                two = lambda o: ps[:, o:o + 2, :].rearrange("p a b -> p (a b)")
                V.tensor_tensor(hs[:, tt, :], two(4), decay, ALU.mult)
                ch.done(V.scalar_tensor_tensor(hd[:, tt, :], two(6), nf[:, tt:tt + 1], decay, ALU.mult, ALU.mult))
                V.scalar_tensor_tensor(ha[:, tt, :], hd[:, tt, :], -1.0, hd[:, tt, :], ALU.mult, ALU.max)
                ch.done(V.scalar_tensor_tensor(decay, hs[:, tt, :], -1.0, hs[:, tt, :], ALU.mult, ALU.max))
                ch.done(V.tensor_tensor(ha[:, tt, :], ha[:, tt, :], decay, ALU.add))
                ch.done(V.tensor_tensor(decay, hs[:, tt, :], hd[:, tt, :], ALU.add))
                ch.done(V.tensor_tensor(hd[:, tt, :], hs[:, tt, :], hd[:, tt, :], ALU.subtract))
                V.tensor_copy(hs[:, tt, :], decay).then_inc(f_h, 1)
            wait((rn_mm, 1))
            rn = small[:, 460:468]
            ch.done(V.tensor_scalar(rn, ps[:, 0, 0:KC], 1e-6, None, ALU.add))
            ch.done(V.reciprocal(rn, rn))
            for q in range(1, 10, 2):
                wait((k_mm, q + 1), (k_copied, q))
                V.tensor_copy(KF[:, q // 2, 512:D], ps[:, 4 + q % 4, :]).then_inc(k_copied, 1)
            w = lambda j, c: vcol[:, 1, 24 * j + c:24 * j + c + 1]
            for c in range(24):
                bk = ps[:, 4 + c % 4, :]
                dst = x0T[:, c, :] if c < 8 else uT[:, c - 8, :] if c < 16 else xn[:, 0, 0:SEQ]
                dve.wait_ge(tile_done, ph["z"]["td"] + c + 1)
                ch.done(V.tensor_scalar(dst, bk[:, 0:SEQ], w(1, c), vcol[:, 1, 72 + c:73 + c], ALU.mult, ALU.add))
                ch.done(V.scalar_tensor_tensor(dst[:, 1:SEQ], bk[:, 0:SEQ - 1], w(0, c), dst[:, 1:SEQ], ALU.mult, ALU.add))
                last = V.scalar_tensor_tensor(dst[:, 0:SEQ - 1], bk[:, 1:SEQ], w(2, c), dst[:, 0:SEQ - 1], ALU.mult, ALU.add)
                if c >= 16:
                    ch.done(last)
                    last = V.tensor_tensor(uT[:, c - 16, :], uT[:, c - 16, :], dst, ALU.mult)
                last.then_inc(z_used, 1)
                dve.wait_ge(z_used, c + 1)
            for half in range(2):
                cs_ = slice(half * 512, (half + 1) * 512)
                t1, t2 = xn[:, 0, 0:512], xn[:, 0, 512:D]
                dve.wait_ge(u_mm, half + 1)
                for fc in range(2):
                    re, im = ps[:, 4 + fc, :], ps[:, 6 + fc, :]
                    V.tensor_tensor(Y[:, fc, cs_], re, KF[:, fc, cs_], ALU.mult)
                    V.tensor_tensor(t1, im, KF[:, 2 + fc, cs_], ALU.mult)
                    V.tensor_tensor(Y[:, 2 + fc, cs_], re, KF[:, 2 + fc, cs_], ALU.mult)
                    ch.done(V.tensor_tensor(t2, im, KF[:, 4 if fc == 0 else 1, cs_], ALU.mult))
                    V.tensor_tensor(Y[:, fc, cs_], Y[:, fc, cs_], t1, ALU.subtract)
                    last = V.tensor_tensor(Y[:, 2 + fc, cs_], Y[:, 2 + fc, cs_], t2, ALU.add)
                    if fc == 0:
                        ch.done(last)
                last.then_inc(y_ready, 1)
                dve.wait_ge(y_ready, half + 1)
            for c in range(KC):
                tmp = xn[:, 0, 0:SEQ]
                ch.done(V.tensor_scalar(tmp, uT[:, c, :], vcol[:, 0, 112 + c:113 + c], None, ALU.mult))
                dve.wait_ge(i_mm, c + 1)
                ch.done(V.scalar_tensor_tensor(tmp, ps[:, c % 2, 0:SEQ], rn[:, c:c + 1], tmp, ALU.mult, ALU.add))
                V.tensor_tensor(uT[:, c, :], tmp, x0T[:, c, :], ALU.mult).then_inc(i_used, 1)
                dve.wait_ge(i_used, c + 1)
            copy_out(ph["hyo"], lambda tt, n, cols: YH[:, tt, n * BW:(n + 1) * BW])
            copy_out(ph["q2"], lambda tt, n, cols: qraw[:, tt, n * BW:(n + 1) * BW])
            wait((rope2_in, 16 * 6), (pj_act, ph["kv2"]["ja"]), (pj_dve, ph["kv2"]["jd"]))
            cos2 = arena[:, 6144:6272].rearrange("p (t d) -> p t d", t=TILES)
            sin2 = arena[:, 6272:6400].rearrange("p (t d) -> p t d", t=TILES)
            for tt in range(TILES):
                ch.done(rotate(qraw[:, tt, :], qraw[:, tt, :], 16, 2, cos2[:, tt, :], sin2[:, tt, :]))
            dve.sem_inc(rope_ready, 1)
            copy_out(ph["kv2"], kv_dst, bank=lambda u, tt: 4 * (1 - u) + tt)
            wait((pj_act, ph["gt2"]["ja"]), (pj_dve, ph["gt2"]["jd"]))
            for tt in range(TILES):
                ch.done(rotate(kraw[:, tt, :], kraw[:, tt, :], 16, 2, cos2[:, tt, :], sin2[:, tt, :]))
            dve.sem_inc(rope_ready, 1)
            for j in range(2):
                o = 128 * j
                ch.done(V.tensor_tensor(small[:, o:o + 64], small[:, o:o + 64], small[:, o + 64:o + 128], ALU.mult))
                ch.done(V.tensor_reduce(small[:, 384 + j:385 + j], small[:, o:o + 64], X, ALU.add))
            dve.sem_inc(lam_ready, 1)
            for q in range(1, 24, 2):
                dve.wait_ge(qt_tp, 28 + q + 1)
                V.tensor_copy(qk_dst(q), ps[:, 3, 0:SEQ]).then_inc(qt_dve, 1)
            wait((lam_ready, 2))
            lam = small[:, 390:391]
            ch.done(V.tensor_tensor(lam, small[:, 388:389], small[:, 389:390], ALU.subtract))
            ch.done(V.tensor_scalar(lam, lam, LAM_INIT, None, ALU.add))

            def rowmax(n):
                m = 2 * (n % 2)
                dve.wait_ge(s2_mm, n + 1)
                ch.done(V.tensor_reduce(small[:, 396 + m:398 + m], ps[:, 4 + m:6 + m, :], X, ALU.max))
                V.tensor_scalar(small[:, 400 + m:402 + m], small[:, 396 + m:398 + m], -SCALE, None, ALU.mult).then_inc(s2_max, 1)

            def gather_out(n):
                h, tt = n // 2, n % 2
                dve.wait_ge(s2_pv, n + 1)
                V.tensor_copy(O2[:, tt, h * P:(h + 1) * P], ps[:, 0, 0:P]).then_inc(s2_o, 1)
            rowmax(0)
            for n in range(16):
                m = 2 * (n % 2)
                dve.wait_ge(s2_exp, n + 1)
                ri = small[:, 408 + m:410 + m]
                ch.done(V.reciprocal(ri, small[:, 404 + m:406 + m]))
                ch.done(V.tensor_tensor(ri[:, 1:2], ri[:, 1:2], lam, ALU.mult))
                e0, e1 = E2[:, n % 2, 0, :], E2[:, n % 2, 1, :]
                ch.done(V.tensor_scalar(e1, e1, ri[:, 1:2], None, ALU.mult))
                V.scalar_tensor_tensor(e0, e0, ri[:, 0:1], e1, ALU.mult, ALU.subtract).then_inc(s2_p, 1)
                if n:
                    gather_out(n - 1)
                if n < 15:
                    rowmax(n + 1)
            gather_out(15)
            dve.wait_ge(s2_o, 16)
            ch.done(V.tensor_tensor(xn[:, :, :], O2[:, :, :], O2[:, :, :], ALU.mult))
            V.tensor_reduce(small[:, 416:432], xn[:, :, :].rearrange("p t (h d) -> p (t h) d", d=P), X, ALU.add).then_inc(sl_sq, 1)
            dve.wait_ge(sl_std, 1)
            ch.done(V.reciprocal(small[:, 416:432], small[:, 432:448]))
            o16 = O2[:, :, :].rearrange("p t (h d) -> p (t h) d", d=P)
            ch.done(V.tensor_tensor(o16, o16, small[:, 416:432].unsqueeze(2).broadcast_to([P, 16, P]), ALU.mult))
            V.scalar_tensor_tensor(o16, o16, 1.0 - LAM_INIT, small[:, 256:384].unsqueeze(1).broadcast_to([P, 16, P]), ALU.mult, ALU.mult).then_inc(sl_std, 1)
            for q in range(25, 32, 2):
                dve.wait_ge(qt_tp, 28 + q + 1)
                V.tensor_copy(hcT[:, q - 24, :], ps[:, 3, 0:SEQ]).then_inc(qt_dve, 1)
            wait((gates_open, 4))
            ch.done(V.tensor_tensor(YH[:, :, :], YH[:, :, :], SGh, ALU.mult))
            p = ph["dao"]
            for n in range(2):
                for tt in range(TILES):
                    c = slice(n * BW, (n + 1) * BW)
                    dve.wait_ge(tile_done, p["td"] + 2 * n + tt + 1)
                    V.tensor_tensor(YD[:, tt, c], ps[:, 4 + 2 * n + tt, :], SGd[:, tt, c], ALU.mult).then_inc(pj_dve, 1)
                    dve.wait_ge(pj_dve, p["jd"] + 2 * n + tt + 1)
                    V.tensor_tensor(YH[:, tt, c], YH[:, tt, c], YD[:, tt, c], ALU.add).then_inc(y_mixed, 1)
            for q in range(33, 40, 2):
                dve.wait_ge(qt_tp, 28 + q + 1)
                V.tensor_copy(hcT[:, q - 32, :], ps[:, 3, 0:SEQ]).then_inc(qt_dve, 1)
            copy_out(ph["wo"], lambda tt, n, cols: YH[:, tt, n * BW:(n + 1) * BW])
            post("wo_out", lambda tt: YH[:, tt, :], 2, x, 0)
            A_parts(ph["ff1"], 0, 0, 0, 0)
            norm(call["ff1"], "ff1", x, dst=hT, parts=ph["ff1"]["xc"], **mod_cols(2, 0))
            A_parts(ph["ff1"], 0, 0, 0, 1)
            feed(ph["ff1"], 2)
            post("ff1_out", acc, 3, x, ph["ff1"]["f"] + 1)


LAYOUT = {
    "x": (SEQ, D), "positions": (SEQ,), "attn_norm": (-1,), "w_in": (2 * D, QKV), "mix_norm_a": (-1,), "mix_norm_b": (-1,),
    "sinks": (-1,), "w_out": (2 * D, D), "ffn_norm": (-1,), "dense_w_gate": (D, FF), "dense_w_up": (D, FF), "dense_w_down": (FF, D),
    "router": (D, NE), "moe_w_gate": (NE, D, FF), "moe_w_up": (NE, D, FF), "moe_w_down": (NE, FF, D), "final_norm": (D,),
    "c_2": (D,), "ctx_2": (SEQ, D), "c_ctx_2": (D,), "w_ada_2": (D, 9 * D), "b_ada_2": (-1,), "norm_g_2": (-1,),
    "w_ff_in_2": (2 * D, 2 * FF2), "w_ff_out_2": (2 * FF2, D), "w_in_2": (D, 8 * D), "hy_conv_w_2": (-1,), "hy_conv_b_2": (-1,),
    "filt_w1_2": (33, 64), "filt_b1_2": (64,), "filt_w2_2": (64, 64), "filt_b2_2": (64,), "filt_w3_2": (64, 64), "filt_b3_2": (64,),
    "filt_w4_2": (64, 2 * D), "filt_freq_2": (64,), "hy_bias_2": (-1,), "lambda_q1_2": (64,), "lambda_k1_2": (64,),
    "lambda_q2_2": (64,), "lambda_k2_2": (64,), "subln_g_2": (P,), "w_hy_out_2": (D, D), "w_da_out_2": (D, D), "w_o_2": (D, D),
}


def kernel(**inputs):
    import concourse.bacc as bacc
    from concourse.bass_utils import run_bass_kernel_spmd as run

    nc = bacc.Bacc("TRN2", target_bir_lowering=False, num_devices=1)
    at1, const1, at2, const2 = shape_constants()
    arrays = {n: np.ascontiguousarray(inputs[n]).reshape(s) for n, s in LAYOUT.items()}
    arrays["const1"], arrays["const2"] = const1, const2
    t = {n: nc.dram_tensor(f"in_{n}", a.shape, mybir.dt.from_np(a.dtype), kind="ExternalInput").ap() for n, a in arrays.items()}
    out = nc.dram_tensor("out", (SEQ, D), F32, kind="ExternalOutput").ap()
    build(nc, t, out, at1, const1.shape[1], at2, const2.shape[1])
    r = run(nc, [{f"in_{n}": a for n, a in arrays.items()}], core_ids=[0])
    return r.results[0]["out"].reshape(1, SEQ, D)
```
